# Optimizing a Trainium2 kernel written in Bass

```python
import math
import jax
import jax.numpy as jnp
from jax import lax
import numpy as np

D_MODEL = 1024
BATCH = 1
SEQ = 256
DEPTH = 2

GRID_W = 64
CTX_LEN = 256
HEAD_DIM = 64
ROPE_FREQS = HEAD_DIM // 4
ROPE_THETA = 10000.0
ATTN_SCALE = HEAD_DIM ** -0.5
NEG_INF = -1e30
Q_BLOCK = 128
WINDOW = 128
A_HEADS = 8
A_KV = 2
W_HEADS = 8
W_KV = 2
HY_WIDTH = 512
HY_SHORT = 3
HY_BANDS = 16
HY_EMB = 1 + 2 * HY_BANDS
HY_HIDDEN = 64
HY_TARGET = 1e-2
HY_FAST_DECAY = 0.3
HY_SLOW_DECAY = 1.5
N_BRANCH = 3
N_GROUPS = 4
EXPERTS_PER_GROUP = 4
N_EXPERTS = N_GROUPS * EXPERTS_PER_GROUP
TOP_K = 2
D_EXPERT = 512
N_MOD = 6
EPS = 1e-6
IN_SPLITS = (A_HEADS * HEAD_DIM, A_KV * HEAD_DIM, A_KV * HEAD_DIM, 3 * HY_WIDTH,
             W_HEADS * HEAD_DIM, W_KV * HEAD_DIM, W_KV * HEAD_DIM, N_BRANCH * D_MODEL)
IN_OFFSETS = tuple(int(o) for o in np.cumsum(IN_SPLITS)[:-1])
D_IN = int(sum(IN_SPLITS))
F32 = jnp.float32

kernel_name = 'hybrid_flow_trunk'

def rms_norm(t, g):
    tf = t.astype(F32)
    return (tf * lax.rsqrt(jnp.mean(tf * tf, axis=-1, keepdims=True) + EPS) * g.astype(F32)).astype(t.dtype)

def modulate(h, shift, scale):
    return h * (1 + scale) + shift

def heads(t, n):
    return t.reshape(t.shape[:-1] + (n, HEAD_DIM))

def group_q(q, n_kv):
    b, l, h, d = q.shape
    return q.reshape(b, l, n_kv, h // n_kv, d)

def axial_rope(t, cos, sin):
    tf = t.reshape(t.shape[:-1] + (2, 2, ROPE_FREQS))
    a, b = tf[..., 0, :], tf[..., 1, :]
    c, s = cos[:, None], sin[:, None]
    out = jnp.stack([a * c - b * s, b * c + a * s], axis=-2)
    return out.reshape(t.shape).astype(t.dtype)

def gqa_attend(q, k, v, sink=None, mask=None):
    s = jnp.einsum('bqkgd,bskd->bkgqs', q, k).astype(F32) * ATTN_SCALE
    if mask is not None:
        s = jnp.where(mask, s, NEG_INF)
    if sink is not None:
        sk = jnp.broadcast_to(sink.astype(F32)[:, :, None, None], s.shape[:-1] + (1,))
        p = jax.nn.softmax(jnp.concatenate([s, sk], axis=-1), axis=-1)[..., :-1]
    else:
        p = jax.nn.softmax(s, axis=-1)
    return jnp.einsum('bkgqs,bskd->bqkgd', p.astype(v.dtype), v)

def to_blocks(q, n_kv):
    b, s, h, d = q.shape
    return jnp.moveaxis(q.reshape(b, s // Q_BLOCK, Q_BLOCK, n_kv, h // n_kv, d), 1, 0)

def from_blocks(o):
    nb, b, qb, kv, g, d = o.shape
    return jnp.moveaxis(o, 0, 1).reshape(b, nb * qb, kv * g * d)

def band_blocks(t):
    b, s, kv, d = t.shape
    tp = jnp.pad(t, ((0, 0), (Q_BLOCK, Q_BLOCK), (0, 0), (0, 0))).reshape(b, s // Q_BLOCK + 2, Q_BLOCK, kv, d)
    band = jnp.concatenate([tp[:, :-2], tp[:, 1:-1], tp[:, 2:]], axis=2)
    return jnp.moveaxis(band, 1, 0)

def hyena_kernel(n, w1, b1, freq, w2, b2, w3):
    pos = jnp.arange(n, dtype=F32)[:, None]
    t = pos / (n - 1)
    bands = jnp.linspace(1e-4, HY_BANDS - 1, HY_BANDS, dtype=F32)
    ang = 2 * math.pi * bands * pos / n
    z = jnp.concatenate([t, jnp.cos(ang), -jnp.sin(ang)], axis=-1)
    h = jnp.sin(freq * (z @ w1 + b1))
    h = jnp.sin(freq * (h @ w2 + b2))
    h = (h @ w3).astype(F32).reshape(n, 2, HY_WIDTH)
    deltas = jnp.abs(jnp.linspace(math.log(HY_TARGET) / HY_SLOW_DECAY, math.log(HY_TARGET) / HY_FAST_DECAY,
                                  HY_WIDTH, dtype=F32))
    h = h * jnp.exp(-t * deltas)[:, None, :]
    kern = jnp.concatenate([h[:, 0], jnp.zeros((1, HY_WIDTH), F32), h[:0:-1, 1]], axis=0)
    return kern / jnp.sum(jnp.abs(kern), axis=0, keepdims=True)

def bidir_long_conv(u, kern):
    n = u.shape[1]
    uf = jnp.fft.rfft(u.astype(F32), n=2 * n, axis=1)
    kf = jnp.fft.rfft(kern, n=2 * n, axis=0)
    return jnp.fft.irfft(uf * kf[None], n=2 * n, axis=1)[:, :n]

def hyena_mixer(u, short_w, short_b, kern, skip):
    uc = lax.conv_general_dilated(u, short_w[:, None, :], (1,), ((HY_SHORT // 2, HY_SHORT // 2),),
                                  dimension_numbers=('NWC', 'WIO', 'NWC'),
                                  feature_group_count=u.shape[-1]) + short_b
    x0, x1, v = jnp.split(uc.astype(F32), 3, axis=-1)
    v = v * x1
    y = bidir_long_conv(v, kern) + skip.astype(F32) * v
    return (x0 * y).astype(u.dtype)

def merge_branches(ya, yh, yw, gate_logits, w_branch, w_out):
    ga, gh, gw = jnp.split(jax.nn.sigmoid(gate_logits), N_BRANCH, axis=-1)
    m = ga * (ya @ w_branch[0]) + gh * (yh @ w_branch[1]) + gw * (yw @ w_branch[2])
    return m @ w_out

def hier_moe(t, rg_w, rg_b, re_w, re_b, w1, w3, w2):
    n = t.shape[0]
    lg = (t @ rg_w + rg_b).astype(F32)
    g_sel = jnp.argmax(lg, axis=-1)
    p_g = jnp.take_along_axis(jax.nn.softmax(lg, axis=-1), g_sel[:, None], axis=-1)
    le = (t @ re_w + re_b).astype(F32).reshape(n, N_GROUPS, EXPERTS_PER_GROUP)
    le_sel = jnp.take_along_axis(le, g_sel[:, None, None], axis=1)[:, 0]
    top_v, top_i = lax.top_k(le_sel, TOP_K)
    p_e = jax.nn.softmax(top_v, axis=-1) * p_g
    eid = g_sel[:, None] * EXPERTS_PER_GROUP + top_i
    combine = jnp.sum(jax.nn.one_hot(eid, N_EXPERTS, dtype=F32) * p_e[..., None], axis=1).astype(t.dtype)
    out = jnp.zeros_like(t)
    for e in range(N_EXPERTS):
        h = jax.nn.silu(t @ w1[e]) * (t @ w3[e])
        out = out + combine[:, e:e + 1] * (h @ w2[e])
    return out

def trunk_layer(x, xc, c, c_ctx, cos, sin, win_mask, update_ctx,
                ada_w, ada_b, norm1_g, norm2_g, w_in, qk_g,
                hy_short_w, hy_short_b, hy_f_w1, hy_f_b1, hy_f_freq, hy_f_w2, hy_f_b2, hy_f_w3, hy_bias,
                sinks, w_branch, w_out, router_g_w, router_g_b, router_e_w, router_e_b, exp_w1, exp_w3, exp_w2):
    bsz, n_tok, _ = x.shape
    n_ctx = xc.shape[1]
    mod = jnp.split((jax.nn.silu(c) @ ada_w + ada_b)[:, None, :], N_MOD, axis=-1)
    mod_c = jnp.split(jax.nn.silu(c_ctx) @ ada_w + ada_b, N_MOD, axis=-1)

    h = modulate(rms_norm(x, norm1_g), mod[0], mod[1])
    hc = modulate(rms_norm(xc, norm1_g), mod_c[0], mod_c[1])
    qa, ka, va, uh, qw, kw, vw, gts = jnp.split(h @ w_in, IN_OFFSETS, axis=-1)
    qa_c, ka_c, va_c, uh_c, qw_c, kw_c, vw_c, gts_c = jnp.split(hc @ w_in, IN_OFFSETS, axis=-1)

    kac = rms_norm(heads(ka_c, A_KV), qk_g[1])
    vac = heads(va_c, A_KV)
    k_all = jnp.concatenate([kac, axial_rope(rms_norm(heads(ka, A_KV), qk_g[1]), cos, sin)], axis=1)
    v_all = jnp.concatenate([vac, heads(va, A_KV)], axis=1)
    qa_l = axial_rope(rms_norm(heads(qa, A_HEADS), qk_g[0]), cos, sin)
    ya = from_blocks(lax.map(lambda qb: gqa_attend(qb, k_all, v_all), to_blocks(qa_l, A_KV)))

    sink = sinks.reshape(W_KV, W_HEADS // W_KV)
    kwc = rms_norm(heads(kw_c, W_KV), qk_g[3])
    vwc = heads(vw_c, W_KV)
    kw_l = axial_rope(rms_norm(heads(kw, W_KV), qk_g[3]), cos, sin)
    qw_l = axial_rope(rms_norm(heads(qw, W_HEADS), qk_g[2]), cos, sin)

    def window_block(args):
        qb, kb, vb, mb = args
        return gqa_attend(qb, jnp.concatenate([kb, kwc], axis=1), jnp.concatenate([vb, vwc], axis=1), sink, mb)

    yw = from_blocks(lax.map(window_block, (to_blocks(qw_l, W_KV), band_blocks(kw_l),
                                            band_blocks(heads(vw, W_KV)), win_mask)))

    kern = hyena_kernel(n_tok, hy_f_w1, hy_f_b1, hy_f_freq, hy_f_w2, hy_f_b2, hy_f_w3)
    yh = hyena_mixer(uh, hy_short_w, hy_short_b, kern, hy_bias)
    x = x + mod[2] * merge_branches(ya, yh, yw, gts, w_branch, w_out)

    if update_ctx:
        ya_c = gqa_attend(group_q(rms_norm(heads(qa_c, A_HEADS), qk_g[0]), A_KV), kac, vac).reshape(bsz, n_ctx, -1)
        yw_c = gqa_attend(group_q(rms_norm(heads(qw_c, W_HEADS), qk_g[2]), W_KV), kwc, vwc, sink).reshape(bsz, n_ctx, -1)
        kern_c = hyena_kernel(n_ctx, hy_f_w1, hy_f_b1, hy_f_freq, hy_f_w2, hy_f_b2, hy_f_w3)
        yh_c = hyena_mixer(uh_c, hy_short_w, hy_short_b, kern_c, hy_bias)
        xc = xc + mod_c[2] * merge_branches(ya_c, yh_c, yw_c, gts_c, w_branch, w_out)

    tokens = modulate(rms_norm(x, norm2_g), mod[3], mod[4]).reshape(-1, D_MODEL)
    if update_ctx:
        tokens_c = modulate(rms_norm(xc, norm2_g), mod_c[3], mod_c[4]).reshape(-1, D_MODEL)
        tokens = jnp.concatenate([tokens, tokens_c], axis=0)
    f = hier_moe(tokens, router_g_w, router_g_b, router_e_w, router_e_b, exp_w1, exp_w3, exp_w2)
    n_lat = bsz * n_tok
    x = x + mod[5] * f[:n_lat].reshape(x.shape)
    if update_ctx:
        xc = xc + mod_c[5] * f[n_lat:].reshape(xc.shape)
    return x, xc

def setup_inputs(seed: int = 0) -> dict:
    key = jax.random.key(seed)
    ks = jax.random.split(key, 32)
    L, D = DEPTH, D_MODEL

    def nrm(k, shape, scale):
        return jax.random.normal(k, shape, F32) * scale

    return {
        'x': nrm(ks[0], (BATCH, SEQ, D), 1.0),
        'c': nrm(ks[1], (BATCH, D), 1.0),
        'ctx': nrm(ks[2], (BATCH, CTX_LEN, D), 1.0),
        'c_ctx': nrm(ks[3], (D,), 1.0),
        'ada_w': nrm(ks[4], (L, D, N_MOD * D), 0.5 * D ** -0.5),
        'ada_b': nrm(ks[5], (L, N_MOD * D), 0.02),
        'norm1_g': 1.0 + nrm(ks[6], (L, D), 0.05),
        'norm2_g': 1.0 + nrm(ks[7], (L, D), 0.05),
        'w_in': nrm(ks[8], (L, D, D_IN), D ** -0.5),
        'qk_g': 1.0 + nrm(ks[9], (L, 4, HEAD_DIM), 0.05),
        'hy_short_w': nrm(ks[10], (L, HY_SHORT, 3 * HY_WIDTH), HY_SHORT ** -0.5),
        'hy_short_b': nrm(ks[11], (L, 3 * HY_WIDTH), 0.02),
        'hy_f_w1': nrm(ks[12], (L, HY_EMB, HY_HIDDEN), HY_EMB ** -0.5),
        'hy_f_b1': nrm(ks[13], (L, HY_HIDDEN), 0.1),
        'hy_f_freq': 1.0 + nrm(ks[14], (L, HY_HIDDEN), 0.05),
        'hy_f_w2': nrm(ks[15], (L, HY_HIDDEN, HY_HIDDEN), HY_HIDDEN ** -0.5),
        'hy_f_b2': nrm(ks[16], (L, HY_HIDDEN), 0.1),
        'hy_f_w3': nrm(ks[17], (L, HY_HIDDEN, 2 * HY_WIDTH), HY_HIDDEN ** -0.5),
        'hy_bias': nrm(ks[18], (L, HY_WIDTH), 0.1),
        'sinks': nrm(ks[19], (L, W_HEADS), 1.0),
        'w_branch': nrm(ks[20], (L, N_BRANCH, HY_WIDTH, D), HY_WIDTH ** -0.5),
        'w_out': nrm(ks[21], (L, D, D), D ** -0.5),
        'router_g_w': nrm(ks[22], (L, D, N_GROUPS), D ** -0.5),
        'router_g_b': nrm(ks[23], (L, N_GROUPS), 0.01),
        'router_e_w': nrm(ks[24], (L, D, N_EXPERTS), D ** -0.5),
        'router_e_b': nrm(ks[25], (L, N_EXPERTS), 0.01),
        'exp_w1': nrm(ks[26], (L, N_EXPERTS, D, D_EXPERT), D ** -0.5),
        'exp_w3': nrm(ks[27], (L, N_EXPERTS, D, D_EXPERT), D ** -0.5),
        'exp_w2': nrm(ks[28], (L, N_EXPERTS, D_EXPERT, D), D_EXPERT ** -0.5),
    }

def reference(x, c, ctx, c_ctx, ada_w, ada_b, norm1_g, norm2_g, w_in, qk_g,
              hy_short_w, hy_short_b, hy_f_w1, hy_f_b1, hy_f_freq, hy_f_w2, hy_f_b2, hy_f_w3, hy_bias,
              sinks, w_branch, w_out, router_g_w, router_g_b, router_e_w, router_e_b, exp_w1, exp_w3, exp_w2):
    n_tok = x.shape[1]
    n_ctx = ctx.shape[1]
    rows = n_tok // GRID_W
    row_id = jnp.repeat(jnp.arange(rows), GRID_W)
    col_id = jnp.tile(jnp.arange(GRID_W), rows)
    inv_freq = ROPE_THETA ** (-jnp.arange(ROPE_FREQS, dtype=F32) / ROPE_FREQS)
    ang = jnp.stack([row_id[:, None] * inv_freq, col_id[:, None] * inv_freq], axis=1)
    cos, sin = jnp.cos(ang), jnp.sin(ang)
    nb = n_tok // Q_BLOCK
    blk = jnp.arange(nb)[:, None, None]
    qpos = blk * Q_BLOCK + jnp.arange(Q_BLOCK)[None, :, None]
    kpos = (blk - 1) * Q_BLOCK + jnp.arange(3 * Q_BLOCK)[None, None, :]
    band = (jnp.abs(kpos - qpos) <= WINDOW) & (kpos >= 0) & (kpos < n_tok)
    win_mask = jnp.concatenate([band, jnp.ones((nb, Q_BLOCK, n_ctx), dtype=bool)], axis=-1)

    xc = ctx
    for l in range(DEPTH):
        x, xc = trunk_layer(x, xc, c, c_ctx, cos, sin, win_mask, l < DEPTH - 1,
                            ada_w[l], ada_b[l], norm1_g[l], norm2_g[l], w_in[l], qk_g[l],
                            hy_short_w[l], hy_short_b[l], hy_f_w1[l], hy_f_b1[l], hy_f_freq[l], hy_f_w2[l],
                            hy_f_b2[l], hy_f_w3[l], hy_bias[l], sinks[l], w_branch[l], w_out[l],
                            router_g_w[l], router_g_b[l], router_e_w[l], router_e_b[l],
                            exp_w1[l], exp_w3[l], exp_w2[l])
    return x


_drawn_inputs = setup_inputs


def setup_inputs(seed=0):
    import zlib

    import numpy as np

    out = dict(_drawn_inputs(seed))
    spreads = {}
    factors = {'norm1_g': 4.502,
     'qk_g': 5.756,
     'hy_short_b': 8.0,
     'hy_f_b1': 5.192,
     'hy_f_freq': 8.0,
     'hy_f_b2': 5.15,
     'sinks': 8.0,
     'router_g_b': 23.643,
     'router_e_b': 44.984,
     'norm2_g': 4.793}
    for name, (base, spread) in spreads.items():
        noise = np.random.default_rng([zlib.crc32(name.encode()), seed]).standard_normal(out[name].shape)
        drawn = base * np.exp(spread * noise) if base else spread * noise
        out[name] = jnp.asarray(drawn.astype(out[name].dtype))
    for name, factor in factors.items():
        out[name] = (out[name] * factor).astype(out[name].dtype)
    return out
```

```python
from contextlib import ExitStack

import numpy as np

import concourse.bass as bass
from concourse import mybir

F32 = mybir.dt.float32
ALU = mybir.AluOpType
ACT = mybir.ActivationFunctionType
AX_X = mybir.AxisListType.X

P = 128
D = 1024
KD = D // P
SEQ = 256
LAYERS = 2
HD = 64
HEADS = 8
HW = 512
CH = HW // P
NEXP = 16
NGRP = 4
DE = 512
FE = DE // P
HID = 64
EMB = 33
SLOTS = 3
SLOT = KD * 512
TT = 4
EPS = 1e-6
BIG = 1e30
MAGIC = 12582912.0
TWO_PI = (6.28125, 0.0019350051879882812, 3.0199159819e-07)
PI_MAX = 3.1415925


def chained(engine, own, count):
    def link(ins, sem=None, value=None):
        if sem is None:
            count[0] += 1
            sem, value = own, count[0]
        ins.then_inc(sem, 1)
        engine.wait_ge(sem, value)
    return link


def tiles_of(l):
    return TT if l < LAYERS - 1 else 2


def attention_units(l):
    return [(kind, t, h) for kind in range(2) for t in range(tiles_of(l)) for h in range(HEADS)]


def keys_of(t):
    return (0, 1, 2, 3) if t < 2 else (2, 3)


LAG_PT, LAG_O = 2, 3


def attention_steps(l):
    units = attention_units(l)
    steps = []
    for i in range(len(units) + LAG_O + 2):
        if i < len(units):
            steps.append(("S", *units[i]))
        if 0 <= i - LAG_O < len(units):
            steps.append(("O", *units[i - LAG_O]))
        if 0 <= i - LAG_PT < len(units):
            steps.append(("PT", *units[i - LAG_PT]))
        j = i - LAG_O - 2
        if 0 <= j < len(units) and units[j][2] == HEADS - 1:
            steps.append(("YAT", *units[j][:2]))
    return steps


ALLB = tuple(range(8))
MOE_H1, MOE_H3, MOE_Y = (0, 1), (2, 3), (4, 5, 6, 7)


def plan_fills():
    at, count, turn = {}, [0] * 8, {}

    def add(key, banks):
        t = turn.get(banks, 0)
        turn[banks] = t + 1
        b = banks[t % len(banks)]
        at[key] = (b, count[b])
        count[b] += 1

    def repeat(banks, more):
        for b in banks:
            count[b] += more

    for l in range(LAYERS):
        T = tiles_of(l)
        add((l, "PR"), ALLB)
        if l == 0:
            add((l, "C"), ALLB)
        for k in ("F1", "F2"):
            add((l, k), ALLB)
        for t in range(2):
            for half in range(2):
                add((l, "F3", t, half), ALLB)
        add((l, "FN"), ALLB)
        for m in range(5):
            add((l, "FK", m), ALLB)
        add((l, "MOD"), ALLB)
        for k in range(KD):
            add((l, "N1", k), ALLB)
        for t in range(T):
            add((l, "QA", t), ALLB)
        for t in range(TT):
            add((l, "KV", t), ALLB)
        for t in range(T):
            add((l, "QAT", t), ALLB)
        for t in range(T):
            add((l, "QW", t), ALLB)
        for t in range(TT):
            add((l, "KVT", t), ALLB)
        for c in range(12):
            add((l, "U", c), ALLB)
        for t in range(T):
            add((l, "QWT", t), ALLB)
        for step in attention_steps(l):
            if step[0] == "S":
                add((l, *step), (0, 1, 2))
            elif step[0] == "PT" or step[0] == "YAT":
                add((l, *step), (3, 4, 5))
            elif step[3] == 0:
                add((l, "O", step[1], step[2]), (6, 7))
        for t in range(T):
            add((l, "VT", t), (0, 1, 2, 3))
        for s in range(T // 2):
            for p in range(2):
                for r in range(2):
                    add((l, "DFT", s, r, p), ALLB)
        for s in range(T // 2):
            for c in range(CH):
                add((l, "INV", s, c), ALLB)
        for s in range(T // 2):
            for half in range(2):
                add((l, "GB", 0, s, half), ALLB)
        for b in (1, 0, 2):
            for c in range(KD):
                add((l, "GATE", b, c), ALLB)
                add((l, "BR", b, c), ALLB)
        for half in range(2):
            for t in range(T):
                add((l, "OUT", half, t), ALLB)
        for k in range(KD):
            add((l, "N2", k), ALLB)
        for t in range(T):
            add((l, "LG", t), ALLB)
        for s in range(T // 2):
            for half in range(2):
                add((l, "GB", 1, s, half), ALLB)
        for i in range(FE):
            add((l, "H1", i), MOE_H1)
            add((l, "H3", i), MOE_H3)
        for t in range(T):
            for half in range(2):
                add((l, "Y", t, half), MOE_Y)
        repeat(MOE_H1 + MOE_H3, (NEXP - 1) * FE // 2)
        repeat(MOE_Y, (NEXP - 1) * T // 2)
    return at


def weight_loads():
    out = []
    for l in range(LAYERS):
        for j in range(12):
            out.append(((l, "ADA", j), None))
        for what in ("QA", "KV", "QW"):
            out.append(((l, what, 0), (l, what, (TT if what == "KV" else tiles_of(l)) - 1)))
        for j in range(3):
            out.append(((l, "U", j), (l, "U", 4 * j + 3)))
        for b in (1, 0, 2):
            out.append(((l, "BR", b), (l, "BR", b, KD - 1)))
            for half in range(2):
                out.append(((l, "GATE", b, half), (l, "GATE", b, 4 * half + 3)))
        for half in range(2):
            out.append(((l, "OUT", half), (l, "OUT", half, tiles_of(l) - 1)))
        for e in range(NEXP):
            for what in ("W1", "W3", "W2"):
                out.append(((l, what, e), None))
    return out


def build(nc, x, c, ctx_in, c_ctx, ada_w, ada_b, norm1_g, norm2_g, w_in, qk_g, hy_short_w, hy_short_b, hy_f_w1,
          hy_f_b1, hy_f_freq, hy_f_w2, hy_f_b2, hy_f_w3, hy_bias, sinks, w_branch, w_out, router_g_w, router_g_b,
          router_e_w, router_e_b, exp_w1, exp_w3, exp_w2, k_ident, k_dft, k_idft, k_decay, k_z, k_rope, k_mask,
          k_first, out):
    fill_at = plan_fills()
    loads = weight_loads()
    load_no = {key: n for n, (key, _) in enumerate(loads)}
    loaded_at, total = [], [0] * SLOTS
    for n, (key, _) in enumerate(loads):
        total[n % SLOTS] += 32 if key[1] == "KV" else 16
        loaded_at.append(total[n % SLOTS])

    with ExitStack() as stack:
        def sb(name, shape):
            return stack.enter_context(nc.sbuf_tensor(name, shape, F32))

        def sem(name):
            return stack.enter_context(nc.semaphore(name))

        ps = [stack.enter_context(nc.psum_tensor(f"bank{b}", [P, 512], F32)) for b in range(8)]

        X = sb("X", [P, TT, D])
        HT = sb("HT", [P, KD, TT * P])
        ring = sb("ring", [P, SLOTS, SLOT])
        R1 = sb("R1", [P, 12 * 512])
        R2 = sb("R2", [P, TT * D])
        R3 = sb("R3", [P, 9216])
        KSG = sb("KSG", [P, 5 * HW])
        YA = sb("YA", [P, 2, 512])
        TMP = sb("TMP", [P, 4, 512])
        ident = sb("ident", [P, P])
        ones = sb("ones", [P, P])
        DF = sb("DF", [P, 2, 6 * P])
        IF = sb("IF", [P, 4, SEQ])
        ROPE = sb("ROPE", [P, 2, 2, HD])
        CG = sb("CG", [P, 3, 4, HD])
        SG = sb("SG", [P, 2, 4, HD])
        MASK = sb("MASK", [P, 2, SEQ])
        QKG = sb("QKG", [P, LAYERS, 4, HD])
        SINK = sb("SINK", [P, LAYERS, HEADS])
        NSINK = sb("NSINK", [P, LAYERS, HEADS])
        PR = sb("PR", [116, LAYERS, P])
        PC = sb("PC", [P, 116])
        CR = sb("CR", [16, P])
        CC = sb("CC", [P, 16])
        FP = sb("FP", [HID, LAYERS, 3])
        FW = sb("FW", [HID, LAYERS, 2, HID])
        MOD = sb("MOD", [P, 48, 2])
        AM = sb("AM", [P, 2, KD, 2])
        RW = sb("RW", [P, LAYERS, KD, 20])
        RB = sb("RB", [P, LAYERS, 20])
        FIRST = sb("FIRST", [P, 20])
        ST = sb("ST", [P, 64])
        HS = sb("HS", [P, 2, 4, HEADS])
        AT = sb("AT", [P, 2, 5, HEADS])
        NMX = sb("NMX", [P, 4])
        CMB = sb("CMB", [P, TT, NEXP])
        CE = sb("CE", [P, TT])
        HALF = sb("HALF", [P, 16])

        KS = KSG[:, :].rearrange("p (m n) -> p m n", m=5)
        GB = KSG[:, 0:2 * D].rearrange("p (s d) -> p s d", s=2)
        UC = R1[:, :].rearrange("p (c n) -> p c n", c=12)
        MT = R1[:, 2048:6144].rearrange("p (k n) -> p k n", k=KD)
        GH = R1[:, 0:2048].rearrange("p (f n) -> p f n", f=FE)
        XN = R2[:, :].rearrange("p (t d) -> p t d", t=TT)
        YT = R2[:, :].rearrange("p (a c n) -> p a c n", a=2, c=CH)
        FACC = R2[:, :].rearrange("p (t d) -> p t d", t=TT)
        DEC = R3[:, 0:2048].rearrange("p (t h n) -> p t h n", t=2, h=2)
        W3 = R3[0:HID, 2048:3072]
        FH = R3[:, 3072:5120].rearrange("p (t h n) -> p t h n", t=2, h=2)
        FAB = R3[:, 5120:7168].rearrange("p (t h n) -> p t h n", t=2, h=2)
        FN = R3[:, 7168:7680]
        Z = R3[0:EMB, 7680:7936]
        FT = R3[0:HID, 7936:9216].rearrange("p (a n) -> p a n", a=5)
        QT = R3[:, 0:4096].rearrange("p (a c n) -> p a c n", a=2, c=4)
        KN = YA[:, :, :].rearrange("p a (b n) -> p (a b) n", b=2)
        KT = R3[:, 4096:5120].rearrange("p (a n) -> p a n", a=2)
        V = R3[:, 5120:6144].rearrange("p (t a n) -> p t a n", t=TT, a=2)
        QN = R3[:, 6144:8192].rearrange("p (t n) -> p t n", t=4)
        PB = R3[:, 6144:7680].rearrange("p (t n) -> p t n", t=3)
        PTB = R3[:, 7680:9216].rearrange("p (t n) -> p t n", t=3)
        RT = R3[:, 5120:5888].rearrange("p (a t n) -> p a t n", a=12, t=TT)
        VT = R3[:, 0:2048].rearrange("p (t n) -> p t n", t=TT)
        YS = R3[:, 2048:6144].rearrange("p (s f n) -> p s f n", s=2, f=4)

        bank_full = [sem(f"bank_full{b}") for b in range(8)]
        bank_free = [sem(f"bank_free{b}") for b in range(8)]
        slot_loaded = [sem(f"slot_loaded{s}") for s in range(SLOTS)]
        consts_loaded = sem("consts_loaded")
        params_loaded = sem("params_loaded")
        x_loaded = sem("x_loaded")
        filter_loaded = sem("filter_loaded")
        out_stored = sem("out_stored")
        dve_steps = sem("dve_steps")
        act_steps = sem("act_steps")
        pool_steps = sem("pool_steps")
        cond_ready = sem("cond_ready")
        ones_ready = sem("ones_ready")
        filter_arg = sem("filter_arg")
        filter_sin = sem("filter_sin")
        qk_ready = sem("qk_ready")
        merged = sem("merged")
        ada_read = sem("ada_read")
        filter_abs = sem("filter_abs")
        filter_ab = sem("filter_ab")
        mod_ready = sem("mod_ready")
        squares = sem("squares")
        rstd_ready = sem("rstd_ready")
        rows_ready = sem("rows_ready")
        head_squares = sem("head_squares")
        head_sums = sem("head_sums")
        head_rstd = sem("head_rstd")
        conv_started = sem("conv_started")
        gated_v = sem("gated_v")
        neg_max = sem("neg_max")
        ya_ready = sem("ya_ready")
        spec_ready = sem("spec_ready")
        yh_ready = sem("yh_ready")
        residual_added = sem("residual_added")
        logits_ready = sem("logits_ready")
        logits_exp = sem("logits_exp")
        experts_done = sem("experts_done")

        def bank(key):
            return ps[fill_at[key][0]]

        def wait_bank(eng, key, more=0):
            b, n = fill_at[key]
            if n:
                eng.wait_ge(bank_free[b], more + n)

        def wait_full(eng, key, more=0):
            b, n = fill_at[key]
            eng.wait_ge(bank_full[b], more + n + 1)

        def wait_read(eng, key, more=0):
            b, n = fill_at[key]
            eng.wait_ge(bank_free[b], more + n + 1)

        def full(ins, key):
            ins.then_inc(bank_full[fill_at[key][0]], 1)

        def slot_of(key):
            return load_no[key] % SLOTS

        def wait_slot(eng, key, more=0):
            n = load_no[key]
            eng.wait_ge(slot_loaded[n % SLOTS], more + loaded_at[n])

        def slot(key):
            return ring[:, slot_of(key), :]

        def slot_kn(key):
            return slot(key).rearrange("p (k n) -> p k n", k=KD)

        T0 = tiles_of(0)
        rows_before = [0, 2 * T0 + (TT - T0)]
        proj = {}
        for l in range(LAYERS):
            for what in ("QA", "KV", "QW"):
                for t in range(TT if what == "KV" else tiles_of(l)):
                    proj[(l, what, t)] = len(proj)
        units = {}
        for l in range(LAYERS):
            for u in attention_units(l):
                units[(l, *u)] = len(units)
        groups = {}
        for l in range(LAYERS):
            for kind in range(2):
                for t in range(tiles_of(l)):
                    groups[(l, kind, t)] = len(groups)
        seqs = {}
        for l in range(LAYERS):
            for s in range(tiles_of(l) // 2):
                seqs[(l, s)] = len(seqs)

        def row_no(l, norm, t):
            return (0 if l == 0 else TT + T0) + (TT if norm else 0) + t

        def residual_no(l, half, t):
            return (0 if l == 0 else 2 * T0) + half * tiles_of(l) + t

        block = stack.enter_context(nc.Block())

        @block.sync
        def _(sp):
            def source(key):
                l, what, j = key[:3]
                if what == "ADA":
                    return ada_w[l].rearrange("(k p) n -> p k n", p=P)[:, :, 512 * j:512 * j + 512]
                if what == "QA":
                    return w_in[l].rearrange("(k p) n -> p k n", p=P)[:, :, 0:512]
                if what == "QW":
                    return w_in[l].rearrange("(k p) n -> p k n", p=P)[:, :, 2304:2816]
                if what == "U":
                    return w_in[l].rearrange("(k p) n -> p k n", p=P)[:, :, 768 + 512 * j:1280 + 512 * j]
                if what == "GATE":
                    n0 = 3072 + D * j + 512 * key[3]
                    return w_in[l].rearrange("(k p) n -> p k n", p=P)[:, :, n0:n0 + 512]
                if what == "BR":
                    return w_branch[l, j].rearrange("(k p) n -> p k n", p=P)
                if what == "OUT":
                    return w_out[l].rearrange("(k p) n -> p k n", p=P)[:, :, 512 * j:512 * j + 512]

            def expert_source(l, what, e):
                w = {"W1": exp_w1, "W3": exp_w3, "W2": exp_w2}[what]
                return w[l, e].rearrange("(k p) n -> p k n", p=P)

            def wait_free(l, n, more=None):
                if n < SLOTS:
                    return
                key, last = loads[n - SLOTS]
                if key[1] == "ADA" and key[2] < 11:
                    sp.wait_ge(ada_read, 11 * key[0] + key[2] + 1)
                elif key[1] == "ADA":
                    wait_full(sp, (key[0], "MOD"))
                elif last is None:
                    raise AssertionError(key)
                else:
                    wait_full(sp, last)

            sp.dma_start(X[:, 0:2, :], x[0].rearrange("(t p) d -> p t d", p=P)).then_inc(x_loaded, 16)
            sp.dma_start(X[:, 2:4, :], ctx_in[0].rearrange("(t p) d -> p t d", p=P)).then_inc(x_loaded, 16)
            for l in range(LAYERS):
                T = tiles_of(l)
                if l:
                    wait_full(sp, (l - 1, "INV", tiles_of(l - 1) // 2 - 1, CH - 1))
                sp.dma_start(Z, k_z).then_inc(filter_loaded, 16)
                sp.dma_start(W3, hy_f_w3[l]).then_inc(filter_loaded, 16)
                sp.dma_start(DEC, k_decay.rearrange("(t p) h n -> p t h n", p=P)).then_inc(filter_loaded, 16)
                for n, (key, _) in enumerate(loads):
                    if key[0] != l or key[1] in ("W1", "W3", "W2"):
                        continue
                    if n >= SLOTS and loads[n - SLOTS][1] is None and loads[n - SLOTS][0][1] in ("W1", "W3", "W2"):
                        pk = loads[n - SLOTS][0]
                        pl, pT = pk[0], tiles_of(pk[0])
                        if pk[1] == "W2":
                            wait_full(sp, (pl, "Y", pT - 1, 1), (NEXP - 1) * pT // 2)
                        else:
                            wait_full(sp, (pl, "H3", FE - 1), (NEXP - 1) * FE // 2)
                    else:
                        wait_free(l, n)
                    if key[1] == "KV":
                        dst = slot(key).rearrange("p (k a n) -> p k a n", k=KD, a=2)
                        for a in range(2):
                            n0 = 512 + 2304 * a
                            src = w_in[l].rearrange("(k p) n -> p k n", p=P)[:, :, n0:n0 + 256]
                            sp.dma_start(dst[:, :, a, :], src).then_inc(slot_loaded[n % SLOTS], 16)
                        continue
                    kk = 4 if key[1] == "BR" else KD
                    sp.dma_start(slot(key).rearrange("p (k n) -> p k n", k=kk), source(key)) \
                        .then_inc(slot_loaded[n % SLOTS], 16)
                for what in ("W1", "W3", "W2"):
                    n = load_no[(l, what, 0)]
                    wait_free(l, n)
                    kk = FE if what == "W2" else KD
                    sp.dma_start(slot((l, what, 0)).rearrange("p (k n) -> p k n", k=kk), expert_source(l, what, 0)) \
                        .then_inc(slot_loaded[n % SLOTS], 16)
                with sp.Fori(1, NEXP) as e:
                    for what in ("W1", "W3", "W2"):
                        n = load_no[(l, what, 0)]
                        if what == "W2":
                            b, m = fill_at[(l, "Y", T - 1, 1)]
                            sp.wait_ge(bank_full[b], e * (T // 2) + (m + 1 - T // 2))
                        else:
                            b, m = fill_at[(l, "H3", FE - 1)]
                            sp.wait_ge(bank_full[b], e * (FE // 2) + (m + 1 - FE // 2))
                        kk = FE if what == "W2" else KD
                        sp.dma_start(slot((l, what, 0)).rearrange("p (k n) -> p k n", k=kk),
                                     expert_source(l, what, e)).then_inc(slot_loaded[n % SLOTS], 16)
            for t in range(2):
                sp.wait_ge(experts_done, T0 + t + 1)
                sp.dma_start(out[0, t * P:(t + 1) * P, :], X[:, t, :]).then_inc(out_stored, 16)
            sp.wait_ge(out_stored, 32)

        @block.gpsimd
        def _(pool):
            link = chained(pool, pool_steps, [0])
            nc.gpsimd.memset(ones[:, :], 1.0).then_inc(ones_ready, 1)
            nc.gpsimd.memset(HALF[:, :], -0.5).then_inc(ones_ready, 1)
            pool.wait_ge(ones_ready, 2)

            def rms_rows(l, norm):
                for t in range(TT if not norm else tiles_of(l)):
                    i = row_no(l, norm, t)
                    pool.wait_ge(squares, i + 1)
                    link(nc.gpsimd.tensor_scalar(ST[:, 8 + t:9 + t], ST[:, t:t + 1], 1.0 / D, EPS, ALU.mult, ALU.add))
                    link(nc.gpsimd.tensor_tensor(ST[:, 16 + t:17 + t], ST[:, 8 + t:9 + t], HALF[:, 0:1], ALU.pow),
                                rstd_ready, i + 1)

            def rms_heads(l, what, t):
                i = proj[(l, what, t)]
                pool.wait_ge(head_sums, i + 1)
                link(nc.gpsimd.tensor_scalar(HS[:, i % 2, 1, :], HS[:, i % 2, 0, :], 1.0 / HD, EPS, ALU.mult, ALU.add))
                link(nc.gpsimd.tensor_tensor(HS[:, i % 2, 2, :], HS[:, i % 2, 1, :], HALF[:, 0:HEADS], ALU.pow),
                            head_rstd, i + 1)

            for l in range(LAYERS):
                rms_rows(l, 0)
                for what in ("QA", "KV", "QW"):
                    for t in range(TT if what == "KV" else tiles_of(l)):
                        rms_heads(l, what, t)
                rms_rows(l, 1)

        @block.scalar
        def _(act):
            link = chained(act, act_steps, [0])

            def read(ins, key, more=0):
                b, n = fill_at[key]
                link(ins, bank_free[b], more + n + 1)

            small = []
            small.append((CR[0:8, :], c[0].rearrange("(k p) -> k p", p=P)))
            small.append((CR[8:16, :], c_ctx.rearrange("(k p) -> k p", p=P)))
            small.append((ident[:, :], k_ident))
            for l in range(LAYERS):
                small += [
                    (PR[0:48, l, :], ada_b[l].rearrange("(k p) -> k p", p=P)),
                    (PR[48:56, l, :], norm1_g[l].rearrange("(k p) -> k p", p=P)),
                    (PR[56:64, l, :], norm2_g[l].rearrange("(k p) -> k p", p=P)),
                    (PR[64:100, l, :], hy_short_w[l].rearrange("j (k p) -> (j k) p", p=P)),
                    (PR[100:112, l, :], hy_short_b[l].rearrange("(k p) -> k p", p=P)),
                    (PR[112:116, l, :], hy_bias[l].rearrange("(k p) -> k p", p=P)),
                    (FP[:, l, 0:1], hy_f_b1[l].rearrange("(p a) -> p a", a=1)),
                    (FP[:, l, 1:2], hy_f_freq[l].rearrange("(p a) -> p a", a=1)),
                    (FP[:, l, 2:3], hy_f_b2[l].rearrange("(p a) -> p a", a=1)),
                    (FW[0:EMB, l, 0, :], hy_f_w1[l]),
                    (FW[:, l, 1, :], hy_f_w2[l]),
                    (QKG[:, l, :, :], qk_g[l].partition_broadcast(P)),
                    (SINK[:, l, :], sinks[l].partition_broadcast(P)),
                    (RB[:, l, 0:4], router_g_b[l].partition_broadcast(P)),
                    (RB[:, l, 4:20], router_e_b[l].partition_broadcast(P)),
                    (RW[:, l, :, 0:4], router_g_w[l].rearrange("(k p) n -> p k n", p=P)),
                    (RW[:, l, :, 4:20], router_e_w[l].rearrange("(k p) n -> p k n", p=P)),
                ]
            small += [
                (DF[:, :, :], k_dft.rearrange("(t p) n -> p t n", p=P)),
                (IF[:, :, :], k_idft.rearrange("(t p) n -> p t n", p=P)),
                (ROPE[:, :, :, :], k_rope.rearrange("(t p) a n -> p t a n", p=P)),
                (MASK[:, :, :], k_mask.rearrange("(t p) n -> p t n", p=P)),
                (FIRST[:, :], k_first.partition_broadcast(P)),
            ]
            assert len(small) == SMALL
            for dst, src in small:
                act.dma_start(dst, src).then_inc(params_loaded, 16)

            act.wait_ge(params_loaded, 16 * SMALL)
            link(nc.scalar.activation(CR[:, :], CR[:, :], ACT.Silu), cond_ready, 1)

            def norm_squares(l, norm):
                T = TT if not norm else tiles_of(l)
                for t in range(T):
                    if norm:
                        act.wait_ge(residual_added, residual_no(l, 1, t) + 1)
                    elif l:
                        act.wait_ge(experts_done, t + 1)
                    elif t == 0:
                        act.wait_ge(x_loaded, 32)
                    if norm and t == 0:
                        wait_full(act, (l, "BR", 2, KD - 1))
                    link(nc.scalar.activation(XN[:, t, :], X[:, t, :], ACT.Square, accum_out=ST[:, t:t + 1]),
                                squares, row_no(l, norm, t) + 1)

            def head_square(l, what, t):
                i = proj[(l, what, t)]
                key = (l, what, t)
                wait_full(act, key)
                if what == "KV":
                    b = bank(key)
                    for kind in range(2):
                        link(nc.scalar.copy(V[:, t, kind, :], b[:, 256 * kind + 128:256 * kind + 256]))
                if i >= 2:
                    act.wait_ge(head_sums, i - 1)
                link(nc.scalar.activation(TMP[:, i % 2, :], bank(key)[:, :], ACT.Square), head_squares, i + 1)

            def copy_out(dst, key, src=None):
                wait_full(act, key)
                read(nc.scalar.copy(dst, bank(key)[:, :] if src is None else src), key)

            def copy_gates(l, which):
                for s in range(tiles_of(l) // 2):
                    for half in range(2):
                        copy_out(GB[:, s, 512 * half:512 * half + 512], (l, "GB", which, s, half))

            for l in range(LAYERS):
                T = tiles_of(l)
                N = T * P
                norm_squares(l, 0)
                for i in range(2):
                    act.wait_ge(filter_arg, 2 * l + i + 1)
                    link(nc.scalar.activation(FT[:, 3 + i, :], FT[:, 1, :], ACT.Sin), filter_sin, 2 * l + i + 1)
                for t in range(2):
                    for half in range(2):
                        j = 4 * l + 2 * t + half
                        wait_read(act, (l, "F3", t, half))
                        link(nc.scalar.activation(DEC[:, t, half, :], FH[:, t, half, :], ACT.Abs),
                                    filter_abs, j + 1)
                for t in range(T):
                    head_square(l, "QA", t)
                for t in range(TT):
                    head_square(l, "KV", t)
                for t in range(T):
                    copy_out(QT[:, 0, :, t * P:(t + 1) * P], (l, "QAT", t),
                             bank((l, "QAT", t))[:, :].rearrange("p (c n) -> p c n", c=4))
                for t in range(T):
                    head_square(l, "QW", t)
                for t in range(TT):
                    copy_out(KT[:, :, t * P:(t + 1) * P], (l, "KVT", t),
                             bank((l, "KVT", t))[:, 0:256].rearrange("p (c n) -> p c n", c=2))
                for ch in range(12):
                    key = (l, "U", ch)
                    wait_full(act, key)
                    link(nc.scalar.activation(UC[:, ch, 0:N], bank(key)[:, 0:N], ACT.Identity,
                                                     bias=PC[:, 100 + ch:101 + ch], scale=PC[:, 76 + ch:77 + ch]),
                                conv_started, 12 * l + ch + 1)
                for t in range(T):
                    copy_out(QT[:, 1, :, t * P:(t + 1) * P], (l, "QWT", t),
                             bank((l, "QWT", t))[:, :].rearrange("p (c n) -> p c n", c=4))
                yat = {i: s for i, s in enumerate(attention_steps(l))}
                for i, s in yat.items():
                    if s[0] == "S":
                        _, kind, t, h = s
                        u = units[(l, kind, t, h)]
                        g = groups[(l, kind, t)]
                        key = (l, *s)
                        nk = len(keys_of(t)) * P
                        act.wait_ge(neg_max, u + 1)
                        if u >= 3:
                            prev = [k for k, v in units.items() if v == u - 3][0]
                            wait_full(act, (prev[0], "PT", *prev[1:]))
                        nm = NMX[:, u % 4:u % 4 + 1]
                        if kind:
                            link(nc.scalar.activation(AT[:, g % 2, 2, h:h + 1], SINK[:, l, h:h + 1], ACT.Exp, bias=nm))
                        read(nc.scalar.activation(PB[:, u % 3, 0:nk], bank(key)[:, 0:nk], ACT.Exp, bias=nm,
                                                  accum_out=AT[:, g % 2, 1, h:h + 1]), key)
                    elif s[0] == "YAT":
                        _, kind, t = s
                        copy_out(YT[:, kind, :, t * P:(t + 1) * P], (l, *s),
                                 bank((l, *s))[:, :].rearrange("p (c n) -> p c n", c=4))
                for t in range(T):
                    copy_out(VT[:, t, :], (l, "VT", t))
                copy_gates(l, 0)
                for j, b in enumerate((1, 0, 2)):
                    for ch in range(KD):
                        key = (l, "GATE", b, ch)
                        i = KD * j + ch - 2
                        wait_full(act, key)
                        if i >= 0:
                            wait_read(act, (l, "BR", (1, 0, 2)[i // KD], i % KD))
                        read(nc.scalar.activation(TMP[:, ch % 2, 0:N], bank(key)[:, 0:N], ACT.Sigmoid), key)
                norm_squares(l, 1)
                copy_gates(l, 1)
                act.wait_ge(logits_ready, l + 1)
                link(nc.scalar.activation(RT[:, 1, 0:T, 0:5], RT[:, 0, 0:T, 0:5], ACT.Exp), logits_exp, l + 1)
                with act.Fori(0, NEXP) as e:
                    for i in range(FE):
                        key = (l, "H1", i)
                        wait_full(act, key, e * (FE // 2))
                        prev = (l, "H3", (i - 2) % FE)
                        b, n = fill_at[prev]
                        act.wait_ge(bank_free[b], e * (FE // 2) + (n + 1 - (FE // 2 if i < 2 else 0)))
                        b, n = fill_at[key]
                        nc.scalar.activation(TMP[:, i % 2, 0:N], bank(key)[:, 0:N], ACT.Silu).then_inc(bank_free[b], 1)

        @block.vector
        def _(dve):
            steps = [0]
            link = chained(dve, dve_steps, steps)
            tt, ts, stt = nc.vector.tensor_tensor, nc.vector.tensor_scalar, nc.vector.scalar_tensor_tensor

            def read(ins, key, more=0):
                b, n = fill_at[key]
                link(ins, bank_free[b], more + n + 1)

            def normalise_rows(l, norm):
                for t in range(TT if not norm else tiles_of(l)):
                    i = row_no(l, norm, t)
                    dve.wait_ge(rstd_ready, i + 1)
                    link(ts(XN[:, t, :], X[:, t, :], ST[:, 16 + t:17 + t], None, ALU.mult), rows_ready, i + 1)

            def modulate(l, norm):
                T = TT if not norm else tiles_of(l)
                for k in range(KD):
                    key = (l, "N2" if norm else "N1", k)
                    wait_full(dve, key)
                    for s in range(T // 2):
                        ins = ts(HT[:, k, SEQ * s:SEQ * s + SEQ], bank(key)[:, SEQ * s:SEQ * s + SEQ],
                                 AM[:, norm, k, s:s + 1], MOD[:, (24 if norm else 0) + k, s:s + 1], ALU.mult, ALU.add)
                        if s == T // 2 - 1:
                            read(ins, key)
                        else:
                            link(ins)

            def head_sum(l, what, t):
                i = proj[(l, what, t)]
                dve.wait_ge(head_squares, i + 1)
                sq = TMP[:, i % 2, :]
                if what == "KV":
                    sq = sq.rearrange("p (a n) -> p a n", a=2)[:, :, 0:P].rearrange("p a (h d) -> p a h d", d=HD)
                    dst = HS[:, i % 2, 0, 0:4].rearrange("p (a h) -> p a h", a=2)
                    link(nc.vector.memset(HS[:, i % 2, 0, 4:8], 1.0))
                else:
                    sq = sq.rearrange("p (h d) -> p h d", d=HD)
                    dst = HS[:, i % 2, 0, :]
                link(nc.vector.tensor_reduce(dst, sq, AX_X, ALU.add), head_sums, i + 1)

            def head_norm(l, what, t):
                i = proj[(l, what, t)]
                key = (l, what, t)
                dve.wait_ge(head_rstd, i + 1)
                if what == "QW":
                    wait_full(dve, (l, "QAT", t))
                rot = t < 2
                tile = t if rot else 2
                if what == "KV":
                    src = bank(key)[:, :].rearrange("p (a n) -> p a n", a=2)[:, :, 0:P] \
                        .rearrange("p a (h d) -> p a h d", d=HD)
                    rs = HS[:, i % 2, 2, 0:4].rearrange("p (a h) -> p a h", a=2).unsqueeze(3) \
                        .to_broadcast([P, 2, 2, HD])
                    mid = TMP[:, 2, 0:256].rearrange("p (a h d) -> p a h d", a=2, d=HD)
                    dst = KN[:, t, :].rearrange("p (a h d) -> p a h d", a=2, d=HD)
                    read(tt(mid, src, rs, ALU.mult), key)
                    for a in range(2):
                        rotate(dst[:, a], mid[:, a], tile, 2 + a, 2, rot, i + 1 if a else None)
                else:
                    src = bank(key)[:, :].rearrange("p (h d) -> p h d", d=HD)
                    rs = HS[:, i % 2, 2, :].unsqueeze(2).to_broadcast([P, HEADS, HD])
                    mid = TMP[:, 2, :].rearrange("p (h d) -> p h d", d=HD)
                    dst = QN[:, t, :].rearrange("p (r g d) -> p g r d", g=2, d=HD)
                    read(tt(mid, src, rs, ALU.mult), key)
                    rotate(dst, mid, tile, 0 if what == "QA" else 1, HEADS, rot, i + 1)

            def rotate(dst, mid, tile, kind, nh, rot, done):
                cg = CG[:, tile, kind, :].unsqueeze(1)
                if nh == HEADS:
                    def by_pair(a):
                        return a.rearrange("p (g r) d -> p g r d", g=2)

                    ins = tt(dst, by_pair(mid), cg.unsqueeze(1).to_broadcast([P, 2, 4, HD]), ALU.mult)
                else:
                    def by_pair(a):
                        return a

                    ins = tt(dst, mid, cg.to_broadcast([P, nh, HD]), ALU.mult)
                if not rot and done:
                    link(ins, qk_ready, done)
                else:
                    link(ins)
                if rot:
                    tmp = TMP[:, 3, 0:nh * HD].rearrange("p (h a b f) -> p h a b f", a=2, b=2, f=16)
                    m5 = mid.rearrange("p h (a b f) -> p h a b f", a=2, b=2)
                    sg = SG[:, tile, kind, :].rearrange("p (a b f) -> p a b f", a=2, b=2)
                    for b in range(2):
                        s1 = sg[:, :, b, :].unsqueeze(1).to_broadcast([P, nh, 2, 16])
                        link(tt(tmp[:, :, :, b, :], m5[:, :, :, 1 - b, :], s1, ALU.mult))
                    ins = tt(dst, dst, by_pair(TMP[:, 3, 0:nh * HD].rearrange("p (h d) -> p h d", d=HD)), ALU.add)
                    if done:
                        link(ins, qk_ready, done)
                    else:
                        link(ins)

            dve.wait_ge(params_loaded, 16 * SMALL)
            link(ts(NSINK[:, :, :], SINK[:, :, :], -1.0, None, ALU.mult))
            for l in range(LAYERS):
                T = tiles_of(l)
                N = T * P
                wait_full(dve, (l, "PR"))
                read(nc.vector.tensor_copy(PC[:, :], bank((l, "PR"))[:, 0:116]), (l, "PR"))
                if l == 0:
                    wait_full(dve, (l, "C"))
                    read(nc.vector.tensor_copy(CC[:, :], bank((l, "C"))[:, 0:16]), (l, "C"))
                for kind, row in enumerate((0, 2, 1, 3)):
                    g = QKG[:, l, row, :]
                    scale = HD ** -0.5 if kind < 2 else 1.0
                    link(ts(CG[:, 2, kind, :], g, scale, None, ALU.mult))
                for tile in range(2):
                    link(tt(CG[:, tile, :, :], CG[:, 2, :, :],
                            ROPE[:, tile, 0, :].unsqueeze(1).to_broadcast([P, 4, HD]), ALU.mult))
                    gg = CG[:, 2, :, :].rearrange("p k (a b f) -> p k a b f", a=2, b=2)
                    so = SG[:, tile, :, :].rearrange("p k (a b f) -> p k a b f", a=2, b=2)
                    sn = ROPE[:, tile, 1, :].rearrange("p (a b f) -> p a b f", a=2, b=2)
                    for b in range(2):
                        link(tt(so[:, :, :, b, :], gg[:, :, :, 1 - b, :],
                                sn[:, :, b, :].unsqueeze(1).to_broadcast([P, 4, 2, 16]), ALU.mult))
                normalise_rows(l, 0)
                for i in range(2):
                    key = (l, f"F{i + 1}")
                    wait_full(dve, key)
                    read(ts(FT[:, 0, :], bank(key)[0:HID, 0:SEQ], FP[:, l, 2 * i:2 * i + 1], FP[:, l, 1:2],
                            ALU.add, ALU.mult), key)
                    link(ts(FT[:, 1, :], FT[:, 0, :], 1.0 / (2 * np.pi), MAGIC, ALU.mult, ALU.add))
                    link(ts(FT[:, 2, :], FT[:, 1, :], -MAGIC, None, ALU.add))
                    for part in TWO_PI:
                        link(stt(FT[:, 0, :], FT[:, 2, :], -part, FT[:, 0, :], ALU.mult, ALU.add))
                    link(ts(FT[:, 1, :], FT[:, 0, :], PI_MAX, -PI_MAX, ALU.min, ALU.max),
                                filter_arg, 2 * l + i + 1)
                    dve.wait_ge(filter_sin, 2 * l + i + 1)
                for t in range(2):
                    for half in range(2):
                        key = (l, "F3", t, half)
                        wait_full(dve, key)
                        if t == 0 and half == 0:
                            dve.wait_ge(filter_loaded, 48 * (l + 1))
                        read(tt(FH[:, t, half, :], bank(key)[:, :], DEC[:, t, half, :], ALU.mult), key)
                for t in range(2):
                    link(tt(FAB[:, t, 0, :], FH[:, t, 0, :], FH[:, t, 1, :], ALU.add))
                    link(tt(FAB[:, t, 1, :], FH[:, t, 0, :], FH[:, t, 1, :], ALU.subtract),
                                filter_ab, 2 * l + t + 1)
                wait_full(dve, (l, "FN"))
                read(nc.vector.reciprocal(FN, bank((l, "FN"))[:, :]), (l, "FN"))
                for m in range(5):
                    key = (l, "FK", m)
                    wait_full(dve, key)
                    read(tt(KS[:, m, :], bank(key)[:, :], FN, ALU.mult), key)
                key = (l, "MOD")
                wait_full(dve, key)
                read(tt(MOD[:, :, :], bank(key)[:, 0:96].rearrange("p (m s) -> p m s", s=2),
                        PC[:, 0:48].unsqueeze(2).to_broadcast([P, 48, 2]), ALU.add), key)
                for norm in range(2):
                    m0 = 24 * norm + 8
                    link(ts(AM[:, norm, :, :], MOD[:, m0:m0 + 8, :], 1.0, None, ALU.add))
                    ins = tt(AM[:, norm, :, :], AM[:, norm, :, :],
                             PC[:, 48 + 8 * norm:56 + 8 * norm].unsqueeze(2).to_broadcast([P, KD, 2]), ALU.mult)
                    if norm:
                        link(ins, mod_ready, l + 1)
                    else:
                        link(ins)
                modulate(l, 0)
                order = [("QA", t) for t in range(T)] + [("KV", t) for t in range(TT)] + [("QW", t) for t in range(T)]
                head_sum(l, *order[0])
                for i, (what, t) in enumerate(order):
                    if i + 1 < len(order) and order[i + 1][0] == what:
                        head_sum(l, *order[i + 1])
                    head_norm(l, what, t)
                    if i + 1 < len(order) and order[i + 1][0] != what:
                        head_sum(l, *order[i + 1])
                S2 = T // 2
                for ch in range(12):
                    key = (l, "U", ch)
                    dve.wait_ge(conv_started, 12 * l + ch + 1)
                    src = bank(key)[:, 0:N].rearrange("p (s n) -> p s n", s=S2)
                    dst = UC[:, ch, 0:N].rearrange("p (s n) -> p s n", s=S2)
                    link(stt(dst[:, :, 1:SEQ], src[:, :, 0:SEQ - 1], PC[:, 64 + ch:65 + ch], dst[:, :, 1:SEQ],
                             ALU.mult, ALU.add))
                    read(stt(dst[:, :, 0:SEQ - 1], src[:, :, 1:SEQ], PC[:, 88 + ch:89 + ch], dst[:, :, 0:SEQ - 1],
                             ALU.mult, ALU.add), key)
                link(tt(UC[:, 8:12, 0:N], UC[:, 8:12, 0:N], UC[:, 4:8, 0:N], ALU.mult), gated_v, l + 1)
                for s in attention_steps(l):
                    if s[0] == "S":
                        _, kind, t, h = s
                        u = units[(l, kind, t, h)]
                        key = (l, *s)
                        nk = len(keys_of(t)) * P
                        wait_full(dve, key)
                        if kind and t < 2:
                            link(tt(bank(key)[:, 0:SEQ], bank(key)[:, 0:SEQ], MASK[:, t, :], ALU.add))
                        nm = NMX[:, u % 4:u % 4 + 1]
                        if u >= 4:
                            prev = [k for k, v in units.items() if v == u - 4][0]
                            wait_read(dve, (prev[0], "S", *prev[1:]))
                        if kind:
                            link(nc.vector.tensor_reduce(nm, bank(key)[:, 0:nk], AX_X, ALU.max, negate=True))
                            link(ts(nm, nm, NSINK[:, l, h:h + 1], None, ALU.min), neg_max, u + 1)
                        else:
                            link(nc.vector.tensor_reduce(nm, bank(key)[:, 0:nk], AX_X, ALU.max, negate=True),
                                        neg_max, u + 1)
                    elif s[0] == "PT":
                        _, kind, t, h = s
                        u = units[(l, kind, t, h)]
                        nk = len(keys_of(t)) * P
                        key = (l, *s)
                        wait_full(dve, key)
                        read(nc.vector.tensor_copy(PTB[:, u % 3, 0:nk], bank(key)[:, 0:nk]), key)
                    elif s[0] == "O" and s[3] == HEADS - 1:
                        _, kind, t, _h = s
                        g = groups[(l, kind, t)]
                        key = (l, "O", kind, t)
                        wait_full(dve, key)
                        tot = AT[:, g % 2, 1, :]
                        if kind:
                            link(tt(AT[:, g % 2, 3, :], tot, AT[:, g % 2, 2, :], ALU.add))
                            tot = AT[:, g % 2, 3, :]
                        link(nc.vector.reciprocal(AT[:, g % 2, 4, :], tot))
                        if g >= 2:
                            prev = [k for k, v in groups.items() if v == g - 2][0]
                            wait_full(dve, (prev[0], "YAT", *prev[1:]))
                        b, n = fill_at[key]
                        read(tt(YA[:, g % 2, :].rearrange("p (h d) -> p h d", d=HD),
                                bank(key)[:, :].rearrange("p (h d) -> p h d", d=HD),
                                AT[:, g % 2, 4, :].unsqueeze(2).to_broadcast([P, HEADS, HD]), ALU.mult), key)
                for s in range(T // 2):
                    for p in range(2):
                        kr, ki = (l, "DFT", s, 0, p), (l, "DFT", s, 1, p)
                        wait_full(dve, kr)
                        wait_full(dve, ki)
                        vr, vi = bank(kr)[:, :], bank(ki)[:, :]
                        Kr, Ki = KS[:, p, :], KS[:, 3 + p, :]
                        KrN = KS[:, 2, :] if p == 0 else Kr
                        link(tt(TMP[:, 0, :], vr, Kr, ALU.mult))
                        link(tt(TMP[:, 1, :], vi, Ki, ALU.mult))
                        read(tt(TMP[:, 2, :], vr, Ki, ALU.mult), kr)
                        read(tt(TMP[:, 3, :], vi, KrN, ALU.mult), ki)
                        link(tt(YS[:, s, p, :], TMP[:, 0, :], TMP[:, 1, :], ALU.subtract))
                        link(tt(YS[:, s, 2 + p, :], TMP[:, 2, :], TMP[:, 3, :], ALU.add),
                                    spec_ready, 2 * seqs[(l, s)] + p + 1)
                for s in range(T // 2):
                    for ch in range(CH):
                        key = (l, "INV", s, ch)
                        wait_full(dve, key)
                        cols = slice(SEQ * s, SEQ * s + SEQ)
                        read(stt(TMP[:, ch % 2, 0:SEQ], UC[:, 8 + ch, cols], PC[:, 112 + ch:113 + ch],
                                 bank(key)[:, 0:SEQ], ALU.mult, ALU.add), key)
                        link(tt(UC[:, ch, cols], UC[:, ch, cols], TMP[:, ch % 2, 0:SEQ], ALU.mult),
                                    yh_ready, CH * seqs[(l, s)] + ch + 1)
                for j, b in enumerate((1, 0, 2)):
                    for ch in range(KD):
                        gate, br = (l, "GATE", b, ch), (l, "BR", b, ch)
                        wait_full(dve, br)
                        wait_read(dve, gate)
                        if j == 0:
                            read(tt(MT[:, ch, 0:N], TMP[:, ch % 2, 0:N], bank(br)[:, 0:N], ALU.mult), br)
                        else:
                            read(tt(TMP[:, 2 + ch % 2, 0:N], TMP[:, ch % 2, 0:N], bank(br)[:, 0:N], ALU.mult), br)
                            ins = tt(MT[:, ch, 0:N], MT[:, ch, 0:N], TMP[:, 2 + ch % 2, 0:N], ALU.add)
                            if j == 2:
                                link(ins, merged, KD * l + ch + 1)
                            else:
                                link(ins)
                for half in range(2):
                    cols = slice(512 * half, 512 * half + 512)
                    for t in range(T):
                        key = (l, "OUT", half, t)
                        wait_full(dve, key)
                        if half == 0 and t == 0:
                            wait_read(dve, (l, "GB", 0, T // 2 - 1, 1))
                        read(tt(TMP[:, 2 + t % 2, :], bank(key)[:, :], GB[:, t // 2, cols], ALU.mult), key)
                        link(tt(X[:, t, cols], X[:, t, cols], TMP[:, 2 + t % 2, :], ALU.add),
                                    residual_added, residual_no(l, half, t) + 1)
                normalise_rows(l, 1)
                modulate(l, 1)
                for t in range(T):
                    key = (l, "LG", t)
                    wait_full(dve, key)
                    link(tt(RT[:, 2, t, 0:4], bank(key)[:, 0:4], RB[:, l, 0:4], ALU.add))
                    read(tt(RT[:, 3, t, :], bank(key)[:, 4:20], RB[:, l, 4:20], ALU.add), key)

                gl, le = RT[:, 2, 0:T, 0:4], RT[:, 3, 0:T, :]
                mx = RT[:, 4, 0:T, 0:1]
                fg = FIRST[:, 0:4].unsqueeze(1).to_broadcast([P, T, 4])
                fe = FIRST[:, 4:20].unsqueeze(1).to_broadcast([P, T, NEXP])

                def red(dst, src):
                    link(nc.vector.tensor_reduce(dst, src, AX_X, ALU.max))

                def op(dst, a, b, alu):
                    link(tt(dst, a, b, alu))

                def first_of_max(dst, src, best, weights, n):
                    op(dst, src, best.to_broadcast([P, T, n]), ALU.is_equal)
                    op(dst, dst, weights, ALU.mult)
                    red(RT[:, 11, 0:T, 0:1], dst)
                    op(dst, dst, RT[:, 11, 0:T, 0:1].to_broadcast([P, T, n]), ALU.is_equal)

                red(mx, gl)
                op(RT[:, 0, 0:T, 0:4], gl, mx.to_broadcast([P, T, 4]), ALU.subtract)
                og = RT[:, 5, 0:T, 0:4]
                first_of_max(og, gl, mx, fg, 4)
                for e4 in range(4):
                    link(nc.vector.tensor_copy(RT[:, 6, 0:T, e4:NEXP:4], og))
                op(le, le, RT[:, 6, 0:T, :], ALU.mult)
                link(ts(RT[:, 6, 0:T, :], RT[:, 6, 0:T, :], BIG, -BIG, ALU.mult, ALU.add))
                op(le, le, RT[:, 6, 0:T, :], ALU.add)
                m1, m2 = RT[:, 4, 0:T, 1:2], RT[:, 4, 0:T, 2:3]
                e1, e2 = RT[:, 7, 0:T, :], RT[:, 8, 0:T, :]
                red(m1, le)
                first_of_max(e1, le, m1, fe, NEXP)
                link(ts(RT[:, 6, 0:T, :], e1, -3 * BIG, None, ALU.mult))
                op(le, le, RT[:, 6, 0:T, :], ALU.add)
                red(m2, le)
                first_of_max(e2, le, m2, fe, NEXP)
                link(tt(RT[:, 0, 0:T, 4:5], m2, m1, ALU.subtract), logits_ready, l + 1)
                dve.wait_ge(logits_exp, l + 1)
                sg_, r2, r1 = RT[:, 4, 0:T, 3:4], RT[:, 4, 0:T, 4:5], RT[:, 4, 0:T, 5:6]
                link(nc.vector.tensor_reduce(sg_, RT[:, 1, 0:T, 0:4], AX_X, ALU.add))
                link(ts(r1, RT[:, 1, 0:T, 4:5], 1.0, None, ALU.add))
                op(r1, r1, sg_, ALU.mult)
                link(nc.vector.reciprocal(r1, r1))
                op(r2, r1, RT[:, 1, 0:T, 4:5], ALU.mult)
                op(e1, e1, r1.to_broadcast([P, T, NEXP]), ALU.mult)
                op(e2, e2, r2.to_broadcast([P, T, NEXP]), ALU.mult)
                link(tt(CMB[:, 0:T, :], e1, e2, ALU.add))
                link(nc.vector.memset(FACC[:, 0:T, :], 0.0))
                base = steps[0]
                with dve.Fori(0, NEXP) as e:
                    for i in range(FE):
                        key = (l, "H3", i)
                        wait_full(dve, key, e * (FE // 2))
                        wait_read(dve, (l, "H1", i), e * (FE // 2))
                        b, n = fill_at[key]
                        tt(GH[:, i, 0:N], TMP[:, i % 2, 0:N], bank(key)[:, 0:N], ALU.mult).then_inc(bank_free[b], 1)
                    nc.vector.tensor_copy(CE[:, 0:T], CMB[:, 0:T, bass.ds(e, 1)].rearrange("p t a -> p (t a)")) \
                        .then_inc(dve_steps, 1)
                    dve.wait_ge(dve_steps, e + (base + 1))
                    for t in range(T):
                        for half in range(2):
                            key = (l, "Y", t, half)
                            wait_full(dve, key, e * (T // 2))
                            b, n = fill_at[key]
                            cols = slice(512 * half, 512 * half + 512)
                            stt(FACC[:, t, cols], bank(key)[:, :], CE[:, t:t + 1], FACC[:, t, cols],
                                ALU.mult, ALU.add).then_inc(bank_free[b], 1)
                steps[0] = base + NEXP
                wait_read(dve, (l, "Y", T - 1, 1), (NEXP - 1) * (T // 2))
                wait_read(dve, (l, "GB", 1, T // 2 - 1, 1))
                for t in range(T):
                    link(tt(FACC[:, t, :], FACC[:, t, :], GB[:, t // 2, :], ALU.mult))
                    link(tt(X[:, t, :], X[:, t, :], FACC[:, t, :], ALU.add),
                                experts_done, (T0 if l else 0) + t + 1)

        @block.tensor
        def _(pe):
            mm = nc.tensor.matmul

            def product(key, dst, pairs):
                for i, (a, b) in enumerate(pairs):
                    ins = mm(dst, a, b, start=(i == 0), stop=(i == len(pairs) - 1))
                return ins

            def norm_transposes(l, norm):
                T = TT if not norm else tiles_of(l)
                for k in range(KD):
                    key = (l, "N2" if norm else "N1", k)
                    wait_bank(pe, key)
                    for t in range(T):
                        if k == 0:
                            pe.wait_ge(rows_ready, row_no(l, norm, t) + 1)
                        ins = nc.tensor.transpose(bank(key)[:, t * P:(t + 1) * P], XN[:, t, k * P:(k + 1) * P],
                                                  ident[:, :])
                    full(ins, key)

            def gate_rows(l, which):
                for s in range(tiles_of(l) // 2):
                    for half in range(2):
                        key = (l, "GB", which, s, half)
                        wait_bank(pe, key)
                        for q in range(4):
                            m = (40 if which else 16) + 4 * half + q
                            ins = mm(bank(key)[:, q * P:(q + 1) * P], MOD[:, m, s:s + 1].to_broadcast([P, P]),
                                     ident[:, :], start=True, stop=True)
                        full(ins, key)

            def token_rows(key, t):
                wait_bank(pe, key)
                w = slot_kn((key[0], key[1], 0))
                full(product(key, bank(key)[:, :], [(HT[:, k, t * P:(t + 1) * P], w[:, k, :]) for k in range(KD)]), key)

            def query_transposes(l, what, src_what, t):
                key = (l, what, t)
                pe.wait_ge(qk_ready, proj[(l, src_what, t)] + 1)
                wait_bank(pe, key)
                for h in range(4):
                    ins = nc.tensor.transpose(bank(key)[:, h * P:(h + 1) * P], QN[:, t, h * P:(h + 1) * P],
                                              ident[:, :])
                full(ins, key)

            pe.wait_ge(params_loaded, 16 * SMALL)
            pe.wait_ge(ones_ready, 2)
            for l in range(LAYERS):
                T = tiles_of(l)
                N = T * P
                key = (l, "PR")
                wait_bank(pe, key)
                full(nc.tensor.transpose(bank(key)[:, 0:116], PR[:, l, :], ident[0:116, 0:116]), key)
                if l == 0:
                    key = (l, "C")
                    pe.wait_ge(cond_ready, 1)
                    wait_bank(pe, key)
                    full(nc.tensor.transpose(bank(key)[:, 0:16], CR[:, :], ident[0:16, 0:16]), key)
                key = (l, "F1")
                pe.wait_ge(filter_loaded, 48 * (l + 1))
                wait_bank(pe, key)
                full(mm(bank(key)[0:HID, 0:SEQ], FW[0:EMB, l, 0, :], Z, start=True, stop=True), key)
                key = (l, "F2")
                pe.wait_ge(filter_sin, 2 * l + 1)
                wait_bank(pe, key)
                full(mm(bank(key)[0:HID, 0:SEQ], FW[:, l, 1, :], FT[:, 3, :], start=True, stop=True), key)
                pe.wait_ge(filter_sin, 2 * l + 2)
                for t in range(2):
                    for half in range(2):
                        key = (l, "F3", t, half)
                        wait_bank(pe, key)
                        full(mm(bank(key)[:, :], FT[:, 4, t * P:(t + 1) * P], W3[:, 512 * half:512 * half + 512],
                                start=True, stop=True), key)
                key = (l, "FN")
                wait_bank(pe, key)
                pe.wait_ge(filter_abs, 4 * l + 4)
                full(product(key, bank(key)[:, :], [(ones[:, :], DEC[:, t, h, :]) for t in range(2) for h in range(2)]),
                     key)
                pe.wait_ge(filter_ab, 2 * l + 2)
                for m in range(5):
                    key = (l, "FK", m)
                    wait_bank(pe, key)
                    full(product(key, bank(key)[:, :], [(DF[:, t, m * P:(m + 1) * P], FAB[:, t, int(m >= 3), :])
                                                        for t in range(2)]), key)
                key = (l, "MOD")
                wait_read(pe, (0, "C"))
                wait_bank(pe, key)
                cc = CC[:, :].rearrange("p (s k) -> p k s", s=2)
                for j in range(12):
                    lk = (l, "ADA", j)
                    wait_slot(pe, lk)
                    w = slot_kn(lk)
                    for q in range(4):
                        m = 4 * j + q
                        ins = product(key, bank(key)[:, 2 * m:2 * m + 2],
                                      [(w[:, k, q * P:(q + 1) * P], cc[:, k, :]) for k in range(KD)])
                        if q == 3 and j < 11:
                            ins.then_inc(ada_read, 1)
                full(ins, key)
                pe.wait_ge(mod_ready, l + 1)
                norm_transposes(l, 0)
                wait_read(pe, (l, "N1", KD - 1))
                wait_slot(pe, (l, "QA", 0))
                for t in range(T):
                    token_rows((l, "QA", t), t)
                wait_slot(pe, (l, "KV", 0))
                for t in range(TT):
                    token_rows((l, "KV", t), t)
                for t in range(T):
                    query_transposes(l, "QAT", "QA", t)
                wait_slot(pe, (l, "QW", 0))
                for t in range(T):
                    token_rows((l, "QW", t), t)
                for t in range(TT):
                    key = (l, "KVT", t)
                    pe.wait_ge(qk_ready, proj[(l, "KV", t)] + 1)
                    wait_bank(pe, key)
                    for kind in range(2):
                        ins = nc.tensor.transpose(bank(key)[:, kind * P:(kind + 1) * P],
                                                  KN[:, t, kind * P:(kind + 1) * P], ident[:, :])
                    full(ins, key)
                for ch in range(12):
                    key = (l, "U", ch)
                    if ch % 4 == 0:
                        wait_slot(pe, (l, "U", ch // 4))
                    w = slot_kn((l, "U", ch // 4))
                    wait_bank(pe, key)
                    q = ch % 4
                    full(product(key, bank(key)[:, 0:N], [(w[:, k, q * P:(q + 1) * P], HT[:, k, 0:N])
                                                          for k in range(KD)]), key)
                for t in range(T):
                    query_transposes(l, "QWT", "QW", t)
                wait_read(pe, (l, "QWT", T - 1))
                for s in attention_steps(l):
                    if s[0] == "S":
                        _, kind, t, h = s
                        key = (l, *s)
                        g, r = h // 4, h % 4
                        rows = slice(HD * g, HD * g + HD)
                        k0, nk = keys_of(t)[0], len(keys_of(t))
                        wait_bank(pe, key)
                        full(mm(bank(key)[:, 0:nk * P], QT[rows, kind, r, t * P:(t + 1) * P],
                                KT[rows, kind, k0 * P:(k0 + nk) * P], start=True, stop=True), key)
                    elif s[0] == "PT":
                        _, kind, t, h = s
                        key = (l, *s)
                        u = units[(l, kind, t, h)]
                        wait_read(pe, (l, "S", kind, t, h))
                        wait_bank(pe, key)
                        for j in range(len(keys_of(t))):
                            ins = nc.tensor.transpose(bank(key)[:, j * P:(j + 1) * P],
                                                      PB[:, u % 3, j * P:(j + 1) * P], ident[:, :])
                        full(ins, key)
                    elif s[0] == "O":
                        _, kind, t, h = s
                        key = (l, "O", kind, t)
                        u = units[(l, kind, t, h)]
                        if h == 0:
                            wait_bank(pe, key)
                        wait_read(pe, (l, "PT", kind, t, h))
                        g = h // 4
                        ins = product(key, bank(key)[:, h * HD:(h + 1) * HD],
                                      [(PTB[:, u % 3, j * P:(j + 1) * P], V[:, kt, kind, g * HD:(g + 1) * HD])
                                       for j, kt in enumerate(keys_of(t))])
                        if h == HEADS - 1:
                            full(ins, key)
                    else:
                        _, kind, t = s
                        key = (l, *s)
                        gi = groups[(l, kind, t)]
                        wait_read(pe, (l, "O", kind, t))
                        wait_bank(pe, key)
                        for q in range(4):
                            ins = nc.tensor.transpose(bank(key)[:, q * P:(q + 1) * P], YA[:, gi % 2, q * P:(q + 1) * P],
                                                      ident[:, :])
                        full(ins, key)
                pe.wait_ge(gated_v, l + 1)
                for t in range(T):
                    key = (l, "VT", t)
                    wait_bank(pe, key)
                    for q in range(CH):
                        ins = nc.tensor.transpose(bank(key)[:, q * P:(q + 1) * P], UC[:, 8 + q, t * P:(t + 1) * P],
                                                  ident[:, :])
                    full(ins, key)
                for s in range(T // 2):
                    wait_read(pe, (l, "VT", 2 * s))
                    wait_read(pe, (l, "VT", 2 * s + 1))
                    for p in range(2):
                        for r in range(2):
                            key = (l, "DFT", s, r, p)
                            col = (0, 1)[p] if r == 0 else (5, 4)[p]
                            wait_bank(pe, key)
                            full(product(key, bank(key)[:, :], [(DF[:, t, col * P:(col + 1) * P], VT[:, 2 * s + t, :])
                                                                for t in range(2)]), key)
                for s in range(T // 2):
                    pe.wait_ge(spec_ready, 2 * seqs[(l, s)] + 2)
                    for ch in range(CH):
                        key = (l, "INV", s, ch)
                        wait_bank(pe, key)
                        full(product(key, bank(key)[:, 0:SEQ], [(YS[:, s, f, ch * P:(ch + 1) * P], IF[:, f, :])
                                                                for f in range(4)]), key)
                gate_rows(l, 0)
                for b in (1, 0, 2):
                    wait_slot(pe, (l, "BR", b))
                    wb = slot((l, "BR", b)).rearrange("p (k n) -> p k n", k=CH)
                    if b == 1:
                        pe.wait_ge(yh_ready, CH * seqs[(l, T // 2 - 1)] + CH)
                    else:
                        wait_read(pe, (l, "YAT", 1, T - 1))
                    for ch in range(KD):
                        if ch % 4 == 0:
                            wait_slot(pe, (l, "GATE", b, ch // 4))
                        wg = slot_kn((l, "GATE", b, ch // 4))
                        key = (l, "GATE", b, ch)
                        q = ch % 4
                        wait_bank(pe, key)
                        full(product(key, bank(key)[:, 0:N], [(wg[:, k, q * P:(q + 1) * P], HT[:, k, 0:N])
                                                              for k in range(KD)]), key)
                        key = (l, "BR", b, ch)
                        wait_bank(pe, key)
                        y = [UC[:, k, 0:N] if b == 1 else YT[:, b // 2, k, 0:N] for k in range(CH)]
                        full(product(key, bank(key)[:, 0:N], [(wb[:, k, ch * P:(ch + 1) * P], y[k])
                                                              for k in range(CH)]), key)
                pe.wait_ge(merged, KD * l + KD)
                for half in range(2):
                    wait_slot(pe, (l, "OUT", half))
                    w = slot_kn((l, "OUT", half))
                    for t in range(T):
                        key = (l, "OUT", half, t)
                        wait_bank(pe, key)
                        full(product(key, bank(key)[:, :], [(MT[:, k, t * P:(t + 1) * P], w[:, k, :])
                                                            for k in range(KD)]), key)
                norm_transposes(l, 1)
                wait_read(pe, (l, "N2", KD - 1))
                for t in range(T):
                    key = (l, "LG", t)
                    wait_bank(pe, key)
                    full(product(key, bank(key)[:, 0:20], [(HT[:, k, t * P:(t + 1) * P], RW[:, l, k, :])
                                                           for k in range(KD)]), key)
                gate_rows(l, 1)
                with pe.Fori(0, NEXP) as e:
                    wait_slot(pe, (l, "W1", 0), e * 16)
                    wait_slot(pe, (l, "W3", 0), e * 16)
                    w1 = slot_kn((l, "W1", 0))
                    w3 = slot_kn((l, "W3", 0))
                    for i in range(FE):
                        for what, w in (("H1", w1), ("H3", w3)):
                            key = (l, what, i)
                            b, n = fill_at[key]
                            pe.wait_ge(bank_free[b], e * (FE // 2) + n)
                            full(product(key, bank(key)[:, 0:N], [(w[:, k, i * P:(i + 1) * P], HT[:, k, 0:N])
                                                                  for k in range(KD)]), key)
                    wait_slot(pe, (l, "W2", 0), e * 16)
                    w2 = slot((l, "W2", 0)).rearrange("p (k n) -> p k n", k=FE)
                    for i in (FE - 2, FE - 1):
                        wait_read(pe, (l, "H3", i), e * (FE // 2))
                    for t in range(T):
                        for half in range(2):
                            key = (l, "Y", t, half)
                            b, n = fill_at[key]
                            pe.wait_ge(bank_free[b], e * (T // 2) + n)
                            full(product(key, bank(key)[:, :],
                                         [(GH[:, k, t * P:(t + 1) * P], w2[:, k, 512 * half:512 * half + 512])
                                          for k in range(FE)]), key)


SMALL = 3 + 17 * LAYERS + 5


def constants():
    n = SEQ
    t = np.arange(n)
    f = np.arange(n)
    ang = 2 * np.pi * np.outer(t, f) / (2 * n)
    cos, sin = np.cos(ang), -np.sin(ang)
    alt = (-1.0) ** t
    cosn, sinn = cos[:, 0:P].copy(), sin[:, 0:P].copy()
    cosn[:, 0] = alt
    sinn[:, 0] = alt
    dft = np.concatenate([cos, cosn, sin, sinn], axis=1)
    icos = 2 * np.cos(ang).T / (2 * n)
    icos[0] /= 2
    isin = -2 * np.sin(ang).T / (2 * n)
    isin[0] = alt / (2 * n)
    idft = np.concatenate([icos, isin], axis=0)
    pos = (np.arange(n) / (n - 1)).astype(np.float32)
    deltas = np.abs(np.linspace(np.log(1e-2) / 1.5, np.log(1e-2) / 0.3, HW)).astype(np.float32)
    dec = np.exp(-pos[:, None] * deltas[None]).astype(np.float32)
    dec2 = np.stack([dec, dec], axis=1)
    dec2[0, 1] = 0.0
    bands = np.linspace(1e-4, 15, 16).astype(np.float32)
    za = (2 * np.pi * bands.astype(np.float64)[None] * np.arange(n)[:, None] / n)
    z = np.concatenate([pos[:, None], np.cos(za), -np.sin(za)], axis=1).T
    inv = 10000.0 ** (-np.arange(16) / 16.0)
    row, col = np.arange(n) // 64, np.arange(n) % 64
    a = np.stack([row[:, None] * inv, col[:, None] * inv], axis=1)
    c = np.stack([np.cos(a), np.cos(a)], axis=2).reshape(n, HD)
    s = np.stack([-np.sin(a), np.sin(a)], axis=2).reshape(n, HD)
    rope = np.stack([c, s], axis=1)
    mask = np.where(np.abs(np.arange(n)[None] - np.arange(n)[:, None]) <= 128, 0.0, -BIG)
    first = np.concatenate([np.arange(4, 0, -1), np.arange(16, 0, -1)])
    out = {"k_ident": np.eye(P), "k_dft": dft, "k_idft": idft, "k_decay": dec2, "k_z": z, "k_rope": rope,
           "k_mask": mask, "k_first": first}
    return {k: np.ascontiguousarray(v, dtype=np.float32) for k, v in out.items()}


_INS = ["x", "c", "ctx", "c_ctx", "ada_w", "ada_b", "norm1_g", "norm2_g", "w_in", "qk_g", "hy_short_w", "hy_short_b",
        "hy_f_w1", "hy_f_b1", "hy_f_freq", "hy_f_w2", "hy_f_b2", "hy_f_w3", "hy_bias", "sinks", "w_branch", "w_out",
        "router_g_w", "router_g_b", "router_e_w", "router_e_b", "exp_w1", "exp_w3", "exp_w2"]


def kernel(**inputs):
    import concourse.bacc as _bacc
    from concourse.bass_utils import run_bass_kernel_spmd as _run

    nc = _bacc.Bacc("TRN2", target_bir_lowering=False, num_devices=1)
    arrays, args = {}, []
    data = {k: np.ascontiguousarray(inputs[k]) for k in _INS}
    data.update(constants())
    for name, a in data.items():
        arrays[f"in_{name}"] = a
        args.append(nc.dram_tensor(f"in_{name}", a.shape, mybir.dt.from_np(a.dtype), kind="ExternalInput").ap())
    args.append(nc.dram_tensor("out_0", (1, SEQ, D), F32, kind="ExternalOutput").ap())
    build(nc, *args)
    r = _run(nc, [arrays], core_ids=[0])
    return r.results[0]["out_0"]
```

```python
from contextlib import ExitStack

import numpy as np

import concourse.bass as bass
from concourse import mybir

F32 = mybir.dt.float32
F32R = mybir.dt.float32r
BF16 = mybir.dt.bfloat16
ALU = mybir.AluOpType
ACT = mybir.ActivationFunctionType
AX_X = mybir.AxisListType.X

P = 128
D = 1024
KD = D // P
SEQ = 256
LAYERS = 2
HD = 64
HEADS = 8
HW = 512
CH = HW // P
NEXP = 16
NGRP = 4
DE = 512
FE = DE // P
HID = 64
EMB = 33
SLOTS = 3
SLOT = KD * 512
TT = 4
EPS = 1e-6
BIG = 1e30
MAGIC = 12582912.0
TWO_PI = (6.28125, 0.0019350051879882812, 3.0199159819e-07)
PI_MAX = 3.1415925


def chained(engine, own, count):
    def link(ins, sem=None, value=None):
        if sem is None:
            count[0] += 1
            sem, value = own, count[0]
        ins.then_inc(sem, 1)
        engine.wait_ge(sem, value)
    return link


def tiles_of(l):
    return TT if l < LAYERS - 1 else 2


def attention_units(l):
    return [(kind, t, h) for kind in range(2) for t in range(tiles_of(l)) for h in range(HEADS)]


def keys_of(t):
    return (0, 1, 2, 3) if t < 2 else (2, 3)


LAG_PT, LAG_O = 2, 3


def attention_steps(l):
    units = attention_units(l)
    steps = []
    for i in range(len(units) + LAG_O + 2):
        if i < len(units):
            steps.append(("S", *units[i]))
        if 0 <= i - LAG_O < len(units):
            steps.append(("O", *units[i - LAG_O]))
        if 0 <= i - LAG_PT < len(units):
            steps.append(("PT", *units[i - LAG_PT]))
        j = i - LAG_O - 2
        if 0 <= j < len(units) and units[j][2] == HEADS - 1:
            steps.append(("YAT", *units[j][:2]))
    return steps


R3_COLS = 9216
PARTS_COLS = 2 * D + TT * P
ALLB = tuple(range(8))
CAP = (112, 96)
FILTER_BANKS = tuple(range(6))
MOD_BANKS = (6, 7)
FILTER_SLOTS = (3, 5, 7, 9, 11)
WIDE = 96
SC_BANKS = (7, 5, 6)
OVER_AT = {(what, i): (2 * w + i % 2, i // 2) for w, what in enumerate(("H1", "H3")) for i in range(FE)}


def plan_fills():
    at, count, turn, per = {}, [0] * 8, {}, {}

    def add(key, banks):
        t = turn.get(banks, 0)
        turn[banks] = t + 1
        b = banks[t % len(banks)]
        at[key] = (b, count[b])
        count[b] += 1

    for l in range(LAYERS):
        T = tiles_of(l)
        add((l, "PR"), ALLB)
        if l == 0:
            add((l, "C"), ALLB)
        for j in range(12):
            add((l, "MOD", j), MOD_BANKS)
        for k in ("F1", "F2"):
            add((l, k), FILTER_BANKS)
        for t in range(2):
            for half in range(2):
                add((l, "F3", t, half), FILTER_BANKS)
        add((l, "FN"), FILTER_BANKS)
        for m in range(5):
            add((l, "FK", m), FILTER_BANKS)
        for k in range(KD):
            add((l, "N1", k), ALLB)
        for t in range(T):
            add((l, "QA", t), ALLB)
        for t in range(TT):
            add((l, "KV", t), ALLB)
        for t in range(T):
            add((l, "QAT", t), ALLB)
        for t in range(T):
            add((l, "QW", t), ALLB)
        for t in range(TT):
            add((l, "KVT", t), ALLB)
        for c in range(12):
            add((l, "U", c), ALLB)
        for t in range(T):
            add((l, "QWT", t), ALLB)
        for step in attention_steps(l):
            if step[0] == "S":
                add((l, *step), (0, 1, 2))
            elif step[0] == "PT" or step[0] == "YAT":
                add((l, *step), (3, 4, 5))
            elif step[3] % 4 == 0:
                add((l, "O", step[1], step[2], step[3] // 4), (6, 7))
        for t in range(T):
            add((l, "VT", t), (0, 1, 2, 3))
        for s in range(T // 2):
            for p in range(2):
                for r in range(2):
                    add((l, "DFT", s, r, p), ALLB)
        for s in range(T // 2):
            for c in range(CH):
                add((l, "INV", s, c), ALLB)
        for s in range(T // 2):
            for half in range(2):
                add((l, "GB", 0, s, half), ALLB)
        for b in (1, 0, 2):
            for c in range(KD):
                add((l, "GATE", b, c), ALLB)
                add((l, "BR", b, c), ALLB)
        for t in range(T):
            for half in range(2):
                add((l, "OUT", half, t), ALLB)
        for k in range(KD):
            add((l, "N2", k), ALLB)
        for t in range(T):
            add((l, "LG", t), ALLB)
        for s in range(T // 2):
            for half in range(2):
                add((l, "GB", 1, s, half), ALLB)
        for t in range(T):
            for half in range(2):
                add((l, "TK", t, half), ALLB)
        add((l, "RANK"), ALLB)
        scatters = [(t, half) for t in range(T) for half in range(2)]
        for half in range(2):
            add((l, "GA0", half), (3 + half,))
        before = list(count)
        add((l, "ST"), (2,))
        add((l, "H1"), (0,))
        add((l, "H3"), (1,))
        for i, (t, half) in enumerate(scatters):
            add((l, "SC", t, half), SC_BANKS[i % 3:i % 3 + 1])
        for half in range(2):
            add((l, "GA", half), (3 + half,))
        for half in range(2):
            add((l, "Y", half), (5 + half,))
        for b in range(8):
            per[(l, b)] = count[b] - before[b]
            count[b] += (NEXP - 1) * per[(l, b)]
        for i, (t, half) in enumerate(scatters):
            add((l, "SCL", t, half), SC_BANKS[i % 3:i % 3 + 1])
    return at, per


def weight_loads():
    out = []
    for l in range(LAYERS):
        for j in range(12):
            out.append(((l, "ADA", j), (l, "MOD", j)))
        for what in ("QA", "KV", "QW"):
            out.append(((l, what, 0), (l, what, (TT if what == "KV" else tiles_of(l)) - 1)))
        for j in range(3):
            out.append(((l, "U", j), (l, "U", 4 * j + 3)))
        for b in (1, 0, 2):
            out.append(((l, "GATE", b, 0), (l, "GATE", b, 3)))
            out.append(((l, "BR", b), (l, "BR", b, KD - 1)))
            out.append(((l, "GATE", b, 1), (l, "GATE", b, 7)))
        for half in range(2):
            out.append(((l, "OUT", half), (l, "OUT", half, tiles_of(l) - 1)))
        for e in range(NEXP):
            for what in ("W1", "W3", "W2"):
                out.append(((l, what, e), None))
    return out


def build(nc, x, c, ctx_in, c_ctx, ada_w, ada_b, norm1_g, norm2_g, w_in, qk_g, hy_short_w, hy_short_b, hy_f_w1,
          hy_f_b1, hy_f_freq, hy_f_w2, hy_f_b2, hy_f_w3, hy_bias, sinks, w_branch, w_out, router_g_w, router_g_b,
          router_e_w, router_e_b, exp_w1, exp_w3, exp_w2, k_ident, k_dft, k_idft, k_decay, k_z, k_rope, k_mask,
          k_first, k_tri, k_iota, out):
    fill_at, fills_per_expert = plan_fills()
    loads = weight_loads()
    load_no = {key: n for n, (key, _) in enumerate(loads)}
    loaded_at, total = [], [0] * SLOTS
    for n, (key, _) in enumerate(loads):
        total[n % SLOTS] += 32 if key[1] == "KV" else 16
        loaded_at.append(total[n % SLOTS])

    with ExitStack() as stack:
        def sb(name, shape):
            return stack.enter_context(nc.sbuf_tensor(name, shape, F32))

        def sem(name):
            return stack.enter_context(nc.semaphore(name))

        ps = [stack.enter_context(nc.psum_tensor(f"bank{b}", [P, 512], F32)) for b in range(8)]

        X = sb("X", [P, TT, D])
        HT = sb("HT", [P, KD, TT * P])
        ring = sb("ring", [P, SLOTS, SLOT])
        R1 = sb("R1", [P, 12 * 512])
        R2 = sb("R2", [P, TT * D])
        with nc.sbuf_tensor("R3", [P, R3_COLS], F32) as R3:
            pass
        parts_r = stack.enter_context(nc.sbuf_tensor("parts_r", [P, PARTS_COLS], F32R))
        sb("R3_rest", [P, R3_COLS - PARTS_COLS])
        KSG = sb("KSG", [P, 5 * HW])
        YA = sb("YA", [P, 2, 512])
        TMP = sb("TMP", [P, 4, 512])
        ident = sb("ident", [P, P])
        ones = sb("ones", [P, P])
        ident_b = stack.enter_context(nc.sbuf_tensor("ident_b", [P, P], BF16))
        DF = sb("DF", [P, 2, 6 * P])
        IF = sb("IF", [P, 4, SEQ])
        ROPE = sb("ROPE", [P, 2, 2, HD])
        CG = sb("CG", [P, 3, 4, HD])
        SG = sb("SG", [P, 2, 4, HD])
        MASK = sb("MASK", [P, 2, SEQ])
        QKG = sb("QKG", [P, LAYERS, 4, HD])
        SINK = sb("SINK", [P, LAYERS, HEADS])
        NSINK = sb("NSINK", [P, LAYERS, HEADS])
        PR = sb("PR", [116, LAYERS, P])
        PC = sb("PC", [P, 116])
        CR = sb("CR", [16, P])
        CC = sb("CC", [P, 16])
        FP = sb("FP", [HID, LAYERS, 3])
        FW = sb("FW", [HID, LAYERS, 2, HID])
        MOD = sb("MOD", [P, 48, 2])
        AM = sb("AM", [P, 2, KD, 2])
        RW = sb("RW", [P, LAYERS, KD, 20])
        RB = sb("RB", [P, LAYERS, 20])
        FIRST = sb("FIRST", [P, 20])
        ST = sb("ST", [P, 64])
        HS = sb("HS", [P, 2, 4, HEADS])
        AT = sb("AT", [P, 2, 5, HEADS])
        NMX = sb("NMX", [P, 4])
        CMB = sb("CMB", [P, TT, NEXP])
        CE = sb("CE", [P, TT])
        TRI = sb("TRI", [P, P])
        IOTA = sb("IOTA", [P, P])
        POS = sb("POS", [P, TT, NEXP + 1])
        CMBX = sb("CMBX", [P, TT, NEXP + 1])
        PCOL = sb("PCOL", [P, TT])
        FLAG = stack.enter_context(nc.sbuf_tensor("FLAG", [P, 1], mybir.dt.int32))
        HALF = sb("HALF", [P, 16])

        KS = KSG[:, :].rearrange("p (m n) -> p m n", m=5)
        GB = KSG[:, 0:2 * D].rearrange("p (s d) -> p s d", s=2)
        UC = R1[:, :].rearrange("p (c n) -> p c n", c=12)
        MT = R1[:, 2048:6144].rearrange("p (k n) -> p k n", k=KD)
        GH = R1[:, 0:2048].rearrange("p (f n) -> p f n", f=FE)
        GM = [R1[:, 2048:2048 + 4 * c] for c in CAP]
        XN = R2[:, :].rearrange("p (t d) -> p t d", t=TT)
        YT = R2[:, :].rearrange("p (a c n) -> p a c n", a=2, c=CH)
        FACC = R2[:, :].rearrange("p (t d) -> p t d", t=TT)
        DEC = R3[:, 0:2048].rearrange("p (t h n) -> p t h n", t=2, h=2)
        W3 = R3[0:HID, 2048:3072]
        FH = R3[:, 3072:5120].rearrange("p (t h n) -> p t h n", t=2, h=2)
        FAB = R3[:, 5120:7168].rearrange("p (t h n) -> p t h n", t=2, h=2)
        FN = R3[:, 7168:7680]
        Z = R3[0:EMB, 7680:7936]
        FT = R3[0:HID, 7936:9216].rearrange("p (a n) -> p a n", a=5)
        QT = R3[:, 0:4096].rearrange("p (a c n) -> p a c n", a=2, c=4)
        KN = YA[:, :, :].rearrange("p a (b n) -> p (a b) n", b=2)
        KT = R3[:, 4096:5120].rearrange("p (a n) -> p a n", a=2)
        V = R3[:, 5120:6144].rearrange("p (t a n) -> p t a n", t=TT, a=2)
        QN = R3[:, 6144:8192].rearrange("p (t n) -> p t n", t=4)
        PB = R3[:, 6144:7680].rearrange("p (t n) -> p t n", t=3)
        PTB = R3[:, 7680:9216].rearrange("p (t n) -> p t n", t=3)
        RT = R3[:, 8448:9216].rearrange("p (a t n) -> p a t n", a=12, t=TT)
        S = R3[:, 2560:2816].bitcast(BF16).rearrange("p (t n) -> p t n", t=TT)
        XG = R3[:, 2816:3840].rearrange("p (k n) -> p k n", k=KD)
        YP = [parts_r[:, p * D:(p + 1) * D] for p in range(2)]
        STB = parts_r[:, 2 * D:2 * D + TT * P]
        TOK = [a.bitcast(BF16).rearrange("p (t d) -> p t d", t=TT)
               for a in (R3[:, 3840:5888], R3[:, 5888:7936], R1[:, 0:2048])]
        TOKR = R1[:, 2048:6144].rearrange("p (t d) -> p t d", t=TT)
        VT = R3[:, 0:2048].rearrange("p (t n) -> p t n", t=TT)
        YS = R3[:, 2048:6144].rearrange("p (s f n) -> p s f n", s=2, f=4)

        bank_full = [sem(f"bank_full{b}") for b in range(8)]
        bank_free = [sem(f"bank_free{b}") for b in range(8)]
        slot_loaded = [sem(f"slot_loaded{s}") for s in range(SLOTS)]
        consts_loaded = sem("consts_loaded")
        early_loaded = sem("early_loaded")
        params_loaded = sem("params_loaded")
        x_loaded = sem("x_loaded")
        filter_loaded = sem("filter_loaded")
        out_stored = sem("out_stored")
        dve_steps = sem("dve_steps")
        act_steps = sem("act_steps")
        pool_steps = sem("pool_steps")
        cond_ready = sem("cond_ready")
        ones_ready = sem("ones_ready")
        filter_arg = sem("filter_arg")
        filter_sin = sem("filter_sin")
        qk_ready = sem("qk_ready")
        merged = sem("merged")
        filter_abs = sem("filter_abs")
        filter_ab = sem("filter_ab")
        mod_ready = sem("mod_ready")
        squares = sem("squares")
        rstd_ready = sem("rstd_ready")
        rows_ready = sem("rows_ready")
        head_squares = sem("head_squares")
        head_sums = sem("head_sums")
        head_rstd = sem("head_rstd")
        conv_started = sem("conv_started")
        gated_v = sem("gated_v")
        neg_max = sem("neg_max")
        ya_ready = sem("ya_ready")
        spec_ready = sem("spec_ready")
        yh_ready = sem("yh_ready")
        residual_added = sem("residual_added")
        logits_ready = sem("logits_ready")
        logits_exp = sem("logits_exp")
        sel_ready = sem("sel_ready")
        places_ready = sem("places_ready")
        tok_high = sem("tok_high")
        tok_mid = sem("tok_mid")
        tok_low = sem("tok_low")
        y_rounded = sem("y_rounded")
        flag_ready = sem("flag_ready")
        over_full = [[sem(f"over_full{l}_{b}") for b in range(8)] for l in range(LAYERS)]
        over_free = [[sem(f"over_free{l}_{b}") for b in range(8)] for l in range(LAYERS)]
        over_steps = [sem(f"over_steps{l}") for l in range(LAYERS)]
        over_loaded = [[sem(f"over_loaded{l}_{s}") for s in range(3)] for l in range(LAYERS)]
        experts_done = sem("experts_done")

        def bank(key):
            return ps[fill_at[key][0]]

        def wait_bank(eng, key, more=0):
            b, n = fill_at[key]
            if n:
                eng.wait_ge(bank_free[b], more + n)

        def wait_full(eng, key, more=0):
            b, n = fill_at[key]
            eng.wait_ge(bank_full[b], more + n + 1)

        def wait_read(eng, key, more=0):
            b, n = fill_at[key]
            eng.wait_ge(bank_free[b], more + n + 1)

        def turn(key, e, n):
            return e * fills_per_expert[(key[0], fill_at[key][0])] + n

        def wait_bank_e(eng, key, e):
            b, n = fill_at[key]
            eng.wait_ge(bank_free[b], turn(key, e, n))

        def wait_full_e(eng, key, e, back=0):
            b, n = fill_at[key]
            eng.wait_ge(bank_full[b], turn(key, e, n + 1 - back * fills_per_expert[(key[0], b)]))

        def wait_read_e(eng, key, e, back=0):
            b, n = fill_at[key]
            eng.wait_ge(bank_free[b], turn(key, e, n + 1 - back * fills_per_expert[(key[0], b)]))

        def over_bank(key, T):
            if key[0] == "Y":
                j = 2 * key[1] + key[2]
                return 4 + j % 4, j // 4, T // 2
            return (*OVER_AT[key], 2)

        def full(ins, key):
            ins.then_inc(bank_full[fill_at[key][0]], 1)

        def slot_of(key):
            return load_no[key] % SLOTS

        def wait_slot(eng, key, more=0):
            n = load_no[key]
            eng.wait_ge(slot_loaded[n % SLOTS], more + loaded_at[n])

        def slot(key):
            return ring[:, slot_of(key), :]

        def slot_kn(key):
            return slot(key).rearrange("p (k n) -> p k n", k=KD)

        T0 = tiles_of(0)
        rows_before = [0, 2 * T0 + (TT - T0)]
        proj = {}
        for l in range(LAYERS):
            for what in ("QA", "KV", "QW"):
                for t in range(TT if what == "KV" else tiles_of(l)):
                    proj[(l, what, t)] = len(proj)
        units = {}
        for l in range(LAYERS):
            for u in attention_units(l):
                units[(l, *u)] = len(units)
        groups = {}
        for l in range(LAYERS):
            for kind in range(2):
                for t in range(tiles_of(l)):
                    groups[(l, kind, t)] = len(groups)
        seqs = {}
        for l in range(LAYERS):
            for s in range(tiles_of(l) // 2):
                seqs[(l, s)] = len(seqs)

        def row_no(l, norm, t):
            return (0 if l == 0 else TT + T0) + (TT if norm else 0) + t

        def tok_no(l, t, half):
            return (0 if l == 0 else 2 * T0) + 2 * t + half

        def residual_no(l, half, t):
            return (0 if l == 0 else 2 * T0) + 2 * t + half

        block = stack.enter_context(nc.Block())

        @block.sync
        def _(sp):
            def source(key):
                l, what, j = key[:3]
                if what == "ADA":
                    return ada_w[l].rearrange("(k p) n -> p k n", p=P)[:, :, 512 * j:512 * j + 512]
                if what == "QA":
                    return w_in[l].rearrange("(k p) n -> p k n", p=P)[:, :, 0:512]
                if what == "QW":
                    return w_in[l].rearrange("(k p) n -> p k n", p=P)[:, :, 2304:2816]
                if what == "U":
                    return w_in[l].rearrange("(k p) n -> p k n", p=P)[:, :, 768 + 512 * j:1280 + 512 * j]
                if what == "GATE":
                    n0 = 3072 + D * j + 512 * key[3]
                    return w_in[l].rearrange("(k p) n -> p k n", p=P)[:, :, n0:n0 + 512]
                if what == "BR":
                    return w_branch[l, j].rearrange("(k p) n -> p k n", p=P)
                if what == "OUT":
                    return w_out[l].rearrange("(k p) n -> p k n", p=P)[:, :, 512 * j:512 * j + 512]

            def expert_source(l, what, e):
                w = {"W1": exp_w1, "W3": exp_w3, "W2": exp_w2}[what]
                return w[l, e].rearrange("(k p) n -> p k n", p=P)

            def wait_free(l, n, more=None):
                if n < SLOTS:
                    return
                key, last = loads[n - SLOTS]
                wait_full(sp, last)

            for l in range(LAYERS):
                T = tiles_of(l)
                for n, (key, _) in enumerate(loads):
                    if key[0] != l or key[1] in ("W1", "W3", "W2"):
                        continue
                    if n >= SLOTS and loads[n - SLOTS][1] is None and loads[n - SLOTS][0][1] in ("W1", "W3", "W2"):
                        pk = loads[n - SLOTS][0]
                        if pk[1] == "W2":
                            wait_full_e(sp, (pk[0], "Y", 1), NEXP - 1)
                        else:
                            wait_full_e(sp, (pk[0], "H1" if pk[1] == "W1" else "H3"), NEXP - 1)
                    else:
                        wait_free(l, n)
                    if key[1] == "KV":
                        dst = slot(key).rearrange("p (k a n) -> p k a n", k=KD, a=2)
                        for a in range(2):
                            n0 = 512 + 2304 * a
                            src = w_in[l].rearrange("(k p) n -> p k n", p=P)[:, :, n0:n0 + 256]
                            sp.dma_start(dst[:, :, a, :], src).then_inc(slot_loaded[n % SLOTS], 16)
                        continue
                    kk = 4 if key[1] == "BR" else KD
                    sp.dma_start(slot(key).rearrange("p (k n) -> p k n", k=kk), source(key)) \
                        .then_inc(slot_loaded[n % SLOTS], 16)
                    if key[1:] == ("ADA", 2):
                        if l:
                            wait_full(sp, (l - 1, "SCL", tiles_of(l - 1) - 1, 1))
                        sp.dma_start(Z, k_z).then_inc(filter_loaded, 16)
                        sp.dma_start(W3, hy_f_w3[l]).then_inc(filter_loaded, 16)
                        sp.dma_start(DEC, k_decay.rearrange("(t p) h n -> p t h n", p=P)).then_inc(filter_loaded, 16)
                        if l == 0:
                            sp.dma_start(X[:, 0:2, :], x[0].rearrange("(t p) d -> p t d", p=P)).then_inc(x_loaded, 16)
                            sp.dma_start(X[:, 2:4, :], ctx_in[0].rearrange("(t p) d -> p t d", p=P)).then_inc(x_loaded, 16)
                for what in ("W1", "W3", "W2"):
                    n = load_no[(l, what, 0)]
                    wait_free(l, n)
                    kk = FE if what == "W2" else KD
                    sp.dma_start(slot((l, what, 0)).rearrange("p (k n) -> p k n", k=kk), expert_source(l, what, 0)) \
                        .then_inc(slot_loaded[n % SLOTS], 16)
                with sp.Fori(1, NEXP) as e:
                    for what in ("W1", "W3", "W2"):
                        n = load_no[(l, what, 0)]
                        wait_full_e(sp, (l, *{"W1": ("H1",), "W3": ("H3",), "W2": ("Y", 1)}[what]), e, back=1)
                        kk = FE if what == "W2" else KD
                        sp.dma_start(slot((l, what, 0)).rearrange("p (k n) -> p k n", k=kk),
                                     expert_source(l, what, e)).then_inc(slot_loaded[n % SLOTS], 16)
                sp.wait_ge(flag_ready, l + 1)
                over = sp.value_load(FLAG[0:1, 0:1], min_val=0, max_val=1)
                with sp.If(over > 0):
                    wait_full_e(sp, (l, "Y", 1), NEXP - 1)
                    for j, what in enumerate(("W1", "W3", "W2")):
                        kk = FE if what == "W2" else KD
                        sp.dma_start(ring[:, j, :].rearrange("p (k n) -> p k n", k=kk), expert_source(l, what, 0)) \
                            .then_inc(over_loaded[l][j], 16)
                    with sp.Fori(1, NEXP) as e:
                        for j, what in enumerate(("W1", "W3", "W2")):
                            b, n, per = over_bank(("Y", T - 1, 1) if what == "W2" else ("H3", FE - 1), T)
                            sp.wait_ge(over_full[l][b], e * per + (n + 1 - per))
                            kk = FE if what == "W2" else KD
                            sp.dma_start(ring[:, j, :].rearrange("p (k n) -> p k n", k=kk),
                                         expert_source(l, what, e)).then_inc(over_loaded[l][j], 16)
                    for key in (("H3", FE - 1), ("Y", T - 1, 1)):
                        b, n, per = over_bank(key, T)
                        sp.wait_ge(over_full[l][b], NEXP * per)
            for t in range(2):
                sp.wait_ge(experts_done, T0 + t + 1)
                sp.dma_start(out[0, t * P:(t + 1) * P, :], X[:, t, :]).then_inc(out_stored, 16)
            sp.wait_ge(out_stored, 32)

        @block.gpsimd
        def _(pool):
            link = chained(pool, pool_steps, [0])
            nc.gpsimd.memset(ones[:, :], 1.0).then_inc(ones_ready, 1)
            nc.gpsimd.memset(HALF[:, :], -0.5).then_inc(ones_ready, 1)
            pool.wait_ge(ones_ready, 2)

            def rms_rows(l, norm):
                for t in range(TT if not norm else tiles_of(l)):
                    i = row_no(l, norm, t)
                    pool.wait_ge(squares, i + 1)
                    link(nc.gpsimd.tensor_scalar(ST[:, 8 + t:9 + t], ST[:, t:t + 1], 1.0 / D, EPS, ALU.mult, ALU.add))
                    link(nc.gpsimd.tensor_tensor(ST[:, 16 + t:17 + t], ST[:, 8 + t:9 + t], HALF[:, 0:1], ALU.pow),
                                rstd_ready, i + 1)

            def rms_heads(l, what, t):
                i = proj[(l, what, t)]
                pool.wait_ge(head_sums, i + 1)
                link(nc.gpsimd.tensor_scalar(HS[:, i % 2, 1, :], HS[:, i % 2, 0, :], 1.0 / HD, EPS, ALU.mult, ALU.add))
                link(nc.gpsimd.tensor_tensor(HS[:, i % 2, 2, :], HS[:, i % 2, 1, :], HALF[:, 0:HEADS], ALU.pow),
                            head_rstd, i + 1)

            for l in range(LAYERS):
                rms_rows(l, 0)
                for what in ("QA", "KV", "QW"):
                    for t in range(TT if what == "KV" else tiles_of(l)):
                        rms_heads(l, what, t)
                rms_rows(l, 1)
                for t in range(tiles_of(l)):
                    for half in range(2):
                        cols = slice(512 * half, 512 * half + 512)
                        pool.wait_ge(tok_mid, tok_no(l, t, half) + 1)
                        link(nc.gpsimd.tensor_tensor(TOK[2][:, t, cols], TOKR[:, t, cols], TOK[1][:, t, cols],
                                                     ALU.subtract), tok_low, tok_no(l, t, half) + 1)

        @block.scalar
        def _(act):
            link = chained(act, act_steps, [0])

            def read(ins, key, more=0):
                b, n = fill_at[key]
                link(ins, bank_free[b], more + n + 1)

            def layer_rows(l):
                return [
                    (PR[0:48, l, :], ada_b[l].rearrange("(k p) -> k p", p=P)),
                    (PR[48:56, l, :], norm1_g[l].rearrange("(k p) -> k p", p=P)),
                    (PR[56:64, l, :], norm2_g[l].rearrange("(k p) -> k p", p=P)),
                    (PR[64:100, l, :], hy_short_w[l].rearrange("j (k p) -> (j k) p", p=P)),
                    (PR[100:112, l, :], hy_short_b[l].rearrange("(k p) -> k p", p=P)),
                    (PR[112:116, l, :], hy_bias[l].rearrange("(k p) -> k p", p=P)),
                    (FP[:, l, 0:1], hy_f_b1[l].rearrange("(p a) -> p a", a=1)),
                    (FP[:, l, 1:2], hy_f_freq[l].rearrange("(p a) -> p a", a=1)),
                    (FP[:, l, 2:3], hy_f_b2[l].rearrange("(p a) -> p a", a=1)),
                    (FW[0:EMB, l, 0, :], hy_f_w1[l]),
                    (FW[:, l, 1, :], hy_f_w2[l]),
                ]

            early = [(CR[0:8, :], c[0].rearrange("(k p) -> k p", p=P)),
                     (CR[8:16, :], c_ctx.rearrange("(k p) -> k p", p=P)),
                     (ident[:, :], k_ident)] + layer_rows(0)
            late = [
                (DF[:, :, :], k_dft.rearrange("(t p) n -> p t n", p=P)),
                (ROPE[:, :, :, :], k_rope.rearrange("(t p) a n -> p t a n", p=P)),
            ]
            for l in range(LAYERS):
                late += [
                    (QKG[:, l, :, :], qk_g[l].partition_broadcast(P)),
                    (SINK[:, l, :], sinks[l].partition_broadcast(P)),
                    (RB[:, l, 0:4], router_g_b[l].partition_broadcast(P)),
                    (RB[:, l, 4:20], router_e_b[l].partition_broadcast(P)),
                    (RW[:, l, :, 0:4], router_g_w[l].rearrange("(k p) n -> p k n", p=P)),
                    (RW[:, l, :, 4:20], router_e_w[l].rearrange("(k p) n -> p k n", p=P)),
                ]
                if l:
                    late += layer_rows(l)
            late += [
                (IF[:, :, :], k_idft.rearrange("(t p) n -> p t n", p=P)),
                (MASK[:, :, :], k_mask.rearrange("(t p) n -> p t n", p=P)),
                (FIRST[:, :], k_first.partition_broadcast(P)),
                (TRI[:, :], k_tri),
                (IOTA[:, :], k_iota.partition_broadcast(P)),
            ]
            assert len(early) == EARLY and len(late) == LATE
            for dst, src in early:
                act.dma_start(dst, src).then_inc(early_loaded, 16)
            for dst, src in late:
                act.dma_start(dst, src).then_inc(params_loaded, 16)

            act.wait_ge(early_loaded, 16 * EARLY)
            link(nc.scalar.activation(CR[:, :], CR[:, :], ACT.Silu), cond_ready, 1)

            def norm_squares(l, norm):
                T = TT if not norm else tiles_of(l)
                for t in range(T):
                    if norm:
                        act.wait_ge(residual_added, residual_no(l, 1, t) + 1)
                    elif l:
                        act.wait_ge(experts_done, t + 1)
                    elif t == 0:
                        act.wait_ge(x_loaded, 32)
                    if norm and t == 0:
                        wait_full(act, (l, "BR", 2, KD - 1))
                    link(nc.scalar.activation(XN[:, t, :], X[:, t, :], ACT.Square, accum_out=ST[:, t:t + 1]),
                                squares, row_no(l, norm, t) + 1)

            def head_square(l, what, t):
                i = proj[(l, what, t)]
                key = (l, what, t)
                wait_full(act, key)
                if what == "KV":
                    b = bank(key)
                    for kind in range(2):
                        link(nc.scalar.copy(V[:, t, kind, :], b[:, 256 * kind + 128:256 * kind + 256]))
                if i >= 2:
                    act.wait_ge(head_sums, i - 1)
                link(nc.scalar.activation(TMP[:, i % 2, :], bank(key)[:, :], ACT.Square), head_squares, i + 1)

            def copy_out(dst, key, src=None):
                wait_full(act, key)
                read(nc.scalar.copy(dst, bank(key)[:, :] if src is None else src), key)

            def copy_gates(l, which):
                for s in range(tiles_of(l) // 2):
                    for half in range(2):
                        copy_out(GB[:, s, 512 * half:512 * half + 512], (l, "GB", which, s, half))

            for l in range(LAYERS):
                T = tiles_of(l)
                N = T * P
                for j in range(12):
                    key = (l, "MOD", j)
                    wait_full(act, key)
                    src = bank(key)[:, 0:4 * WIDE].rearrange("p (m r s) -> p m r s", m=4, s=2)[:, :, 0, :]
                    read(nc.scalar.copy(MOD[:, 4 * j:4 * j + 4, :], src), key)
                    if j in FILTER_SLOTS[0:2]:
                        i = FILTER_SLOTS.index(j)
                        act.wait_ge(filter_arg, 2 * l + i + 1)
                        link(nc.scalar.activation(FT[:, 3 + i, :], FT[:, 1, :], ACT.Sin), filter_sin, 2 * l + i + 1)
                    if j == FILTER_SLOTS[2]:
                        for t in range(2):
                            for half in range(2):
                                wait_read(act, (l, "F3", t, half))
                                link(nc.scalar.activation(DEC[:, t, half, :], FH[:, t, half, :], ACT.Abs),
                                     filter_abs, 4 * l + 2 * t + half + 1)
                    if j == FILTER_SLOTS[3]:
                        norm_squares(l, 0)
                if l == 0:
                    act.wait_ge(params_loaded, 16 * LATE)
                for t in range(T):
                    head_square(l, "QA", t)
                for t in range(TT):
                    head_square(l, "KV", t)
                for t in range(T):
                    copy_out(QT[:, 0, :, t * P:(t + 1) * P], (l, "QAT", t),
                             bank((l, "QAT", t))[:, :].rearrange("p (c n) -> p c n", c=4))
                for t in range(T):
                    head_square(l, "QW", t)
                for t in range(TT):
                    copy_out(KT[:, :, t * P:(t + 1) * P], (l, "KVT", t),
                             bank((l, "KVT", t))[:, 0:256].rearrange("p (c n) -> p c n", c=2))
                for ch in range(12):
                    key = (l, "U", ch)
                    wait_full(act, key)
                    link(nc.scalar.activation(UC[:, ch, 0:N], bank(key)[:, 0:N], ACT.Identity,
                                                     bias=PC[:, 100 + ch:101 + ch], scale=PC[:, 76 + ch:77 + ch]),
                                conv_started, 12 * l + ch + 1)
                for t in range(T):
                    copy_out(QT[:, 1, :, t * P:(t + 1) * P], (l, "QWT", t),
                             bank((l, "QWT", t))[:, :].rearrange("p (c n) -> p c n", c=4))
                yat = {i: s for i, s in enumerate(attention_steps(l))}
                for i, s in yat.items():
                    if s[0] == "S":
                        _, kind, t, h = s
                        u = units[(l, kind, t, h)]
                        g = groups[(l, kind, t)]
                        key = (l, *s)
                        nk = len(keys_of(t)) * P
                        act.wait_ge(neg_max, u + 1)
                        if u >= 3:
                            prev = [k for k, v in units.items() if v == u - 3][0]
                            wait_full(act, (prev[0], "PT", *prev[1:]))
                        nm = NMX[:, u % 4:u % 4 + 1]
                        if kind:
                            link(nc.scalar.activation(AT[:, g % 2, 2, h:h + 1], SINK[:, l, h:h + 1], ACT.Exp, bias=nm))
                        read(nc.scalar.activation(PB[:, u % 3, 0:nk], bank(key)[:, 0:nk], ACT.Exp, bias=nm,
                                                  accum_out=AT[:, g % 2, 1, h:h + 1]), key)
                    elif s[0] == "YAT":
                        _, kind, t = s
                        copy_out(YT[:, kind, :, t * P:(t + 1) * P], (l, *s),
                                 bank((l, *s))[:, :].rearrange("p (c n) -> p c n", c=4))
                for t in range(T):
                    copy_out(VT[:, t, :], (l, "VT", t))
                copy_gates(l, 0)
                for j, b in enumerate((1, 0, 2)):
                    for ch in range(KD):
                        key = (l, "GATE", b, ch)
                        i = KD * j + ch - 2
                        wait_full(act, key)
                        if i >= 0:
                            wait_read(act, (l, "BR", (1, 0, 2)[i // KD], i % KD))
                        read(nc.scalar.activation(TMP[:, ch % 2, 0:N], bank(key)[:, 0:N], ACT.Sigmoid), key)
                norm_squares(l, 1)
                copy_gates(l, 1)
                for t in range(T):
                    for half in range(2):
                        key = (l, "TK", t, half)
                        wait_full(act, key)
                        link(nc.scalar.copy(TOK[0][:, t, 512 * half:512 * half + 512], bank(key)[:, :]),
                             tok_high, tok_no(l, t, half) + 1)
                act.wait_ge(logits_ready, l + 1)
                link(nc.scalar.activation(RT[:, 1, 0:T, 0:5], RT[:, 0, 0:T, 0:5], ACT.Exp), logits_exp, l + 1)
                for t in range(T):
                    for half in range(2):
                        cols = slice(512 * half, 512 * half + 512)
                        wait_read(act, (l, "TK", t, half))
                        link(nc.scalar.copy(TOK[1][:, t, cols], TOKR[:, t, cols]), tok_mid, tok_no(l, t, half) + 1)
                C = CAP[l]
                for half in range(2):
                    key = (l, "GA0", half)
                    copy_out(XG[:, 4 * half:4 * half + 4, 0:C], key,
                             bank(key)[:, 0:4 * C].rearrange("p (k n) -> p k n", k=4))
                with act.Fori(0, NEXP) as e:
                    wait_full_e(act, (l, "H1"), e)
                    wait_read_e(act, (l, "H3"), e, back=1)
                    nc.scalar.activation(TMP[:, 0, 0:4 * C], bank((l, "H1"))[:, 0:4 * C], ACT.Silu) \
                        .then_inc(bank_free[fill_at[(l, "H1")][0]], 1)
                    for half in range(2):
                        key = (l, "GA", half)
                        wait_full_e(act, key, e)
                        nc.scalar.copy(XG[:, 4 * half:4 * half + 4, 0:C],
                                       bank(key)[:, 0:4 * C].rearrange("p (k n) -> p k n", k=4)) \
                            .then_inc(bank_free[fill_at[key][0]], 1)
                    for half in range(2):
                        key = (l, "Y", half)
                        wait_full_e(act, key, e)
                        nc.scalar.copy(YP[0][0:C, 512 * half:512 * half + 512], bank(key)[0:C, :]) \
                            .then_inc(y_rounded, 1)
                act.wait_ge(flag_ready, l + 1)
                over = act.value_load(FLAG[0:1, 0:1], min_val=0, max_val=1)
                with act.If(over > 0):
                    with act.Fori(0, NEXP) as e:
                        for i in range(FE):
                            b, n, per = over_bank(("H1", i), T)
                            act.wait_ge(over_full[l][b], e * per + (n + 1))
                            b2, n2, _ = over_bank(("H3", (i - 2) % FE), T)
                            act.wait_ge(over_free[l][b2], e * per + (n2 + 2 - (per if i < 2 else 0)))
                            nc.scalar.activation(TMP[:, i % 2, 0:N], ps[b][:, 0:N], ACT.Silu) \
                                .then_inc(over_free[l][b], 1)
                    act.wait_ge(over_free[l][over_bank(("H3", FE - 1), T)[0]], NEXP * 2 + 1)

        @block.vector
        def _(dve):
            steps = [0]
            link = chained(dve, dve_steps, steps)
            tt, ts, stt = nc.vector.tensor_tensor, nc.vector.tensor_scalar, nc.vector.scalar_tensor_tensor

            def read(ins, key, more=0):
                b, n = fill_at[key]
                link(ins, bank_free[b], more + n + 1)

            def normalise_rows(l, norm):
                for t in range(TT if not norm else tiles_of(l)):
                    i = row_no(l, norm, t)
                    dve.wait_ge(rstd_ready, i + 1)
                    link(ts(XN[:, t, :], X[:, t, :], ST[:, 16 + t:17 + t], None, ALU.mult), rows_ready, i + 1)

            def modulate(l, norm):
                T = TT if not norm else tiles_of(l)
                for k in range(KD):
                    key = (l, "N2" if norm else "N1", k)
                    wait_full(dve, key)
                    for s in range(T // 2):
                        ins = ts(HT[:, k, SEQ * s:SEQ * s + SEQ], bank(key)[:, SEQ * s:SEQ * s + SEQ],
                                 AM[:, norm, k, s:s + 1], MOD[:, (24 if norm else 0) + k, s:s + 1], ALU.mult, ALU.add)
                        if s == T // 2 - 1:
                            read(ins, key)
                        else:
                            link(ins)

            def head_sum(l, what, t):
                i = proj[(l, what, t)]
                dve.wait_ge(head_squares, i + 1)
                sq = TMP[:, i % 2, :]
                if what == "KV":
                    sq = sq.rearrange("p (a n) -> p a n", a=2)[:, :, 0:P].rearrange("p a (h d) -> p a h d", d=HD)
                    dst = HS[:, i % 2, 0, 0:4].rearrange("p (a h) -> p a h", a=2)
                    link(nc.vector.memset(HS[:, i % 2, 0, 4:8], 1.0))
                else:
                    sq = sq.rearrange("p (h d) -> p h d", d=HD)
                    dst = HS[:, i % 2, 0, :]
                link(nc.vector.tensor_reduce(dst, sq, AX_X, ALU.add), head_sums, i + 1)

            def head_norm(l, what, t):
                i = proj[(l, what, t)]
                key = (l, what, t)
                dve.wait_ge(head_rstd, i + 1)
                if what == "QW":
                    wait_full(dve, (l, "QAT", t))
                rot = t < 2
                tile = t if rot else 2
                if what == "KV":
                    src = bank(key)[:, :].rearrange("p (a n) -> p a n", a=2)[:, :, 0:P] \
                        .rearrange("p a (h d) -> p a h d", d=HD)
                    rs = HS[:, i % 2, 2, 0:4].rearrange("p (a h) -> p a h", a=2).unsqueeze(3) \
                        .to_broadcast([P, 2, 2, HD])
                    mid = TMP[:, 2, 0:256].rearrange("p (a h d) -> p a h d", a=2, d=HD)
                    dst = KN[:, t, :].rearrange("p (a h d) -> p a h d", a=2, d=HD)
                    read(tt(mid, src, rs, ALU.mult), key)
                    for a in range(2):
                        rotate(dst[:, a], mid[:, a], tile, 2 + a, 2, rot, i + 1 if a else None)
                else:
                    src = bank(key)[:, :].rearrange("p (h d) -> p h d", d=HD)
                    rs = HS[:, i % 2, 2, :].unsqueeze(2).to_broadcast([P, HEADS, HD])
                    mid = TMP[:, 2, :].rearrange("p (h d) -> p h d", d=HD)
                    dst = QN[:, t, :].rearrange("p (r g d) -> p g r d", g=2, d=HD)
                    read(tt(mid, src, rs, ALU.mult), key)
                    rotate(dst, mid, tile, 0 if what == "QA" else 1, HEADS, rot, i + 1)

            def rotate(dst, mid, tile, kind, nh, rot, done):
                cg = CG[:, tile, kind, :].unsqueeze(1)
                if nh == HEADS:
                    def by_pair(a):
                        return a.rearrange("p (g r) d -> p g r d", g=2)

                    ins = tt(dst, by_pair(mid), cg.unsqueeze(1).to_broadcast([P, 2, 4, HD]), ALU.mult)
                else:
                    def by_pair(a):
                        return a

                    ins = tt(dst, mid, cg.to_broadcast([P, nh, HD]), ALU.mult)
                if not rot and done:
                    link(ins, qk_ready, done)
                else:
                    link(ins)
                if rot:
                    tmp = TMP[:, 3, 0:nh * HD].rearrange("p (h a b f) -> p h a b f", a=2, b=2, f=16)
                    m5 = mid.rearrange("p h (a b f) -> p h a b f", a=2, b=2)
                    sg = SG[:, tile, kind, :].rearrange("p (a b f) -> p a b f", a=2, b=2)
                    for b in range(2):
                        s1 = sg[:, :, b, :].unsqueeze(1).to_broadcast([P, nh, 2, 16])
                        link(tt(tmp[:, :, :, b, :], m5[:, :, :, 1 - b, :], s1, ALU.mult))
                    ins = tt(dst, dst, by_pair(TMP[:, 3, 0:nh * HD].rearrange("p (h d) -> p h d", d=HD)), ALU.add)
                    if done:
                        link(ins, qk_ready, done)
                    else:
                        link(ins)

            dve.wait_ge(early_loaded, 16 * EARLY)
            for l in range(LAYERS):
                T = tiles_of(l)
                N = T * P
                wait_full(dve, (l, "PR"))
                read(nc.vector.tensor_copy(PC[:, :], bank((l, "PR"))[:, 0:116]), (l, "PR"))
                if l == 0:
                    wait_full(dve, (l, "C"))
                    read(nc.vector.tensor_copy(CC[:, :], bank((l, "C"))[:, 0:16]), (l, "C"))
                for i in range(2):
                    key = (l, f"F{i + 1}")
                    wait_full(dve, key)
                    read(ts(FT[:, 0, :], bank(key)[0:HID, 0:SEQ], FP[:, l, 2 * i:2 * i + 1], FP[:, l, 1:2],
                            ALU.add, ALU.mult), key)
                    link(ts(FT[:, 1, :], FT[:, 0, :], 1.0 / (2 * np.pi), MAGIC, ALU.mult, ALU.add))
                    link(ts(FT[:, 2, :], FT[:, 1, :], -MAGIC, None, ALU.add))
                    for part in TWO_PI:
                        link(stt(FT[:, 0, :], FT[:, 2, :], -part, FT[:, 0, :], ALU.mult, ALU.add))
                    link(ts(FT[:, 1, :], FT[:, 0, :], PI_MAX, -PI_MAX, ALU.min, ALU.max),
                                filter_arg, 2 * l + i + 1)
                    dve.wait_ge(filter_sin, 2 * l + i + 1)
                for t in range(2):
                    for half in range(2):
                        key = (l, "F3", t, half)
                        wait_full(dve, key)
                        if t == 0 and half == 0:
                            dve.wait_ge(filter_loaded, 48 * (l + 1))
                        read(tt(FH[:, t, half, :], bank(key)[:, :], DEC[:, t, half, :], ALU.mult), key)
                for t in range(2):
                    link(tt(FAB[:, t, 0, :], FH[:, t, 0, :], FH[:, t, 1, :], ALU.add))
                    link(tt(FAB[:, t, 1, :], FH[:, t, 0, :], FH[:, t, 1, :], ALU.subtract),
                                filter_ab, 2 * l + t + 1)
                wait_full(dve, (l, "FN"))
                read(nc.vector.reciprocal(FN, bank((l, "FN"))[:, :]), (l, "FN"))
                for m in range(5):
                    key = (l, "FK", m)
                    wait_full(dve, key)
                    read(tt(KS[:, m, :], bank(key)[:, :], FN, ALU.mult), key)
                if l == 0:
                    link(nc.vector.tensor_copy(ident_b[:, :], ident[:, :]))
                    dve.wait_ge(params_loaded, 16 * LATE)
                    link(ts(NSINK[:, :, :], SINK[:, :, :], -1.0, None, ALU.mult))
                for kind, row in enumerate((0, 2, 1, 3)):
                    g = QKG[:, l, row, :]
                    scale = HD ** -0.5 if kind < 2 else 1.0
                    link(ts(CG[:, 2, kind, :], g, scale, None, ALU.mult))
                for tile in range(2):
                    link(tt(CG[:, tile, :, :], CG[:, 2, :, :],
                            ROPE[:, tile, 0, :].unsqueeze(1).to_broadcast([P, 4, HD]), ALU.mult))
                    gg = CG[:, 2, :, :].rearrange("p k (a b f) -> p k a b f", a=2, b=2)
                    so = SG[:, tile, :, :].rearrange("p k (a b f) -> p k a b f", a=2, b=2)
                    sn = ROPE[:, tile, 1, :].rearrange("p (a b f) -> p a b f", a=2, b=2)
                    for b in range(2):
                        link(tt(so[:, :, :, b, :], gg[:, :, :, 1 - b, :],
                                sn[:, :, b, :].unsqueeze(1).to_broadcast([P, 4, 2, 16]), ALU.mult))
                normalise_rows(l, 0)
                wait_read(dve, (l, "MOD", 11))
                link(tt(MOD[:, :, :], MOD[:, :, :], PC[:, 0:48].unsqueeze(2).to_broadcast([P, 48, 2]), ALU.add))
                for norm in range(2):
                    m0 = 24 * norm + 8
                    link(ts(AM[:, norm, :, :], MOD[:, m0:m0 + 8, :], 1.0, None, ALU.add))
                    ins = tt(AM[:, norm, :, :], AM[:, norm, :, :],
                             PC[:, 48 + 8 * norm:56 + 8 * norm].unsqueeze(2).to_broadcast([P, KD, 2]), ALU.mult)
                    if norm:
                        link(ins, mod_ready, l + 1)
                    else:
                        link(ins)
                modulate(l, 0)
                order = [("QA", t) for t in range(T)] + [("KV", t) for t in range(TT)] + [("QW", t) for t in range(T)]
                head_sum(l, *order[0])
                for i, (what, t) in enumerate(order):
                    if i + 1 < len(order) and order[i + 1][0] == what:
                        head_sum(l, *order[i + 1])
                    head_norm(l, what, t)
                    if i + 1 < len(order) and order[i + 1][0] != what:
                        head_sum(l, *order[i + 1])
                S2 = T // 2
                for ch in range(12):
                    key = (l, "U", ch)
                    dve.wait_ge(conv_started, 12 * l + ch + 1)
                    src = bank(key)[:, 0:N].rearrange("p (s n) -> p s n", s=S2)
                    dst = UC[:, ch, 0:N].rearrange("p (s n) -> p s n", s=S2)
                    link(stt(dst[:, :, 1:SEQ], src[:, :, 0:SEQ - 1], PC[:, 64 + ch:65 + ch], dst[:, :, 1:SEQ],
                             ALU.mult, ALU.add))
                    read(stt(dst[:, :, 0:SEQ - 1], src[:, :, 1:SEQ], PC[:, 88 + ch:89 + ch], dst[:, :, 0:SEQ - 1],
                             ALU.mult, ALU.add), key)
                link(tt(UC[:, 8:12, 0:N], UC[:, 8:12, 0:N], UC[:, 4:8, 0:N], ALU.mult), gated_v, l + 1)
                for s in attention_steps(l):
                    if s[0] == "S":
                        _, kind, t, h = s
                        u = units[(l, kind, t, h)]
                        key = (l, *s)
                        nk = len(keys_of(t)) * P
                        wait_full(dve, key)
                        if kind and t < 2:
                            link(tt(bank(key)[:, 0:SEQ], bank(key)[:, 0:SEQ], MASK[:, t, :], ALU.add))
                        nm = NMX[:, u % 4:u % 4 + 1]
                        if u >= 4:
                            prev = [k for k, v in units.items() if v == u - 4][0]
                            wait_read(dve, (prev[0], "S", *prev[1:]))
                        if kind:
                            link(nc.vector.tensor_reduce(nm, bank(key)[:, 0:nk], AX_X, ALU.max, negate=True))
                            link(ts(nm, nm, NSINK[:, l, h:h + 1], None, ALU.min), neg_max, u + 1)
                        else:
                            link(nc.vector.tensor_reduce(nm, bank(key)[:, 0:nk], AX_X, ALU.max, negate=True),
                                        neg_max, u + 1)
                    elif s[0] == "PT":
                        _, kind, t, h = s
                        u = units[(l, kind, t, h)]
                        nk = len(keys_of(t)) * P
                        key = (l, *s)
                        wait_full(dve, key)
                        read(nc.vector.tensor_copy(PTB[:, u % 3, 0:nk], bank(key)[:, 0:nk]), key)
                    elif s[0] == "O" and s[3] % 4 == 3:
                        _, kind, t, h = s
                        g = groups[(l, kind, t)]
                        kv = h // 4
                        four = slice(4 * kv, 4 * kv + 4)
                        key = (l, "O", kind, t, kv)
                        wait_full(dve, key)
                        tot = AT[:, g % 2, 1, four]
                        if kind:
                            link(tt(AT[:, g % 2, 3, four], tot, AT[:, g % 2, 2, four], ALU.add))
                            tot = AT[:, g % 2, 3, four]
                        link(nc.vector.reciprocal(AT[:, g % 2, 4, four], tot))
                        if g >= 2 and kv == 0:
                            prev = [k for k, v in groups.items() if v == g - 2][0]
                            wait_full(dve, (prev[0], "YAT", *prev[1:]))
                        src = bank(key)[:, :].rearrange("p (h a d) -> p h a d", a=2, d=HD)[:, :, kv, :]
                        read(tt(YA[:, g % 2, 256 * kv:256 * kv + 256].rearrange("p (h d) -> p h d", d=HD), src,
                                AT[:, g % 2, 4, four].unsqueeze(2).to_broadcast([P, 4, HD]), ALU.mult), key)
                for s in range(T // 2):
                    for p in range(2):
                        kr, ki = (l, "DFT", s, 0, p), (l, "DFT", s, 1, p)
                        wait_full(dve, kr)
                        wait_full(dve, ki)
                        vr, vi = bank(kr)[:, :], bank(ki)[:, :]
                        Kr, Ki = KS[:, p, :], KS[:, 3 + p, :]
                        KrN = KS[:, 2, :] if p == 0 else Kr
                        link(tt(TMP[:, 0, :], vr, Kr, ALU.mult))
                        link(tt(TMP[:, 1, :], vi, Ki, ALU.mult))
                        read(tt(TMP[:, 2, :], vr, Ki, ALU.mult), kr)
                        read(tt(TMP[:, 3, :], vi, KrN, ALU.mult), ki)
                        link(tt(YS[:, s, p, :], TMP[:, 0, :], TMP[:, 1, :], ALU.subtract))
                        link(tt(YS[:, s, 2 + p, :], TMP[:, 2, :], TMP[:, 3, :], ALU.add),
                                    spec_ready, 2 * seqs[(l, s)] + p + 1)
                for s in range(T // 2):
                    for ch in range(CH):
                        key = (l, "INV", s, ch)
                        wait_full(dve, key)
                        cols = slice(SEQ * s, SEQ * s + SEQ)
                        read(stt(TMP[:, ch % 2, 0:SEQ], UC[:, 8 + ch, cols], PC[:, 112 + ch:113 + ch],
                                 bank(key)[:, 0:SEQ], ALU.mult, ALU.add), key)
                        link(tt(UC[:, ch, cols], UC[:, ch, cols], TMP[:, ch % 2, 0:SEQ], ALU.mult),
                                    yh_ready, CH * seqs[(l, s)] + ch + 1)
                for j, b in enumerate((1, 0, 2)):
                    for ch in range(KD):
                        gate, br = (l, "GATE", b, ch), (l, "BR", b, ch)
                        wait_full(dve, br)
                        wait_read(dve, gate)
                        if j == 0:
                            read(tt(MT[:, ch, 0:N], TMP[:, ch % 2, 0:N], bank(br)[:, 0:N], ALU.mult), br)
                        else:
                            read(tt(TMP[:, 2 + ch % 2, 0:N], TMP[:, ch % 2, 0:N], bank(br)[:, 0:N], ALU.mult), br)
                            ins = tt(MT[:, ch, 0:N], MT[:, ch, 0:N], TMP[:, 2 + ch % 2, 0:N], ALU.add)
                            if j == 2:
                                link(ins, merged, KD * l + ch + 1)
                            else:
                                link(ins)
                for t in range(T):
                    for half in range(2):
                        cols = slice(512 * half, 512 * half + 512)
                        key = (l, "OUT", half, t)
                        wait_full(dve, key)
                        if half == 0 and t == 0:
                            wait_read(dve, (l, "GB", 0, T // 2 - 1, 1))
                        read(tt(TMP[:, 2 + half, :], bank(key)[:, :], GB[:, t // 2, cols], ALU.mult), key)
                        link(tt(X[:, t, cols], X[:, t, cols], TMP[:, 2 + half, :], ALU.add),
                                    residual_added, residual_no(l, half, t) + 1)
                normalise_rows(l, 1)
                modulate(l, 1)
                for t in range(T):
                    key = (l, "LG", t)
                    wait_full(dve, key)
                    link(tt(RT[:, 2, t, 0:4], bank(key)[:, 0:4], RB[:, l, 0:4], ALU.add))
                    read(tt(RT[:, 3, t, :], bank(key)[:, 4:20], RB[:, l, 4:20], ALU.add), key)

                gl, le = RT[:, 2, 0:T, 0:4], RT[:, 3, 0:T, :]
                mx = RT[:, 4, 0:T, 0:1]
                fg = FIRST[:, 0:4].unsqueeze(1).to_broadcast([P, T, 4])
                fe = FIRST[:, 4:20].unsqueeze(1).to_broadcast([P, T, NEXP])

                def red(dst, src):
                    link(nc.vector.tensor_reduce(dst, src, AX_X, ALU.max))

                def op(dst, a, b, alu):
                    link(tt(dst, a, b, alu))

                def first_of_max(dst, src, best, weights, n):
                    op(dst, src, best.to_broadcast([P, T, n]), ALU.is_equal)
                    op(dst, dst, weights, ALU.mult)
                    red(RT[:, 11, 0:T, 0:1], dst)
                    op(dst, dst, RT[:, 11, 0:T, 0:1].to_broadcast([P, T, n]), ALU.is_equal)

                red(mx, gl)
                op(RT[:, 0, 0:T, 0:4], gl, mx.to_broadcast([P, T, 4]), ALU.subtract)
                og = RT[:, 5, 0:T, 0:4]
                first_of_max(og, gl, mx, fg, 4)
                for e4 in range(4):
                    link(nc.vector.tensor_copy(RT[:, 6, 0:T, e4:NEXP:4], og))
                op(le, le, RT[:, 6, 0:T, :], ALU.mult)
                link(ts(RT[:, 6, 0:T, :], RT[:, 6, 0:T, :], BIG, -BIG, ALU.mult, ALU.add))
                op(le, le, RT[:, 6, 0:T, :], ALU.add)
                m1, m2 = RT[:, 4, 0:T, 1:2], RT[:, 4, 0:T, 2:3]
                e1, e2, sel = RT[:, 7, 0:T, :], RT[:, 8, 0:T, :], RT[:, 9, 0:T, :]
                red(m1, le)
                first_of_max(e1, le, m1, fe, NEXP)
                link(ts(RT[:, 6, 0:T, :], e1, -3 * BIG, None, ALU.mult))
                op(le, le, RT[:, 6, 0:T, :], ALU.add)
                red(m2, le)
                first_of_max(e2, le, m2, fe, NEXP)
                link(tt(sel, e1, e2, ALU.add), sel_ready, l + 1)
                link(tt(RT[:, 0, 0:T, 4:5], m2, m1, ALU.subtract), logits_ready, l + 1)
                for t in range(T):
                    for half in range(2):
                        key = (l, "TK", t, half)
                        cols = slice(512 * half, 512 * half + 512)
                        dve.wait_ge(tok_high, tok_no(l, t, half) + 1)
                        read(tt(TOKR[:, t, cols], bank(key)[:, :], TOK[0][:, t, cols], ALU.subtract), key)
                dve.wait_ge(logits_exp, l + 1)
                sg_, r2, r1 = RT[:, 4, 0:T, 3:4], RT[:, 4, 0:T, 4:5], RT[:, 4, 0:T, 5:6]
                link(nc.vector.tensor_reduce(sg_, RT[:, 1, 0:T, 0:4], AX_X, ALU.add))
                link(ts(r1, RT[:, 1, 0:T, 4:5], 1.0, None, ALU.add))
                op(r1, r1, sg_, ALU.mult)
                link(nc.vector.reciprocal(r1, r1))
                op(r2, r1, RT[:, 1, 0:T, 4:5], ALU.mult)
                op(e1, e1, r1.to_broadcast([P, T, NEXP]), ALU.mult)
                op(e2, e2, r2.to_broadcast([P, T, NEXP]), ALU.mult)
                link(tt(CMB[:, 0:T, :], e1, e2, ALU.add))
                C = CAP[l]
                link(nc.vector.memset(CMBX[:, :, 0:1], 0.0))
                link(nc.vector.memset(POS[:, :, NEXP:NEXP + 1], -1.0))
                link(nc.vector.tensor_copy(CMBX[:, 0:T, 1:NEXP + 1], CMB[:, 0:T, :]))
                key = (l, "RANK")
                wait_full(dve, key)
                rank = bank(key)[:, 0:T * WIDE].rearrange("p (t n) -> p t n", t=T)[:, :, 0:NEXP]
                rk, far = RT[:, 10, 0:T, :], RT[:, 6, 0:T, :]
                link(ts(rk, rank, 1.0, None, ALU.add))
                link(nc.vector.tensor_reduce(ST[:, 40:41], bank(key)[:, T * WIDE:T * WIDE + NEXP], AX_X, ALU.max))
                read(ts(far, rank, float(C), None, ALU.is_ge), key)
                link(tt(rk, rk, sel, ALU.mult))
                link(ts(POS[:, 0:T, 0:NEXP], rk, -1.0, None, ALU.add))
                link(tt(CMB[:, 0:T, :], CMB[:, 0:T, :], far, ALU.mult))
                link(ts(FLAG[:, :], ST[:, 40:41], float(C), None, ALU.is_gt), flag_ready, l + 1)
                link(nc.vector.memset(FACC[:, 0:T, :], 0.0))
                for part in YP:
                    link(ts(part, FACC[:, 0, :], 0.0, None, ALU.add))
                link(ts(STB[:, 0:N], FACC[:, 0, 0:N], 0.0, None, ALU.add))
                places = (NEXP + 1) * l
                for t in range(T):
                    ins = ts(S[:, t, 0:C], IOTA[:, 0:C], POS[:, t, 0:1], None, ALU.is_equal)
                    if t < T - 1:
                        link(ins)
                    else:
                        link(ins, places_ready, places + 1)
                base = steps[0]
                with dve.Fori(0, NEXP) as e:
                    nc.vector.tensor_copy(PCOL[:, 0:T], POS[:, 0:T, bass.ds(e + 1, 1)].rearrange("p t a -> p (t a)")) \
                        .then_inc(dve_steps, 1)
                    dve.wait_ge(dve_steps, 2 * e + (base + 1))
                    wait_full_e(dve, (l, "ST"), e)
                    for t in range(T):
                        ins = ts(S[:, t, 0:C], IOTA[:, 0:C], PCOL[:, t:t + 1], None, ALU.is_equal)
                    ins.then_inc(places_ready, 1)
                    key = (l, "H3")
                    wait_full_e(dve, key, e)
                    wait_read_e(dve, (l, "H1"), e)
                    tt(GM[l], TMP[:, 0, 0:4 * C], bank(key)[:, 0:4 * C], ALU.mult) \
                        .then_inc(bank_free[fill_at[key][0]], 1)
                    nc.vector.tensor_copy(CE[:, 0:T], CMBX[:, 0:T, bass.ds(e, 1)].rearrange("p t a -> p (t a)")) \
                        .then_inc(dve_steps, 1)
                    dve.wait_ge(dve_steps, 2 * e + (base + 2))
                    for t in range(T):
                        for half in range(2):
                            key = (l, "SC", t, half)
                            wait_full_e(dve, key, e)
                            cols = slice(512 * half, 512 * half + 512)
                            stt(FACC[:, t, cols], bank(key)[:, :], CE[:, t:t + 1], FACC[:, t, cols],
                                ALU.mult, ALU.add).then_inc(bank_free[fill_at[key][0]], 1)
                    key = (l, "ST")
                    nc.vector.tensor_copy(STB[0:C, 0:N], bank(key)[0:C, 0:N]).then_inc(bank_free[fill_at[key][0]], 1)
                    for half in range(2):
                        key = (l, "Y", half)
                        cols = slice(512 * half, 512 * half + 512)
                        dve.wait_ge(y_rounded, 2 * e + (2 * NEXP * l + half + 1))
                        tt(YP[1][0:C, cols], bank(key)[0:C, :], YP[0][0:C, cols].bitcast(F32), ALU.subtract) \
                            .then_inc(bank_free[fill_at[key][0]], 1)
                steps[0] = base + 2 * NEXP
                wait_read_e(dve, (l, "Y", 1), NEXP - 1)
                link(nc.vector.tensor_copy(CE[:, 0:T], CMBX[:, 0:T, NEXP]))
                for t in range(T):
                    for half in range(2):
                        key = (l, "SCL", t, half)
                        wait_full(dve, key)
                        cols = slice(512 * half, 512 * half + 512)
                        read(stt(FACC[:, t, cols], bank(key)[:, :], CE[:, t:t + 1], FACC[:, t, cols],
                                 ALU.mult, ALU.add), key)
                over = dve.value_load(FLAG[0:1, 0:1], min_val=0, max_val=1)
                with dve.If(over > 0):
                    for b in range(8):
                        dve.sem_inc(over_free[l][b], 1)
                    with dve.Fori(0, NEXP) as e:
                        for i in range(FE):
                            b1, n1, per = over_bank(("H1", i), T)
                            b, n, _ = over_bank(("H3", i), T)
                            dve.wait_ge(over_full[l][b], e * per + (n + 1))
                            dve.wait_ge(over_free[l][b1], e * per + (n1 + 2))
                            tt(GH[:, i, 0:N], TMP[:, i % 2, 0:N], ps[b][:, 0:N], ALU.mult) \
                                .then_inc(over_free[l][b], 1)
                        nc.vector.tensor_copy(CE[:, 0:T],
                                              CMB[:, 0:T, bass.ds(e, 1)].rearrange("p t a -> p (t a)")) \
                            .then_inc(over_steps[l], 1)
                        dve.wait_ge(over_steps[l], e + 1)
                        for t in range(T):
                            for half in range(2):
                                b, n, per = over_bank(("Y", t, half), T)
                                dve.wait_ge(over_full[l][b], e * per + (n + 1))
                                cols = slice(512 * half, 512 * half + 512)
                                stt(FACC[:, t, cols], ps[b][:, :], CE[:, t:t + 1], FACC[:, t, cols],
                                    ALU.mult, ALU.add).then_inc(over_free[l][b], 1)
                    b, n, per = over_bank(("Y", T - 1, 1), T)
                    dve.wait_ge(over_free[l][b], NEXP * per + 1)
                wait_read(dve, (l, "GB", 1, T // 2 - 1, 1))
                for t in range(T):
                    link(tt(FACC[:, t, :], FACC[:, t, :], GB[:, t // 2, :], ALU.mult))
                    link(tt(X[:, t, :], X[:, t, :], FACC[:, t, :], ALU.add),
                                experts_done, (T0 if l else 0) + t + 1)

        @block.tensor
        def _(pe):
            mm = nc.tensor.matmul

            def product(key, dst, pairs):
                for i, (a, b) in enumerate(pairs):
                    ins = mm(dst, a, b, start=(i == 0), stop=(i == len(pairs) - 1))
                return ins

            def norm_transposes(l, norm):
                T = TT if not norm else tiles_of(l)
                for k in range(KD):
                    key = (l, "N2" if norm else "N1", k)
                    wait_bank(pe, key)
                    for t in range(T):
                        if k == 0:
                            pe.wait_ge(rows_ready, row_no(l, norm, t) + 1)
                        ins = nc.tensor.transpose(bank(key)[:, t * P:(t + 1) * P], XN[:, t, k * P:(k + 1) * P],
                                                  ident[:, :])
                    full(ins, key)

            def gate_rows(l, which):
                for s in range(tiles_of(l) // 2):
                    for half in range(2):
                        key = (l, "GB", which, s, half)
                        wait_bank(pe, key)
                        for q in range(4):
                            m = (40 if which else 16) + 4 * half + q
                            ins = mm(bank(key)[:, q * P:(q + 1) * P], MOD[:, m, s:s + 1].to_broadcast([P, P]),
                                     ident[:, :], start=True, stop=True)
                        full(ins, key)

            def token_rows(key, t):
                wait_bank(pe, key)
                w = slot_kn((key[0], key[1], 0))
                full(product(key, bank(key)[:, :], [(HT[:, k, t * P:(t + 1) * P], w[:, k, :]) for k in range(KD)]), key)

            def query_transposes(l, what, src_what, t):
                key = (l, what, t)
                pe.wait_ge(qk_ready, proj[(l, src_what, t)] + 1)
                wait_bank(pe, key)
                for h in range(4):
                    ins = nc.tensor.transpose(bank(key)[:, h * P:(h + 1) * P], QN[:, t, h * P:(h + 1) * P],
                                              ident[:, :])
                full(ins, key)

            def filter_step(l, step):
                if step == 0:
                    key = (l, "F1")
                    pe.wait_ge(filter_loaded, 48 * (l + 1))
                    wait_bank(pe, key)
                    full(mm(bank(key)[0:HID, 0:SEQ], FW[0:EMB, l, 0, :], Z, start=True, stop=True), key)
                elif step == 1:
                    key = (l, "F2")
                    pe.wait_ge(filter_sin, 2 * l + 1)
                    wait_bank(pe, key)
                    full(mm(bank(key)[0:HID, 0:SEQ], FW[:, l, 1, :], FT[:, 3, :], start=True, stop=True), key)
                elif step == 2:
                    pe.wait_ge(filter_sin, 2 * l + 2)
                    for t in range(2):
                        for half in range(2):
                            key = (l, "F3", t, half)
                            wait_bank(pe, key)
                            full(mm(bank(key)[:, :], FT[:, 4, t * P:(t + 1) * P], W3[:, 512 * half:512 * half + 512],
                                    start=True, stop=True), key)
                elif step == 3:
                    key = (l, "FN")
                    wait_bank(pe, key)
                    pe.wait_ge(filter_abs, 4 * l + 4)
                    full(product(key, bank(key)[:, :],
                                 [(ones[:, :], DEC[:, t, h, :]) for t in range(2) for h in range(2)]), key)
                else:
                    pe.wait_ge(filter_ab, 2 * l + 2)
                    pe.wait_ge(params_loaded, 16 * LATE)
                    for m in range(5):
                        key = (l, "FK", m)
                        wait_bank(pe, key)
                        full(product(key, bank(key)[:, :], [(DF[:, t, m * P:(m + 1) * P], FAB[:, t, int(m >= 3), :])
                                                            for t in range(2)]), key)

            pe.wait_ge(early_loaded, 16 * EARLY)
            pe.wait_ge(ones_ready, 2)
            for l in range(LAYERS):
                T = tiles_of(l)
                N = T * P
                key = (l, "PR")
                wait_bank(pe, key)
                full(nc.tensor.transpose(bank(key)[:, 0:116], PR[:, l, :], ident[0:116, 0:116]), key)
                if l == 0:
                    key = (l, "C")
                    pe.wait_ge(cond_ready, 1)
                    wait_bank(pe, key)
                    full(nc.tensor.transpose(bank(key)[:, 0:16], CR[:, :], ident[0:16, 0:16]), key)
                wait_read(pe, (0, "C"))
                cc = CC[:, :].rearrange("p (s k) -> p k s", s=2)
                for j in range(12):
                    if j in FILTER_SLOTS:
                        filter_step(l, FILTER_SLOTS.index(j))
                    key = (l, "MOD", j)
                    wait_slot(pe, (l, "ADA", j))
                    w = slot_kn((l, "ADA", j))
                    wait_bank(pe, key)
                    for q in range(4):
                        ins = product(key, bank(key)[:, q * WIDE:(q + 1) * WIDE],
                                      [(w[:, k, q * P:(q + 1) * P],
                                        cc[:, k, :].unsqueeze(1).to_broadcast([P, WIDE // 2, 2])) for k in range(KD)])
                    full(ins, key)
                pe.wait_ge(mod_ready, l + 1)
                norm_transposes(l, 0)
                wait_read(pe, (l, "N1", KD - 1))
                wait_slot(pe, (l, "QA", 0))
                for t in range(T):
                    token_rows((l, "QA", t), t)
                wait_slot(pe, (l, "KV", 0))
                for t in range(TT):
                    token_rows((l, "KV", t), t)
                for t in range(T):
                    query_transposes(l, "QAT", "QA", t)
                wait_slot(pe, (l, "QW", 0))
                for t in range(T):
                    token_rows((l, "QW", t), t)
                for t in range(TT):
                    key = (l, "KVT", t)
                    pe.wait_ge(qk_ready, proj[(l, "KV", t)] + 1)
                    wait_bank(pe, key)
                    for kind in range(2):
                        ins = nc.tensor.transpose(bank(key)[:, kind * P:(kind + 1) * P],
                                                  KN[:, t, kind * P:(kind + 1) * P], ident[:, :])
                    full(ins, key)
                for ch in range(12):
                    key = (l, "U", ch)
                    if ch % 4 == 0:
                        wait_slot(pe, (l, "U", ch // 4))
                    w = slot_kn((l, "U", ch // 4))
                    wait_bank(pe, key)
                    q = ch % 4
                    full(product(key, bank(key)[:, 0:N], [(w[:, k, q * P:(q + 1) * P], HT[:, k, 0:N])
                                                          for k in range(KD)]), key)
                for t in range(T):
                    query_transposes(l, "QWT", "QW", t)
                wait_read(pe, (l, "QWT", T - 1))
                for s in attention_steps(l):
                    if s[0] == "S":
                        _, kind, t, h = s
                        key = (l, *s)
                        g, r = h // 4, h % 4
                        rows = slice(HD * g, HD * g + HD)
                        k0, nk = keys_of(t)[0], len(keys_of(t))
                        wait_bank(pe, key)
                        full(mm(bank(key)[:, 0:nk * P], QT[rows, kind, r, t * P:(t + 1) * P],
                                KT[rows, kind, k0 * P:(k0 + nk) * P], start=True, stop=True), key)
                    elif s[0] == "PT":
                        _, kind, t, h = s
                        key = (l, *s)
                        u = units[(l, kind, t, h)]
                        wait_read(pe, (l, "S", kind, t, h))
                        wait_bank(pe, key)
                        for j in range(len(keys_of(t))):
                            ins = nc.tensor.transpose(bank(key)[:, j * P:(j + 1) * P],
                                                      PB[:, u % 3, j * P:(j + 1) * P], ident[:, :])
                        full(ins, key)
                    elif s[0] == "O":
                        _, kind, t, h = s
                        key = (l, "O", kind, t, h // 4)
                        u = units[(l, kind, t, h)]
                        if h % 4 == 0:
                            wait_bank(pe, key)
                        wait_read(pe, (l, "PT", kind, t, h))
                        q = h % 4
                        ins = product(key, bank(key)[:, q * P:(q + 1) * P],
                                      [(PTB[:, u % 3, j * P:(j + 1) * P], V[:, kt, kind, :])
                                       for j, kt in enumerate(keys_of(t))])
                        if q == 3:
                            full(ins, key)
                    else:
                        _, kind, t = s
                        key = (l, *s)
                        gi = groups[(l, kind, t)]
                        wait_read(pe, (l, "O", kind, t, 1))
                        wait_bank(pe, key)
                        for q in range(4):
                            ins = nc.tensor.transpose(bank(key)[:, q * P:(q + 1) * P], YA[:, gi % 2, q * P:(q + 1) * P],
                                                      ident[:, :])
                        full(ins, key)
                pe.wait_ge(gated_v, l + 1)
                for t in range(T):
                    key = (l, "VT", t)
                    wait_bank(pe, key)
                    for q in range(CH):
                        ins = nc.tensor.transpose(bank(key)[:, q * P:(q + 1) * P], UC[:, 8 + q, t * P:(t + 1) * P],
                                                  ident[:, :])
                    full(ins, key)
                for s in range(T // 2):
                    wait_read(pe, (l, "VT", 2 * s))
                    wait_read(pe, (l, "VT", 2 * s + 1))
                    for p in range(2):
                        for r in range(2):
                            key = (l, "DFT", s, r, p)
                            col = (0, 1)[p] if r == 0 else (5, 4)[p]
                            wait_bank(pe, key)
                            full(product(key, bank(key)[:, :], [(DF[:, t, col * P:(col + 1) * P], VT[:, 2 * s + t, :])
                                                                for t in range(2)]), key)
                for s in range(T // 2):
                    pe.wait_ge(spec_ready, 2 * seqs[(l, s)] + 2)
                    for ch in range(CH):
                        key = (l, "INV", s, ch)
                        wait_bank(pe, key)
                        full(product(key, bank(key)[:, 0:SEQ], [(YS[:, s, f, ch * P:(ch + 1) * P], IF[:, f, :])
                                                                for f in range(4)]), key)
                gate_rows(l, 0)
                for b in (1, 0, 2):
                    wb = slot((l, "BR", b)).rearrange("p (k n) -> p k n", k=CH)
                    if b == 1:
                        pe.wait_ge(yh_ready, CH * seqs[(l, T // 2 - 1)] + CH)
                    else:
                        wait_read(pe, (l, "YAT", 1, T - 1))
                    for ch in range(KD):
                        if ch % 4 == 0:
                            wait_slot(pe, (l, "GATE", b, ch // 4))
                        wg = slot_kn((l, "GATE", b, ch // 4))
                        key = (l, "GATE", b, ch)
                        q = ch % 4
                        wait_bank(pe, key)
                        full(product(key, bank(key)[:, 0:N], [(wg[:, k, q * P:(q + 1) * P], HT[:, k, 0:N])
                                                              for k in range(KD)]), key)
                        key = (l, "BR", b, ch)
                        if ch == 0:
                            wait_slot(pe, (l, "BR", b))
                        wait_bank(pe, key)
                        y = [UC[:, k, 0:N] if b == 1 else YT[:, b // 2, k, 0:N] for k in range(CH)]
                        full(product(key, bank(key)[:, 0:N], [(wb[:, k, ch * P:(ch + 1) * P], y[k])
                                                              for k in range(CH)]), key)
                pe.wait_ge(merged, KD * l + KD)
                for t in range(T):
                    for half in range(2):
                        if t == 0:
                            wait_slot(pe, (l, "OUT", half))
                        w = slot_kn((l, "OUT", half))
                        key = (l, "OUT", half, t)
                        wait_bank(pe, key)
                        full(product(key, bank(key)[:, :], [(MT[:, k, t * P:(t + 1) * P], w[:, k, :])
                                                            for k in range(KD)]), key)
                norm_transposes(l, 1)
                wait_read(pe, (l, "N2", KD - 1))
                for t in range(T):
                    key = (l, "LG", t)
                    wait_bank(pe, key)
                    full(product(key, bank(key)[:, 0:100],
                                 [(HT[:, k, t * P:(t + 1) * P], RW[:, l, k, :].unsqueeze(1).to_broadcast([P, 5, 20]))
                                  for k in range(KD)]), key)
                gate_rows(l, 1)
                C = CAP[l]
                for t in range(T):
                    for half in range(2):
                        key = (l, "TK", t, half)
                        wait_bank(pe, key)
                        for q in range(4):
                            ins = nc.tensor.transpose(bank(key)[:, q * P:(q + 1) * P],
                                                      HT[:, 4 * half + q, t * P:(t + 1) * P], ident[:, :])
                        full(ins, key)
                key = (l, "RANK")
                wait_bank(pe, key)
                pe.wait_ge(sel_ready, l + 1)
                sel = RT[:, 9, :, :].unsqueeze(2).to_broadcast([P, TT, WIDE // NEXP, NEXP])
                for t in range(T):
                    product(key, bank(key)[:, t * WIDE:(t + 1) * WIDE],
                            [(TRI[:, :] if u == t else ones[:, :], sel[:, u]) for u in range(t + 1)])
                full(product(key, bank(key)[:, T * WIDE:(T + 1) * WIDE], [(ones[:, :], sel[:, u]) for u in range(T)]),
                     key)

                def gather(key):
                    for q in range(4):
                        k = 4 * key[2] + q
                        ins = product(key, bank(key)[:, q * C:(q + 1) * C],
                                      [(part[:, t, k * P:(k + 1) * P], S[:, t, 0:C]) for part in TOK
                                       for t in range(T)])
                    full(ins, key)

                def scatter(key):
                    _, _, t, half = key
                    full(product(key, bank(key)[:, :], [(STB[0:C, t * P:(t + 1) * P],
                                                         part[0:C, 512 * half:512 * half + 512]) for part in YP]), key)

                pe.wait_ge(places_ready, (NEXP + 1) * l + 1)
                pe.wait_ge(tok_low, tok_no(l, T - 1, 1) + 1)
                for half in range(2):
                    wait_bank(pe, (l, "GA0", half))
                    gather((l, "GA0", half))
                with pe.Fori(0, NEXP) as e:
                    key = (l, "ST")
                    wait_bank_e(pe, key, e)
                    for t in range(T):
                        ins = mm(bank(key)[0:C, t * P:(t + 1) * P], S[:, t, 0:C], ident_b[:, :], start=True, stop=True)
                    full(ins, key)
                    wait_read_e(pe, (l, "GA", 1), e, back=1)
                    for what, lk in (("H1", "W1"), ("H3", "W3")):
                        key = (l, what)
                        wait_slot(pe, (l, lk, 0), e * 16)
                        w = slot_kn((l, lk, 0))
                        wait_bank_e(pe, key, e)
                        for i in range(FE):
                            ins = product(key, bank(key)[:, i * C:(i + 1) * C],
                                          [(w[:, k, i * P:(i + 1) * P], XG[:, k, 0:C]) for k in range(KD)])
                        full(ins, key)
                    wait_read_e(pe, (l, "Y", 1), e, back=1)
                    wait_read_e(pe, (l, "ST"), e, back=1)
                    for t in range(T):
                        for half in range(2):
                            wait_bank_e(pe, (l, "SC", t, half), e)
                            scatter((l, "SC", t, half))
                    pe.wait_ge(places_ready, e + ((NEXP + 1) * l + 2))
                    for half in range(2):
                        wait_bank_e(pe, (l, "GA", half), e)
                        gather((l, "GA", half))
                    wait_slot(pe, (l, "W2", 0), e * 16)
                    w2 = slot((l, "W2", 0)).rearrange("p (k n) -> p k n", k=FE)
                    wait_read_e(pe, (l, "H3"), e)
                    gm = GM[l].rearrange("p (f n) -> p f n", f=FE)
                    for half in range(2):
                        key = (l, "Y", half)
                        wait_bank_e(pe, key, e)
                        full(product(key, bank(key)[0:C, :], [(gm[:, k, :], w2[:, k, 512 * half:512 * half + 512])
                                                              for k in range(FE)]), key)
                wait_read_e(pe, (l, "Y", 1), NEXP - 1)
                wait_read_e(pe, (l, "ST"), NEXP - 1)
                for t in range(T):
                    for half in range(2):
                        wait_bank(pe, (l, "SCL", t, half))
                        scatter((l, "SCL", t, half))
                pe.wait_ge(flag_ready, l + 1)
                over = pe.value_load(FLAG[0:1, 0:1], min_val=0, max_val=1)
                with pe.If(over > 0):
                    with pe.Fori(0, NEXP) as e:
                        for j in range(2):
                            pe.wait_ge(over_loaded[l][j], e * 16 + 16)
                        for i in range(FE):
                            for j, what in enumerate(("H1", "H3")):
                                b, n, per = over_bank((what, i), T)
                                w = ring[:, j, :].rearrange("p (k n) -> p k n", k=KD)
                                pe.wait_ge(over_free[l][b], e * per + (n + 1))
                                product(None, ps[b][:, 0:N], [(w[:, k, i * P:(i + 1) * P], HT[:, k, 0:N])
                                                              for k in range(KD)]).then_inc(over_full[l][b], 1)
                        pe.wait_ge(over_loaded[l][2], e * 16 + 16)
                        w2 = ring[:, 2, :].rearrange("p (k n) -> p k n", k=FE)
                        for i in (FE - 2, FE - 1):
                            b, n, per = over_bank(("H3", i), T)
                            pe.wait_ge(over_free[l][b], e * per + (n + 2))
                        for t in range(T):
                            for half in range(2):
                                b, n, per = over_bank(("Y", t, half), T)
                                pe.wait_ge(over_free[l][b], e * per + (n + 1))
                                product(None, ps[b][:, :],
                                        [(GH[:, k, t * P:(t + 1) * P], w2[:, k, 512 * half:512 * half + 512])
                                         for k in range(FE)]).then_inc(over_full[l][b], 1)
                    for b in range(4, 8):
                        pe.wait_ge(over_free[l][b], NEXP * (T // 2) + 1)


EARLY = 3 + 11
LATE = 6 * LAYERS + 11 * (LAYERS - 1) + 7


def constants():
    n = SEQ
    t = np.arange(n)
    f = np.arange(n)
    ang = 2 * np.pi * np.outer(t, f) / (2 * n)
    cos, sin = np.cos(ang), -np.sin(ang)
    alt = (-1.0) ** t
    cosn, sinn = cos[:, 0:P].copy(), sin[:, 0:P].copy()
    cosn[:, 0] = alt
    sinn[:, 0] = alt
    dft = np.concatenate([cos, cosn, sin, sinn], axis=1)
    icos = 2 * np.cos(ang).T / (2 * n)
    icos[0] /= 2
    isin = -2 * np.sin(ang).T / (2 * n)
    isin[0] = alt / (2 * n)
    idft = np.concatenate([icos, isin], axis=0)
    pos = (np.arange(n) / (n - 1)).astype(np.float32)
    deltas = np.abs(np.linspace(np.log(1e-2) / 1.5, np.log(1e-2) / 0.3, HW)).astype(np.float32)
    dec = np.exp(-pos[:, None] * deltas[None]).astype(np.float32)
    dec2 = np.stack([dec, dec], axis=1)
    dec2[0, 1] = 0.0
    bands = np.linspace(1e-4, 15, 16).astype(np.float32)
    za = (2 * np.pi * bands.astype(np.float64)[None] * np.arange(n)[:, None] / n)
    z = np.concatenate([pos[:, None], np.cos(za), -np.sin(za)], axis=1).T
    inv = 10000.0 ** (-np.arange(16) / 16.0)
    row, col = np.arange(n) // 64, np.arange(n) % 64
    a = np.stack([row[:, None] * inv, col[:, None] * inv], axis=1)
    c = np.stack([np.cos(a), np.cos(a)], axis=2).reshape(n, HD)
    s = np.stack([-np.sin(a), np.sin(a)], axis=2).reshape(n, HD)
    rope = np.stack([c, s], axis=1)
    mask = np.where(np.abs(np.arange(n)[None] - np.arange(n)[:, None]) <= 128, 0.0, -BIG)
    first = np.concatenate([np.arange(4, 0, -1), np.arange(16, 0, -1)])
    out = {"k_ident": np.eye(P), "k_dft": dft, "k_idft": idft, "k_decay": dec2, "k_z": z, "k_rope": rope,
           "k_mask": mask, "k_first": first, "k_tri": np.triu(np.ones((P, P)), 1), "k_iota": np.arange(P)}
    return {k: np.ascontiguousarray(v, dtype=np.float32) for k, v in out.items()}


_INS = ["x", "c", "ctx", "c_ctx", "ada_w", "ada_b", "norm1_g", "norm2_g", "w_in", "qk_g", "hy_short_w", "hy_short_b",
        "hy_f_w1", "hy_f_b1", "hy_f_freq", "hy_f_w2", "hy_f_b2", "hy_f_w3", "hy_bias", "sinks", "w_branch", "w_out",
        "router_g_w", "router_g_b", "router_e_w", "router_e_b", "exp_w1", "exp_w3", "exp_w2"]


def kernel(**inputs):
    import concourse.bacc as _bacc
    from concourse.bass_utils import run_bass_kernel_spmd as _run

    nc = _bacc.Bacc("TRN2", target_bir_lowering=False, num_devices=1)
    arrays, args = {}, []
    data = {k: np.ascontiguousarray(inputs[k]) for k in _INS}
    data.update(constants())
    for name, a in data.items():
        arrays[f"in_{name}"] = a
        args.append(nc.dram_tensor(f"in_{name}", a.shape, mybir.dt.from_np(a.dtype), kind="ExternalInput").ap())
    args.append(nc.dram_tensor("out_0", (1, SEQ, D), F32, kind="ExternalOutput").ap())
    build(nc, *args)
    r = _run(nc, [arrays], core_ids=[0])
    return r.results[0]["out_0"]
```

```python
from contextlib import ExitStack

import numpy as np

import concourse.bass as bass
from concourse import mybir

F32 = mybir.dt.float32
F32R = mybir.dt.float32r
BF16 = mybir.dt.bfloat16
ALU = mybir.AluOpType
ACT = mybir.ActivationFunctionType
AX_X = mybir.AxisListType.X

P = 128
D = 1024
KD = D // P
SEQ = 256
LAYERS = 2
HD = 64
HEADS = 8
HW = 512
CH = HW // P
NEXP = 16
NGRP = 4
DE = 512
FE = DE // P
HID = 64
EMB = 33
SLOTS = 3
SLOT = KD * 512
TT = 4
EPS = 1e-6
BIG = 1e30
MAGIC = 12582912.0
TWO_PI = (6.28125, 0.0019350051879882812, 3.0199159819e-07)
PI_MAX = 3.1415925


def chained(engine, own, count):
    def link(ins, sem=None, value=None):
        if sem is None:
            count[0] += 1
            sem, value = own, count[0]
        ins.then_inc(sem, 1)
        engine.wait_ge(sem, value)
    return link


def tiles_of(l):
    return TT if l < LAYERS - 1 else 2


def attention_units(l):
    return [(kind, t, h) for kind in range(2) for t in range(tiles_of(l)) for h in range(HEADS)]


def keys_of(t):
    return (0, 1, 2, 3) if t < 2 else (2, 3)


LAG_PT, LAG_O = 2, 3


def attention_steps(l):
    units = attention_units(l)
    steps = []
    for i in range(len(units) + LAG_O + 2):
        if i < len(units):
            steps.append(("S", *units[i]))
        if 0 <= i - LAG_O < len(units):
            steps.append(("O", *units[i - LAG_O]))
        if 0 <= i - LAG_PT < len(units):
            steps.append(("PT", *units[i - LAG_PT]))
        j = i - LAG_O - 2
        if 0 <= j < len(units) and units[j][2] == HEADS - 1:
            steps.append(("YAT", *units[j][:2]))
    return steps


CHUNK = 512
CHUNKS = 3 * SLOT // CHUNK
BUFS = 4
ALLB = tuple(range(8))
CAP = (112, 96)
PARTS_COLS = 2 * (D + (KD + FE) * max(CAP) + BUFS * CHUNK) + TT * P
FILTER_BANKS = tuple(range(6))
MOD_BANKS = (6, 7)
FILTER_SLOTS = (3, 5, 7, 9, 11)
WIDE = 96
SC_BANKS = (7, 5, 6)
OVER_AT = {(what, i): (2 * w + i % 2, i // 2) for w, what in enumerate(("H1", "H3")) for i in range(FE)}


def by_pool(c):
    return c % 3 == 1


def split_count(c):
    p = (c + 2) // 3
    return c + 1 - p, p


ENDS = {CHUNKS // 3 - 1: ("H1",), 2 * CHUNKS // 3 - 1: ("H3",), CHUNKS - 2: ("Y", 0), CHUNKS - 1: ("Y", 1)}
USED = CHUNKS - len(ENDS)


SCATTER_AFTER = [3 + 3 * i // 2 for i in range(2 * TT)]


GATE_GROUPS = [(b, g) for b in (1, 0, 2) for g in range(2)]


def used_count(c):
    return len([i for i in range(c + 1) if i not in ENDS])


def plan_fills():
    at, count, turn, per = {}, [0] * 8, {}, {}

    def add(key, banks):
        t = turn.get(banks, 0)
        turn[banks] = t + 1
        b = banks[t % len(banks)]
        at[key] = (b, count[b])
        count[b] += 1

    for l in range(LAYERS):
        T = tiles_of(l)
        add((l, "PR"), ALLB)
        if l == 0:
            add((l, "C"), ALLB)
        for j in range(12):
            add((l, "MOD", j), MOD_BANKS)
        for k in ("F1", "F2"):
            add((l, k), FILTER_BANKS)
        for t in range(2):
            for half in range(2):
                add((l, "F3", t, half), FILTER_BANKS)
        add((l, "FN"), FILTER_BANKS)
        for m in range(5):
            add((l, "FK", m), FILTER_BANKS)
        for k in range(KD):
            add((l, "N1", k), ALLB)
        for t in range(T):
            add((l, "QA", t), ALLB)
        for t in range(TT):
            add((l, "KV", t), ALLB)
        for t in range(T):
            add((l, "QAT", t), ALLB)
        for t in range(T):
            add((l, "QW", t), ALLB)
        for t in range(TT):
            add((l, "KVT", t), ALLB)
        for c in range(12):
            add((l, "U", c), ALLB)
        for t in range(T):
            add((l, "QWT", t), ALLB)
        for step in attention_steps(l):
            if step[0] == "S":
                add((l, *step), (0, 1, 2))
            elif step[0] == "PT" or step[0] == "YAT":
                add((l, *step), (3, 4, 5))
            elif step[3] % 4 == 0:
                add((l, "O", step[1], step[2], step[3] // 4), (6, 7))
        for t in range(T):
            add((l, "VT", t), (0, 1, 2, 3))
        for s in range(T // 2):
            for p in range(2):
                for r in range(2):
                    add((l, "DFT", s, r, p), ALLB)
        for s in range(T // 2):
            for c in range(CH):
                add((l, "INV", s, c), ALLB)
        for s in range(T // 2):
            for half in range(2):
                add((l, "GB", 0, s, half), ALLB)
        for b, g in GATE_GROUPS:
            for q in range(4):
                add((l, "GATE", b, 4 * g + q), (4 + q,))
                add((l, "BR", b, 4 * g + q), (q,))
        for t in range(T):
            for half in range(2):
                add((l, "OUT", half, t), ALLB)
        for k in range(KD):
            add((l, "N2", k), ALLB)
        for t in range(T):
            add((l, "LG", t), ALLB)
        for s in range(T // 2):
            for half in range(2):
                add((l, "GB", 1, s, half), ALLB)
        for t in range(T):
            for half in range(2):
                add((l, "TK", t, half), ALLB)
        add((l, "RANK"), ALLB)
        scatters = [(t, half) for t in range(T) for half in range(2)]
        for half in range(2):
            add((l, "GA0", half), (3 + half,))
            add((l, "Y0", half), (5 + half,))
        before = list(count)
        add((l, "ST"), (2,))
        add((l, "H1"), (0,))
        add((l, "H3"), (1,))
        for i, (t, half) in enumerate(scatters):
            add((l, "SC", t, half), SC_BANKS[i % 3:i % 3 + 1])
        add((l, "GA", 0), (3,))
        add((l, "GT"), (2,))
        add((l, "GA", 1), (4,))
        for half in range(2):
            add((l, "Y", half), (5 + half,))
        for b in range(8):
            per[(l, b)] = count[b] - before[b]
            count[b] += (NEXP - 1) * per[(l, b)]
        for i, (t, half) in enumerate(scatters):
            add((l, "SCL", t, half), SC_BANKS[i % 3:i % 3 + 1])
    return at, per


def weight_loads():
    out = []
    for l in range(LAYERS):
        for j in range(12):
            out.append(((l, "ADA", j), (l, "MOD", j)))
        for what in ("QA", "KV", "QW"):
            out.append(((l, what, 0), (l, what, (TT if what == "KV" else tiles_of(l)) - 1)))
        for j in range(3):
            out.append(((l, "U", j), (l, "U", 4 * j + 3)))
        for b in (1, 0, 2):
            out.append(((l, "GATE", b, 0), (l, "GATE", b, 3)))
            out.append(((l, "BR", b), (l, "BR", b, KD - 1)))
            out.append(((l, "GATE", b, 1), (l, "GATE", b, 7)))
        for half in range(2):
            out.append(((l, "OUT", half), (l, "OUT", half, tiles_of(l) - 1)))
        for e in range(NEXP):
            for what in ("W1", "W3", "W2"):
                out.append(((l, what, e), None))
    return out


def build(nc, x, c, ctx_in, c_ctx, ada_w, ada_b, norm1_g, norm2_g, w_in, qk_g, hy_short_w, hy_short_b, hy_f_w1,
          hy_f_b1, hy_f_freq, hy_f_w2, hy_f_b2, hy_f_w3, hy_bias, sinks, w_branch, w_out, router_g_w, router_g_b,
          router_e_w, router_e_b, exp_w1, exp_w3, exp_w2, k_ident, k_dft, k_idft, k_decay, k_z, k_rope, k_mask,
          k_first, k_tri, k_iota, out):
    fill_at, fills_per_expert = plan_fills()
    loads = weight_loads()
    load_no = {key: n for n, (key, _) in enumerate(loads)}
    loaded_at, total = [], [0] * SLOTS
    for n, (key, _) in enumerate(loads):
        total[n % SLOTS] += 32 if key[1] == "KV" else 16
        loaded_at.append(total[n % SLOTS])

    with ExitStack() as stack:
        def sb(name, shape):
            return stack.enter_context(nc.sbuf_tensor(name, shape, F32))

        def sem(name):
            return stack.enter_context(nc.semaphore(name))

        ps = [stack.enter_context(nc.psum_tensor(f"bank{b}", [P, 512], F32)) for b in range(8)]

        X = sb("X", [P, TT, D])
        HT = sb("HT", [P, KD, TT * P])
        ring = sb("ring", [P, SLOTS, SLOT])
        R1 = sb("R1", [P, 12 * 512])
        R2 = sb("R2", [P, TT * D])
        with nc.sbuf_tensor("R3", [P, PARTS_COLS], F32) as R3:
            pass
        parts_r = stack.enter_context(nc.sbuf_tensor("parts_r", [P, PARTS_COLS], F32R))
        KSG = sb("KSG", [P, 5 * HW])
        with nc.sbuf_tensor("YA", [P, 2, 512], F32) as YA:
            pass
        YA_r = stack.enter_context(nc.sbuf_tensor("YA_r", [P, 2 * CHUNK], F32R))
        TMP = sb("TMP", [P, 4, 512])
        ident = sb("ident", [P, P])
        ones = sb("ones", [P, P])
        ident_b = stack.enter_context(nc.sbuf_tensor("ident_b", [P, P], BF16))
        DF = sb("DF", [P, 2, 6 * P])
        IF = sb("IF", [P, 4, SEQ])
        ROPE = sb("ROPE", [P, 2, 2, HD])
        CG = sb("CG", [P, 3, 4, HD])
        SG = sb("SG", [P, 2, 4, HD])
        MASK = sb("MASK", [P, 2, SEQ])
        QKG = sb("QKG", [P, LAYERS, 4, HD])
        SINK = sb("SINK", [P, LAYERS, HEADS])
        NSINK = sb("NSINK", [P, LAYERS, HEADS])
        PR = sb("PR", [116, LAYERS, P])
        PC = sb("PC", [P, 116])
        CR = sb("CR", [16, P])
        CC = sb("CC", [P, 16])
        FP = sb("FP", [HID, LAYERS, 3])
        FW = sb("FW", [HID, LAYERS, 2, HID])
        MOD = sb("MOD", [P, 48, 2])
        AM = sb("AM", [P, 2, KD, 2])
        RW = sb("RW", [P, LAYERS, KD, 20])
        RB = sb("RB", [P, LAYERS, 20])
        FIRST = sb("FIRST", [P, 20])
        ST = sb("ST", [P, 64])
        HS = sb("HS", [P, 2, 4, HEADS])
        AT = sb("AT", [P, 2, 5, HEADS])
        NMX = sb("NMX", [P, 4])
        CMB = sb("CMB", [P, TT, NEXP])
        CE = sb("CE", [P, TT])
        TRI = sb("TRI", [P, P])
        IOTA = sb("IOTA", [P, P])
        POS = sb("POS", [P, TT, NEXP + 1])
        CMBX = sb("CMBX", [P, TT, NEXP + 1])
        PCOL = sb("PCOL", [P, TT])
        FLAG = stack.enter_context(nc.sbuf_tensor("FLAG", [P, 1], mybir.dt.int32))
        HALF = sb("HALF", [P, 16])

        KS = KSG[:, :].rearrange("p (m n) -> p m n", m=5)
        GB = KSG[:, 0:2 * D].rearrange("p (s d) -> p s d", s=2)
        UC = R1[:, :].rearrange("p (c n) -> p c n", c=12)
        MT = R1[:, 2048:6144].rearrange("p (k n) -> p k n", k=KD)
        GH = R1[:, 0:2048].rearrange("p (f n) -> p f n", f=FE)
        XN = R2[:, :].rearrange("p (t d) -> p t d", t=TT)
        YT = R2[:, :].rearrange("p (a c n) -> p a c n", a=2, c=CH)
        FACC = R2[:, :].rearrange("p (t d) -> p t d", t=TT)
        DEC = R3[:, 0:2048].rearrange("p (t h n) -> p t h n", t=2, h=2)
        W3 = R3[0:HID, 2048:3072]
        FH = R3[:, 3072:5120].rearrange("p (t h n) -> p t h n", t=2, h=2)
        FAB = R3[:, 5120:7168].rearrange("p (t h n) -> p t h n", t=2, h=2)
        FN = R3[:, 7168:7680]
        Z = R3[0:EMB, 7680:7936]
        FT = R3[0:HID, 7936:9216].rearrange("p (a n) -> p a n", a=5)
        QT = R3[:, 0:4096].rearrange("p (a c n) -> p a c n", a=2, c=4)
        KN = YA[:, :, :].rearrange("p a (b n) -> p (a b) n", b=2)
        KT = R3[:, 4096:5120].rearrange("p (a n) -> p a n", a=2)
        V = R3[:, 5120:6144].rearrange("p (t a n) -> p t a n", t=TT, a=2)
        QN = R3[:, 6144:8192].rearrange("p (t n) -> p t n", t=4)
        PB = R3[:, 6144:7680].rearrange("p (t n) -> p t n", t=3)
        PTB = R3[:, 7680:9216].rearrange("p (t n) -> p t n", t=3)
        RT = R3[:, 8448:9216].rearrange("p (a t n) -> p a t n", a=12, t=TT)
        S = YA[:, 0, 0:256].bitcast(BF16).rearrange("p (t n) -> p t n", t=TT)
        YP = [parts_r[:, p * D:(p + 1) * D] for p in range(2)]
        STB = parts_r[:, 2 * D:2 * D + TT * P]
        pos, XGP, GTP = 2 * D + TT * P, [], []
        for p in range(2):
            XGP.append(parts_r[:, pos:pos + KD * max(CAP)].rearrange("p (k n) -> p k n", k=KD))
            pos += KD * max(CAP)
        for p in range(2):
            GTP.append(parts_r[:, pos:pos + FE * max(CAP)].rearrange("p (k n) -> p k n", k=FE))
            pos += FE * max(CAP)
        WP = parts_r[:, pos:PARTS_COLS].rearrange("p (b a n) -> p b a n", b=BUFS, a=2)
        GM = TMP[:, 1, :]
        HTP, GW = [], []
        for l in range(LAYERS):
            n = KD * P * tiles_of(l)
            HTP.append([parts_r[:, p * n:(p + 1) * n].rearrange("p (k n) -> p k n", k=KD) for p in range(2)])
            room = [parts_r[:, 2 * n + 2 * CHUNK * i:2 * n + 2 * CHUNK * (i + 1)]
                    for i in range((PARTS_COLS - 2 * n) // (2 * CHUNK))] + [YA_r[:, :]]
            GW.append([a.rearrange("p (a n) -> p a n", a=2) for a in room])
        TOK = [R1[:, 2048 * i:2048 * i + 2048].bitcast(BF16).rearrange("p (t d) -> p t d", t=TT) for i in range(3)]
        TOKR = R2[:, :].rearrange("p (t d) -> p t d", t=TT)
        VT = R3[:, 0:2048].rearrange("p (t n) -> p t n", t=TT)
        YS = R3[:, 2048:6144].rearrange("p (s f n) -> p s f n", s=2, f=4)

        bank_full = [sem(f"bank_full{b}") for b in range(8)]
        bank_free = [sem(f"bank_free{b}") for b in range(8)]
        slot_loaded = [sem(f"slot_loaded{s}") for s in range(SLOTS)]
        consts_loaded = sem("consts_loaded")
        early_loaded = sem("early_loaded")
        network_loaded = sem("network_loaded")
        params_loaded = sem("params_loaded")
        x_loaded = sem("x_loaded")
        filter_loaded = sem("filter_loaded")
        out_stored = sem("out_stored")
        dve_steps = sem("dve_steps")
        act_steps = sem("act_steps")
        pool_steps = sem("pool_steps")
        cond_ready = sem("cond_ready")
        ones_ready = sem("ones_ready")
        filter_arg = sem("filter_arg")
        filter_sin = sem("filter_sin")
        qk_ready = sem("qk_ready")
        merged = sem("merged")
        filter_abs = sem("filter_abs")
        filter_ab = sem("filter_ab")
        mod_ready = sem("mod_ready")
        squares = sem("squares")
        rstd_ready = sem("rstd_ready")
        rows_ready = sem("rows_ready")
        head_squares = sem("head_squares")
        head_sums = sem("head_sums")
        head_rstd = sem("head_rstd")
        conv_started = sem("conv_started")
        gated_v = sem("gated_v")
        neg_max = sem("neg_max")
        ya_ready = sem("ya_ready")
        spec_ready = sem("spec_ready")
        yh_ready = sem("yh_ready")
        residual_added = sem("residual_added")
        logits_ready = sem("logits_ready")
        logits_exp = sem("logits_exp")
        sel_ready = sem("sel_ready")
        places_ready = sem("places_ready")
        tok_high = sem("tok_high")
        tok_mid = sem("tok_mid")
        tok_low = sem("tok_low")
        tok_low_dve = sem("tok_low_dve")
        ht_high = sem("ht_high")
        ht_low = sem("ht_low")
        gate_high = sem("gate_high")
        gate_low = sem("gate_low")
        gate_used = sem("gate_used")
        chunk_high = sem("chunk_high")
        chunk_low = sem("chunk_low")
        chunk_low_pool = sem("chunk_low_pool")
        chunk_used = sem("chunk_used")
        x_rounded = sem("x_rounded")
        g_rounded = sem("g_rounded")
        y_rounded = sem("y_rounded")
        flag_ready = sem("flag_ready")
        over_full = [[sem(f"over_full{l}_{b}") for b in range(8)] for l in range(LAYERS)]
        over_free = [[sem(f"over_free{l}_{b}") for b in range(8)] for l in range(LAYERS)]
        over_steps = [sem(f"over_steps{l}") for l in range(LAYERS)]
        over_loaded = [[sem(f"over_loaded{l}_{s}") for s in range(3)] for l in range(LAYERS)]
        experts_done = sem("experts_done")

        def bank(key):
            return ps[fill_at[key][0]]

        def wait_bank(eng, key, more=0):
            b, n = fill_at[key]
            if n:
                eng.wait_ge(bank_free[b], more + n)

        def wait_full(eng, key, more=0):
            b, n = fill_at[key]
            eng.wait_ge(bank_full[b], more + n + 1)

        def wait_read(eng, key, more=0):
            b, n = fill_at[key]
            eng.wait_ge(bank_free[b], more + n + 1)

        def turn(key, e, n):
            return e * fills_per_expert[(key[0], fill_at[key][0])] + n

        def wait_bank_e(eng, key, e):
            b, n = fill_at[key]
            eng.wait_ge(bank_free[b], turn(key, e, n))

        def wait_full_e(eng, key, e, back=0):
            b, n = fill_at[key]
            eng.wait_ge(bank_full[b], turn(key, e, n + 1 - back * fills_per_expert[(key[0], b)]))

        def wait_read_e(eng, key, e, back=0):
            b, n = fill_at[key]
            eng.wait_ge(bank_free[b], turn(key, e, n + 1 - back * fills_per_expert[(key[0], b)]))

        def over_bank(key, T):
            if key[0] == "Y":
                j = 2 * key[1] + key[2]
                return 4 + j % 4, j // 4, T // 2
            return (*OVER_AT[key], 2)

        def full(ins, key):
            ins.then_inc(bank_full[fill_at[key][0]], 1)

        def slot_of(key):
            return load_no[key] % SLOTS

        def wait_slot(eng, key, more=0):
            n = load_no[key]
            eng.wait_ge(slot_loaded[n % SLOTS], more + loaded_at[n])

        def slot(key):
            return ring[:, slot_of(key), :]

        def slot_kn(key):
            return slot(key).rearrange("p (k n) -> p k n", k=KD)

        T0 = tiles_of(0)
        rows_before = [0, 2 * T0 + (TT - T0)]
        proj = {}
        for l in range(LAYERS):
            for what in ("QA", "KV", "QW"):
                for t in range(TT if what == "KV" else tiles_of(l)):
                    proj[(l, what, t)] = len(proj)
        units = {}
        for l in range(LAYERS):
            for u in attention_units(l):
                units[(l, *u)] = len(units)
        groups = {}
        for l in range(LAYERS):
            for kind in range(2):
                for t in range(tiles_of(l)):
                    groups[(l, kind, t)] = len(groups)
        seqs = {}
        for l in range(LAYERS):
            for s in range(tiles_of(l) // 2):
                seqs[(l, s)] = len(seqs)

        def row_no(l, norm, t):
            return (0 if l == 0 else TT + T0) + (TT if norm else 0) + t

        def chunk_source(l, c):
            what = ("W1", "W3", "W2")[c // 8]
            return slot((l, what, 0))[:, CHUNK * (c % 8):CHUNK * (c % 8) + CHUNK]

        def gate_chunk(l, i, k):
            n = (len(GATE_GROUPS) * l + i) * KD + k
            b, g = GATE_GROUPS[i]
            return n, GW[l][(i * KD + k) % len(GW[l])], slot((l, "GATE", b, g))[:, CHUNK * k:CHUNK * k + CHUNK]

        def split_low(nc_engine, l, c):
            src, b = chunk_source(l, c), c % BUFS
            return nc_engine.tensor_tensor(WP[:, b, 1, :], src, WP[:, b, 0, :].bitcast(F32), ALU.subtract)

        def tok_no(l, t, half):
            return (0 if l == 0 else 2 * T0) + 2 * t + half

        def tile_no(l, t):
            return (0 if l == 0 else T0) + t

        def residual_no(l, half, t):
            return (0 if l == 0 else 2 * T0) + 2 * t + half

        def layer_rows(l):
            return [
                (PR[0:48, l, :], ada_b[l].rearrange("(k p) -> k p", p=P)),
                (PR[48:56, l, :], norm1_g[l].rearrange("(k p) -> k p", p=P)),
                (PR[56:64, l, :], norm2_g[l].rearrange("(k p) -> k p", p=P)),
                (PR[64:100, l, :], hy_short_w[l].rearrange("j (k p) -> (j k) p", p=P)),
                (PR[100:112, l, :], hy_short_b[l].rearrange("(k p) -> k p", p=P)),
                (PR[112:116, l, :], hy_bias[l].rearrange("(k p) -> k p", p=P)),
            ]

        def network(l):
            return [
                (FP[:, l, 0:1], hy_f_b1[l].rearrange("(p a) -> p a", a=1)),
                (FP[:, l, 1:2], hy_f_freq[l].rearrange("(p a) -> p a", a=1)),
                (FP[:, l, 2:3], hy_f_b2[l].rearrange("(p a) -> p a", a=1)),
                (FW[0:EMB, l, 0, :], hy_f_w1[l]),
                (FW[:, l, 1, :], hy_f_w2[l]),
            ]

        early = [(CR[0:8, :], c[0].rearrange("(k p) -> k p", p=P)),
                 (CR[8:16, :], c_ctx.rearrange("(k p) -> k p", p=P)),
                 (ident[:, :], k_ident)] + layer_rows(0)
        assert len(early) == EARLY

        block = stack.enter_context(nc.Block())

        @block.sync
        def _(sp):
            def source(key):
                l, what, j = key[:3]
                if what == "ADA":
                    return ada_w[l].rearrange("(k p) n -> p k n", p=P)[:, :, 512 * j:512 * j + 512]
                if what == "QA":
                    return w_in[l].rearrange("(k p) n -> p k n", p=P)[:, :, 0:512]
                if what == "QW":
                    return w_in[l].rearrange("(k p) n -> p k n", p=P)[:, :, 2304:2816]
                if what == "U":
                    return w_in[l].rearrange("(k p) n -> p k n", p=P)[:, :, 768 + 512 * j:1280 + 512 * j]
                if what == "GATE":
                    n0 = 3072 + D * j + 512 * key[3]
                    return w_in[l].rearrange("(k p) n -> p k n", p=P)[:, :, n0:n0 + 512]
                if what == "BR":
                    return w_branch[l, j].rearrange("(k p) n -> p k n", p=P)
                if what == "OUT":
                    return w_out[l].rearrange("(k p) n -> p k n", p=P)[:, :, 512 * j:512 * j + 512]

            def expert_source(l, what, e):
                w = {"W1": exp_w1, "W3": exp_w3, "W2": exp_w2}[what]
                return w[l, e].rearrange("(k p) n -> p k n", p=P)

            def wait_free(l, n, more=None):
                if n < SLOTS:
                    return
                key, last = loads[n - SLOTS]
                wait_full(sp, last)

            for dst, src in early:
                sp.dma_start(dst, src).then_inc(early_loaded, 16)
            for l in range(LAYERS):
                T = tiles_of(l)
                for n, (key, _) in enumerate(loads):
                    if key[0] != l or key[1] in ("W1", "W3", "W2"):
                        continue
                    if n >= SLOTS and loads[n - SLOTS][1] is None and loads[n - SLOTS][0][1] in ("W1", "W3", "W2"):
                        pk = loads[n - SLOTS][0]
                        if pk[1] == "W2":
                            wait_full_e(sp, (pk[0], "Y", 1), NEXP - 1)
                        else:
                            wait_full_e(sp, (pk[0], "H1" if pk[1] == "W1" else "H3"), NEXP - 1)
                    else:
                        wait_free(l, n)
                    if key[1] == "KV":
                        dst = slot(key).rearrange("p (k a n) -> p k a n", k=KD, a=2)
                        for a in range(2):
                            n0 = 512 + 2304 * a
                            src = w_in[l].rearrange("(k p) n -> p k n", p=P)[:, :, n0:n0 + 256]
                            sp.dma_start(dst[:, :, a, :], src).then_inc(slot_loaded[n % SLOTS], 16)
                        continue
                    kk = 4 if key[1] == "BR" else KD
                    sp.dma_start(slot(key).rearrange("p (k n) -> p k n", k=kk), source(key)) \
                        .then_inc(slot_loaded[n % SLOTS], 16)
                    if key[1:] == ("ADA", 2):
                        if l:
                            wait_full(sp, (l - 1, "SCL", tiles_of(l - 1) - 1, 1))
                        sp.dma_start(Z, k_z).then_inc(filter_loaded, 16)
                        sp.dma_start(W3, hy_f_w3[l]).then_inc(filter_loaded, 16)
                        sp.dma_start(DEC, k_decay.rearrange("(t p) h n -> p t h n", p=P)).then_inc(filter_loaded, 16)
                        if l == 0:
                            sp.dma_start(X[:, 0:2, :], x[0].rearrange("(t p) d -> p t d", p=P)).then_inc(x_loaded, 16)
                            sp.dma_start(X[:, 2:4, :], ctx_in[0].rearrange("(t p) d -> p t d", p=P)).then_inc(x_loaded, 16)
                for what in ("W1", "W3", "W2"):
                    n = load_no[(l, what, 0)]
                    wait_free(l, n)
                    kk = FE if what == "W2" else KD
                    sp.dma_start(slot((l, what, 0)).rearrange("p (k n) -> p k n", k=kk), expert_source(l, what, 0)) \
                        .then_inc(slot_loaded[n % SLOTS], 16)
                with sp.Fori(1, NEXP) as e:
                    for what in ("W1", "W3", "W2"):
                        n = load_no[(l, what, 0)]
                        wait_full_e(sp, (l, *{"W1": ("H1",), "W3": ("H3",), "W2": ("Y", 1)}[what]), e, back=1)
                        kk = FE if what == "W2" else KD
                        sp.dma_start(slot((l, what, 0)).rearrange("p (k n) -> p k n", k=kk),
                                     expert_source(l, what, e)).then_inc(slot_loaded[n % SLOTS], 16)
                sp.wait_ge(flag_ready, l + 1)
                over = sp.value_load(FLAG[0:1, 0:1], min_val=0, max_val=1)
                with sp.If(over > 0):
                    wait_full_e(sp, (l, "Y", 1), NEXP - 1)
                    for j, what in enumerate(("W1", "W3", "W2")):
                        kk = FE if what == "W2" else KD
                        sp.dma_start(ring[:, j, :].rearrange("p (k n) -> p k n", k=kk), expert_source(l, what, 0)) \
                            .then_inc(over_loaded[l][j], 16)
                    with sp.Fori(1, NEXP) as e:
                        for j, what in enumerate(("W1", "W3", "W2")):
                            b, n, per = over_bank(("Y", T - 1, 1) if what == "W2" else ("H3", FE - 1), T)
                            sp.wait_ge(over_full[l][b], e * per + (n + 1 - per))
                            kk = FE if what == "W2" else KD
                            sp.dma_start(ring[:, j, :].rearrange("p (k n) -> p k n", k=kk),
                                         expert_source(l, what, e)).then_inc(over_loaded[l][j], 16)
                    for key in (("H3", FE - 1), ("Y", T - 1, 1)):
                        b, n, per = over_bank(key, T)
                        sp.wait_ge(over_full[l][b], NEXP * per)
            for t in range(2):
                sp.wait_ge(experts_done, T0 + t + 1)
                sp.dma_start(out[0, t * P:(t + 1) * P, :], X[:, t, :]).then_inc(out_stored, 16)
            sp.wait_ge(out_stored, 32)

        @block.gpsimd
        def _(pool):
            link = chained(pool, pool_steps, [0])
            nc.gpsimd.memset(ones[:, :], 1.0).then_inc(ones_ready, 1)
            nc.gpsimd.memset(HALF[:, :], -0.5).then_inc(ones_ready, 1)
            pool.wait_ge(ones_ready, 2)
            late = [
                (DF[:, :, :], k_dft.rearrange("(t p) n -> p t n", p=P)),
                (ROPE[:, :, :, :], k_rope.rearrange("(t p) a n -> p t a n", p=P)),
            ]
            for l in range(LAYERS):
                late += [
                    (QKG[:, l, :, :], qk_g[l].partition_broadcast(P)),
                    (SINK[:, l, :], sinks[l].partition_broadcast(P)),
                    (RB[:, l, 0:4], router_g_b[l].partition_broadcast(P)),
                    (RB[:, l, 4:20], router_e_b[l].partition_broadcast(P)),
                    (RW[:, l, :, 0:4], router_g_w[l].rearrange("(k p) n -> p k n", p=P)),
                    (RW[:, l, :, 4:20], router_e_w[l].rearrange("(k p) n -> p k n", p=P)),
                ]
                if l:
                    late += layer_rows(l) + network(l)
            late += [
                (IF[:, :, :], k_idft.rearrange("(t p) n -> p t n", p=P)),
                (MASK[:, :, :], k_mask.rearrange("(t p) n -> p t n", p=P)),
                (FIRST[:, :], k_first.partition_broadcast(P)),
                (TRI[:, :], k_tri),
                (IOTA[:, :], k_iota.partition_broadcast(P)),
            ]
            assert len(late) == LATE
            for dst, src in late:
                pool.dma_start(dst, src).then_inc(params_loaded, 16)

            def rms_rows(l, norm):
                for t in range(TT if not norm else tiles_of(l)):
                    i = row_no(l, norm, t)
                    pool.wait_ge(squares, i + 1)
                    link(nc.gpsimd.tensor_scalar(ST[:, 8 + t:9 + t], ST[:, t:t + 1], 1.0 / D, EPS, ALU.mult, ALU.add))
                    link(nc.gpsimd.tensor_tensor(ST[:, 16 + t:17 + t], ST[:, 8 + t:9 + t], HALF[:, 0:1], ALU.pow),
                                rstd_ready, i + 1)

            def rms_heads(l, what, t):
                i = proj[(l, what, t)]
                pool.wait_ge(head_sums, i + 1)
                link(nc.gpsimd.tensor_scalar(HS[:, i % 2, 1, :], HS[:, i % 2, 0, :], 1.0 / HD, EPS, ALU.mult, ALU.add))
                link(nc.gpsimd.tensor_tensor(HS[:, i % 2, 2, :], HS[:, i % 2, 1, :], HALF[:, 0:HEADS], ALU.pow),
                            head_rstd, i + 1)

            for l in range(LAYERS):
                rms_rows(l, 0)
                for what in ("QA", "KV", "QW"):
                    for t in range(TT if what == "KV" else tiles_of(l)):
                        rms_heads(l, what, t)
                N = tiles_of(l) * P
                for k in range(KD):
                    pool.wait_ge(ht_high, KD * l + k + 1)
                    link(nc.gpsimd.tensor_tensor(HTP[l][1][:, k, :], HT[:, k, 0:N], HTP[l][0][:, k, :].bitcast(F32),
                                                 ALU.subtract), ht_low, KD * l + k + 1)
                for i in range(len(GATE_GROUPS)):
                    for k in range(KD):
                        n, dst, src = gate_chunk(l, i, k)
                        pool.wait_ge(gate_high, n + 1)
                        link(nc.gpsimd.tensor_tensor(dst[:, 1, :], src, dst[:, 0, :].bitcast(F32), ALU.subtract),
                             gate_low, n + 1)
                rms_rows(l, 1)
                for t in range(tiles_of(l)):
                    pool.wait_ge(tok_mid, tok_no(l, t, 0) + 1)
                    link(nc.gpsimd.tensor_tensor(TOK[2][:, t, 0:512], TOKR[:, t, 0:512], TOK[1][:, t, 0:512],
                                                 ALU.subtract), tok_low, tile_no(l, t) + 1)
                with pool.Fori(0, NEXP) as e:
                    for c in range(1, CHUNKS, 3):
                        pool.wait_ge(chunk_high, e * CHUNKS + (CHUNKS * NEXP * l + c + 1))
                        split_low(nc.gpsimd, l, c).then_inc(chunk_low_pool, 1)

        @block.scalar
        def _(act):
            link = chained(act, act_steps, [0])

            def read(ins, key, more=0):
                b, n = fill_at[key]
                link(ins, bank_free[b], more + n + 1)

            for dst, src in network(0):
                act.dma_start(dst, src).then_inc(network_loaded, 16)
            act.wait_ge(early_loaded, 16 * EARLY)
            link(nc.scalar.activation(CR[:, :], CR[:, :], ACT.Silu), cond_ready, 1)

            def norm_squares(l, norm):
                T = TT if not norm else tiles_of(l)
                for t in range(T):
                    if norm:
                        act.wait_ge(residual_added, residual_no(l, 1, t) + 1)
                    elif l:
                        act.wait_ge(experts_done, t + 1)
                    elif t == 0:
                        act.wait_ge(x_loaded, 32)
                    if norm and t == 0:
                        wait_full(act, (l, "BR", 2, KD - 1))
                    link(nc.scalar.activation(XN[:, t, :], X[:, t, :], ACT.Square, accum_out=ST[:, t:t + 1]),
                                squares, row_no(l, norm, t) + 1)

            def head_square(l, what, t):
                i = proj[(l, what, t)]
                key = (l, what, t)
                wait_full(act, key)
                if what == "KV":
                    b = bank(key)
                    for kind in range(2):
                        link(nc.scalar.copy(V[:, t, kind, :], b[:, 256 * kind + 128:256 * kind + 256]))
                if i >= 2:
                    act.wait_ge(head_sums, i - 1)
                link(nc.scalar.activation(TMP[:, i % 2, :], bank(key)[:, :], ACT.Square), head_squares, i + 1)

            def copy_out(dst, key, src=None):
                wait_full(act, key)
                read(nc.scalar.copy(dst, bank(key)[:, :] if src is None else src), key)

            def copy_gates(l, which):
                for s in range(tiles_of(l) // 2):
                    for half in range(2):
                        copy_out(GB[:, s, 512 * half:512 * half + 512], (l, "GB", which, s, half))

            act.sem_inc(chunk_used, 1)
            for l in range(LAYERS):
                T = tiles_of(l)
                N = T * P
                for j in range(12):
                    key = (l, "MOD", j)
                    wait_full(act, key)
                    src = bank(key)[:, 0:4 * WIDE].rearrange("p (m r s) -> p m r s", m=4, s=2)[:, :, 0, :]
                    read(nc.scalar.copy(MOD[:, 4 * j:4 * j + 4, :], src), key)
                    if j in FILTER_SLOTS[0:2]:
                        i = FILTER_SLOTS.index(j)
                        act.wait_ge(filter_arg, 2 * l + i + 1)
                        link(nc.scalar.activation(FT[:, 3 + i, :], FT[:, 1, :], ACT.Sin), filter_sin, 2 * l + i + 1)
                    if j == FILTER_SLOTS[2]:
                        for t in range(2):
                            for half in range(2):
                                wait_read(act, (l, "F3", t, half))
                                link(nc.scalar.activation(DEC[:, t, half, :], FH[:, t, half, :], ACT.Abs),
                                     filter_abs, 4 * l + 2 * t + half + 1)
                    if j == FILTER_SLOTS[3]:
                        norm_squares(l, 0)
                if l == 0:
                    act.wait_ge(params_loaded, 16 * LATE)
                for t in range(T):
                    head_square(l, "QA", t)
                for t in range(TT):
                    head_square(l, "KV", t)
                for t in range(T):
                    copy_out(QT[:, 0, :, t * P:(t + 1) * P], (l, "QAT", t),
                             bank((l, "QAT", t))[:, :].rearrange("p (c n) -> p c n", c=4))
                for t in range(T):
                    head_square(l, "QW", t)
                for t in range(TT):
                    copy_out(KT[:, :, t * P:(t + 1) * P], (l, "KVT", t),
                             bank((l, "KVT", t))[:, 0:256].rearrange("p (c n) -> p c n", c=2))
                for ch in range(12):
                    key = (l, "U", ch)
                    wait_full(act, key)
                    link(nc.scalar.activation(UC[:, ch, 0:N], bank(key)[:, 0:N], ACT.Identity,
                                                     bias=PC[:, 100 + ch:101 + ch], scale=PC[:, 76 + ch:77 + ch]),
                                conv_started, 12 * l + ch + 1)
                for t in range(T):
                    copy_out(QT[:, 1, :, t * P:(t + 1) * P], (l, "QWT", t),
                             bank((l, "QWT", t))[:, :].rearrange("p (c n) -> p c n", c=4))
                yat = {i: s for i, s in enumerate(attention_steps(l))}
                for i, s in yat.items():
                    if s[0] == "S":
                        _, kind, t, h = s
                        u = units[(l, kind, t, h)]
                        g = groups[(l, kind, t)]
                        key = (l, *s)
                        nk = len(keys_of(t)) * P
                        act.wait_ge(neg_max, u + 1)
                        if u >= 3:
                            prev = [k for k, v in units.items() if v == u - 3][0]
                            wait_full(act, (prev[0], "PT", *prev[1:]))
                        nm = NMX[:, u % 4:u % 4 + 1]
                        if kind:
                            link(nc.scalar.activation(AT[:, g % 2, 2, h:h + 1], SINK[:, l, h:h + 1], ACT.Exp, bias=nm))
                        read(nc.scalar.activation(PB[:, u % 3, 0:nk], bank(key)[:, 0:nk], ACT.Exp, bias=nm,
                                                  accum_out=AT[:, g % 2, 1, h:h + 1]), key)
                    elif s[0] == "YAT":
                        _, kind, t = s
                        copy_out(YT[:, kind, :, t * P:(t + 1) * P], (l, *s),
                                 bank((l, *s))[:, :].rearrange("p (c n) -> p c n", c=4))
                for t in range(T):
                    copy_out(VT[:, t, :], (l, "VT", t))
                copy_gates(l, 0)
                wait_full(act, (l, "INV", T // 2 - 1, CH - 1))
                for k in range(KD):
                    link(nc.scalar.copy(HTP[l][0][:, k, :], HT[:, k, 0:N]), ht_high, KD * l + k + 1)
                for j, (b, g) in enumerate(GATE_GROUPS):
                    for k in range(KD):
                        n, dst, src = gate_chunk(l, j, k)
                        if k == 0:
                            wait_slot(act, (l, "GATE", b, g))
                        before = j * KD + k - len(GW[l])
                        if before >= 0:
                            bj, bk = before // KD, before % KD
                            if bk == KD - 1:
                                wait_full(act, (l, "GATE", GATE_GROUPS[bj][0], 4 * GATE_GROUPS[bj][1] + 3))
                            else:
                                act.wait_ge(gate_used, (KD - 1) * (len(GATE_GROUPS) * l + bj) + bk + 1)
                        link(nc.scalar.copy(dst[:, 0, :], src), gate_high, n + 1)
                    for ch in range(4 * g, 4 * g + 4):
                        key = (l, "GATE", b, ch)
                        i = 4 * j + ch % 4 - 2
                        wait_full(act, key)
                        if i >= 0:
                            wait_read(act, (l, "BR", (1, 0, 2)[i // KD], i % KD))
                        read(nc.scalar.activation(TMP[:, ch % 2, 0:N], bank(key)[:, 0:N], ACT.Sigmoid), key)
                norm_squares(l, 1)
                copy_gates(l, 1)
                for t in range(T):
                    for half in range(2):
                        key = (l, "TK", t, half)
                        wait_full(act, key)
                        link(nc.scalar.copy(TOK[0][:, t, 512 * half:512 * half + 512], bank(key)[:, :]),
                             tok_high, tok_no(l, t, half) + 1)
                act.wait_ge(logits_ready, l + 1)
                link(nc.scalar.activation(RT[:, 1, 0:T, 0:5], RT[:, 0, 0:T, 0:5], ACT.Exp), logits_exp, l + 1)
                for t in range(T):
                    for half in range(2):
                        cols = slice(512 * half, 512 * half + 512)
                        wait_read(act, (l, "TK", t, half))
                        link(nc.scalar.copy(TOK[1][:, t, cols], TOKR[:, t, cols]), tok_mid, tok_no(l, t, half) + 1)
                C = CAP[l]
                for half in range(2):
                    key = (l, "GA0", half)
                    wait_full(act, key)
                    link(nc.scalar.copy(XGP[0][:, 4 * half:4 * half + 4, 0:C],
                                        bank(key)[:, 0:4 * C].rearrange("p (k n) -> p k n", k=4)),
                         x_rounded, (2 * NEXP + 2) * l + half + 1)

                def high(chunk, e, ahead):
                    if chunk % 8 == 0:
                        n = load_no[(l, ("W1", "W3", "W2")[chunk // 8], 0)]
                        act.wait_ge(slot_loaded[n % SLOTS], e * 16 + (16 * ahead + loaded_at[n]))
                    before = (chunk - BUFS) % CHUNKS
                    back = int(chunk < BUFS)
                    if before in ENDS:
                        wait_full_e(act, (l, *ENDS[before]), e, back=back - ahead)
                    else:
                        used = 0 if back else used_count(before)
                        act.wait_ge(chunk_used, e * USED + (USED * (NEXP * l + ahead) + 1 + used))
                    nc.scalar.copy(WP[:, chunk % BUFS, 0, :], chunk_source(l, chunk)).then_inc(chunk_high, 1)

                def round_rows(half, e):
                    key = (l, "GA", half)
                    wait_full_e(act, key, e)
                    nc.scalar.copy(XGP[0][:, 4 * half:4 * half + 4, 0:C],
                                   bank(key)[:, 0:4 * C].rearrange("p (k n) -> p k n", k=4)).then_inc(x_rounded, 1)

                def round_outputs(e, back):
                    for half in range(2):
                        wait_full_e(act, (l, "Y", half), e, back=back)
                        nc.scalar.copy(YP[0][0:C, 512 * half:512 * half + 512], bank((l, "Y", half))[0:C, :]) \
                            .then_inc(y_rounded, 1)

                def first_half(e, ahead):
                    for chunk in range(CHUNKS // 2):
                        high(chunk, e, ahead)
                        if chunk == BUFS - 1:
                            round_outputs(e, 1 - ahead)

                def second_half(e):
                    wait_full_e(act, (l, "H1"), e)
                    wait_read_e(act, (l, "H3"), e, back=1)
                    nc.scalar.activation(TMP[0:C, 0, :], bank((l, "H1"))[0:C, :], ACT.Silu) \
                        .then_inc(bank_free[fill_at[(l, "H1")][0]], 1)
                    for chunk in range(CHUNKS // 2, CHUNKS):
                        high(chunk, e, 0)
                        if chunk == 19:
                            round_rows(0, e)
                            key = (l, "GT")
                            wait_full_e(act, key, e)
                            nc.scalar.copy(GTP[0][:, :, 0:C],
                                           bank(key)[:, 0:4 * C].rearrange("p (k n) -> p k n", k=4)) \
                                .then_inc(g_rounded, 1)
                            round_rows(1, e)

                act.wait_ge(flag_ready, l + 1)
                first_half(0, 0)
                with act.Fori(0, NEXP - 1) as e:
                    second_half(e)
                    first_half(e, 1)
                second_half(NEXP - 1)
                round_outputs(NEXP - 1, 0)
                act.wait_ge(flag_ready, l + 1)
                over = act.value_load(FLAG[0:1, 0:1], min_val=0, max_val=1)
                with act.If(over > 0):
                    with act.Fori(0, NEXP) as e:
                        for i in range(FE):
                            b, n, per = over_bank(("H1", i), T)
                            act.wait_ge(over_full[l][b], e * per + (n + 1))
                            b2, n2, _ = over_bank(("H3", (i - 2) % FE), T)
                            act.wait_ge(over_free[l][b2], e * per + (n2 + 2 - (per if i < 2 else 0)))
                            nc.scalar.activation(TMP[:, i % 2, 0:N], ps[b][:, 0:N], ACT.Silu) \
                                .then_inc(over_free[l][b], 1)
                    act.wait_ge(over_free[l][over_bank(("H3", FE - 1), T)[0]], NEXP * 2 + 1)

        @block.vector
        def _(dve):
            steps = [0]
            link = chained(dve, dve_steps, steps)
            tt, ts, stt = nc.vector.tensor_tensor, nc.vector.tensor_scalar, nc.vector.scalar_tensor_tensor

            def read(ins, key, more=0):
                b, n = fill_at[key]
                link(ins, bank_free[b], more + n + 1)

            def normalise_rows(l, norm):
                for t in range(TT if not norm else tiles_of(l)):
                    i = row_no(l, norm, t)
                    dve.wait_ge(rstd_ready, i + 1)
                    link(ts(XN[:, t, :], X[:, t, :], ST[:, 16 + t:17 + t], None, ALU.mult), rows_ready, i + 1)

            def modulate(l, norm):
                T = TT if not norm else tiles_of(l)
                for k in range(KD):
                    key = (l, "N2" if norm else "N1", k)
                    wait_full(dve, key)
                    for s in range(T // 2):
                        ins = ts(HT[:, k, SEQ * s:SEQ * s + SEQ], bank(key)[:, SEQ * s:SEQ * s + SEQ],
                                 AM[:, norm, k, s:s + 1], MOD[:, (24 if norm else 0) + k, s:s + 1], ALU.mult, ALU.add)
                        if s == T // 2 - 1:
                            read(ins, key)
                        else:
                            link(ins)

            def head_sum(l, what, t):
                i = proj[(l, what, t)]
                dve.wait_ge(head_squares, i + 1)
                sq = TMP[:, i % 2, :]
                if what == "KV":
                    sq = sq.rearrange("p (a n) -> p a n", a=2)[:, :, 0:P].rearrange("p a (h d) -> p a h d", d=HD)
                    dst = HS[:, i % 2, 0, 0:4].rearrange("p (a h) -> p a h", a=2)
                    link(nc.vector.memset(HS[:, i % 2, 0, 4:8], 1.0))
                else:
                    sq = sq.rearrange("p (h d) -> p h d", d=HD)
                    dst = HS[:, i % 2, 0, :]
                link(nc.vector.tensor_reduce(dst, sq, AX_X, ALU.add), head_sums, i + 1)

            def head_norm(l, what, t):
                i = proj[(l, what, t)]
                key = (l, what, t)
                dve.wait_ge(head_rstd, i + 1)
                if what == "QW":
                    wait_full(dve, (l, "QAT", t))
                rot = t < 2
                tile = t if rot else 2
                if what == "KV":
                    src = bank(key)[:, :].rearrange("p (a n) -> p a n", a=2)[:, :, 0:P] \
                        .rearrange("p a (h d) -> p a h d", d=HD)
                    rs = HS[:, i % 2, 2, 0:4].rearrange("p (a h) -> p a h", a=2).unsqueeze(3) \
                        .to_broadcast([P, 2, 2, HD])
                    mid = TMP[:, 2, 0:256].rearrange("p (a h d) -> p a h d", a=2, d=HD)
                    dst = KN[:, t, :].rearrange("p (a h d) -> p a h d", a=2, d=HD)
                    read(tt(mid, src, rs, ALU.mult), key)
                    for a in range(2):
                        rotate(dst[:, a], mid[:, a], tile, 2 + a, 2, rot, i + 1 if a else None)
                else:
                    src = bank(key)[:, :].rearrange("p (h d) -> p h d", d=HD)
                    rs = HS[:, i % 2, 2, :].unsqueeze(2).to_broadcast([P, HEADS, HD])
                    mid = TMP[:, 2, :].rearrange("p (h d) -> p h d", d=HD)
                    dst = QN[:, t, :].rearrange("p (r g d) -> p g r d", g=2, d=HD)
                    read(tt(mid, src, rs, ALU.mult), key)
                    rotate(dst, mid, tile, 0 if what == "QA" else 1, HEADS, rot, i + 1)

            def rotate(dst, mid, tile, kind, nh, rot, done):
                cg = CG[:, tile, kind, :].unsqueeze(1)
                if nh == HEADS:
                    def by_pair(a):
                        return a.rearrange("p (g r) d -> p g r d", g=2)

                    ins = tt(dst, by_pair(mid), cg.unsqueeze(1).to_broadcast([P, 2, 4, HD]), ALU.mult)
                else:
                    def by_pair(a):
                        return a

                    ins = tt(dst, mid, cg.to_broadcast([P, nh, HD]), ALU.mult)
                if not rot and done:
                    link(ins, qk_ready, done)
                else:
                    link(ins)
                if rot:
                    tmp = TMP[:, 3, 0:nh * HD].rearrange("p (h a b f) -> p h a b f", a=2, b=2, f=16)
                    m5 = mid.rearrange("p h (a b f) -> p h a b f", a=2, b=2)
                    sg = SG[:, tile, kind, :].rearrange("p (a b f) -> p a b f", a=2, b=2)
                    for b in range(2):
                        s1 = sg[:, :, b, :].unsqueeze(1).to_broadcast([P, nh, 2, 16])
                        link(tt(tmp[:, :, :, b, :], m5[:, :, :, 1 - b, :], s1, ALU.mult))
                    ins = tt(dst, dst, by_pair(TMP[:, 3, 0:nh * HD].rearrange("p (h d) -> p h d", d=HD)), ALU.add)
                    if done:
                        link(ins, qk_ready, done)
                    else:
                        link(ins)

            dve.wait_ge(early_loaded, 16 * EARLY)
            for l in range(LAYERS):
                T = tiles_of(l)
                N = T * P
                wait_full(dve, (l, "PR"))
                read(nc.vector.tensor_copy(PC[:, :], bank((l, "PR"))[:, 0:116]), (l, "PR"))
                if l == 0:
                    wait_full(dve, (l, "C"))
                    read(nc.vector.tensor_copy(CC[:, :], bank((l, "C"))[:, 0:16]), (l, "C"))
                for i in range(2):
                    key = (l, f"F{i + 1}")
                    wait_full(dve, key)
                    if l == 0 and i == 0:
                        dve.wait_ge(network_loaded, 80)
                    read(ts(FT[:, 0, :], bank(key)[0:HID, 0:SEQ], FP[:, l, 2 * i:2 * i + 1], FP[:, l, 1:2],
                            ALU.add, ALU.mult), key)
                    link(ts(FT[:, 1, :], FT[:, 0, :], 1.0 / (2 * np.pi), MAGIC, ALU.mult, ALU.add))
                    link(ts(FT[:, 2, :], FT[:, 1, :], -MAGIC, None, ALU.add))
                    for part in TWO_PI:
                        link(stt(FT[:, 0, :], FT[:, 2, :], -part, FT[:, 0, :], ALU.mult, ALU.add))
                    link(ts(FT[:, 1, :], FT[:, 0, :], PI_MAX, -PI_MAX, ALU.min, ALU.max),
                                filter_arg, 2 * l + i + 1)
                    dve.wait_ge(filter_sin, 2 * l + i + 1)
                for t in range(2):
                    for half in range(2):
                        key = (l, "F3", t, half)
                        wait_full(dve, key)
                        if t == 0 and half == 0:
                            dve.wait_ge(filter_loaded, 48 * (l + 1))
                        read(tt(FH[:, t, half, :], bank(key)[:, :], DEC[:, t, half, :], ALU.mult), key)
                for t in range(2):
                    link(tt(FAB[:, t, 0, :], FH[:, t, 0, :], FH[:, t, 1, :], ALU.add))
                    link(tt(FAB[:, t, 1, :], FH[:, t, 0, :], FH[:, t, 1, :], ALU.subtract),
                                filter_ab, 2 * l + t + 1)
                wait_full(dve, (l, "FN"))
                read(nc.vector.reciprocal(FN, bank((l, "FN"))[:, :]), (l, "FN"))
                for m in range(5):
                    key = (l, "FK", m)
                    wait_full(dve, key)
                    read(tt(KS[:, m, :], bank(key)[:, :], FN, ALU.mult), key)
                if l == 0:
                    link(nc.vector.tensor_copy(ident_b[:, :], ident[:, :]))
                    dve.wait_ge(params_loaded, 16 * LATE)
                    link(ts(NSINK[:, :, :], SINK[:, :, :], -1.0, None, ALU.mult))
                for kind, row in enumerate((0, 2, 1, 3)):
                    g = QKG[:, l, row, :]
                    scale = HD ** -0.5 if kind < 2 else 1.0
                    link(ts(CG[:, 2, kind, :], g, scale, None, ALU.mult))
                for tile in range(2):
                    link(tt(CG[:, tile, :, :], CG[:, 2, :, :],
                            ROPE[:, tile, 0, :].unsqueeze(1).to_broadcast([P, 4, HD]), ALU.mult))
                    gg = CG[:, 2, :, :].rearrange("p k (a b f) -> p k a b f", a=2, b=2)
                    so = SG[:, tile, :, :].rearrange("p k (a b f) -> p k a b f", a=2, b=2)
                    sn = ROPE[:, tile, 1, :].rearrange("p (a b f) -> p a b f", a=2, b=2)
                    for b in range(2):
                        link(tt(so[:, :, :, b, :], gg[:, :, :, 1 - b, :],
                                sn[:, :, b, :].unsqueeze(1).to_broadcast([P, 4, 2, 16]), ALU.mult))
                normalise_rows(l, 0)
                wait_read(dve, (l, "MOD", 11))
                link(tt(MOD[:, :, :], MOD[:, :, :], PC[:, 0:48].unsqueeze(2).to_broadcast([P, 48, 2]), ALU.add))
                for norm in range(2):
                    m0 = 24 * norm + 8
                    link(ts(AM[:, norm, :, :], MOD[:, m0:m0 + 8, :], 1.0, None, ALU.add))
                    ins = tt(AM[:, norm, :, :], AM[:, norm, :, :],
                             PC[:, 48 + 8 * norm:56 + 8 * norm].unsqueeze(2).to_broadcast([P, KD, 2]), ALU.mult)
                    if norm:
                        link(ins, mod_ready, l + 1)
                    else:
                        link(ins)
                modulate(l, 0)
                order = [("QA", t) for t in range(T)] + [("KV", t) for t in range(TT)] + [("QW", t) for t in range(T)]
                head_sum(l, *order[0])
                for i, (what, t) in enumerate(order):
                    if i + 1 < len(order) and order[i + 1][0] == what:
                        head_sum(l, *order[i + 1])
                    head_norm(l, what, t)
                    if i + 1 < len(order) and order[i + 1][0] != what:
                        head_sum(l, *order[i + 1])
                S2 = T // 2
                for ch in range(12):
                    key = (l, "U", ch)
                    dve.wait_ge(conv_started, 12 * l + ch + 1)
                    src = bank(key)[:, 0:N].rearrange("p (s n) -> p s n", s=S2)
                    dst = UC[:, ch, 0:N].rearrange("p (s n) -> p s n", s=S2)
                    link(stt(dst[:, :, 1:SEQ], src[:, :, 0:SEQ - 1], PC[:, 64 + ch:65 + ch], dst[:, :, 1:SEQ],
                             ALU.mult, ALU.add))
                    read(stt(dst[:, :, 0:SEQ - 1], src[:, :, 1:SEQ], PC[:, 88 + ch:89 + ch], dst[:, :, 0:SEQ - 1],
                             ALU.mult, ALU.add), key)
                link(tt(UC[:, 8:12, 0:N], UC[:, 8:12, 0:N], UC[:, 4:8, 0:N], ALU.mult), gated_v, l + 1)
                for s in attention_steps(l):
                    if s[0] == "S":
                        _, kind, t, h = s
                        u = units[(l, kind, t, h)]
                        key = (l, *s)
                        nk = len(keys_of(t)) * P
                        wait_full(dve, key)
                        if kind and t < 2:
                            link(tt(bank(key)[:, 0:SEQ], bank(key)[:, 0:SEQ], MASK[:, t, :], ALU.add))
                        nm = NMX[:, u % 4:u % 4 + 1]
                        if u >= 4:
                            prev = [k for k, v in units.items() if v == u - 4][0]
                            wait_read(dve, (prev[0], "S", *prev[1:]))
                        if kind:
                            link(nc.vector.tensor_reduce(nm, bank(key)[:, 0:nk], AX_X, ALU.max, negate=True))
                            link(ts(nm, nm, NSINK[:, l, h:h + 1], None, ALU.min), neg_max, u + 1)
                        else:
                            link(nc.vector.tensor_reduce(nm, bank(key)[:, 0:nk], AX_X, ALU.max, negate=True),
                                        neg_max, u + 1)
                    elif s[0] == "PT":
                        _, kind, t, h = s
                        u = units[(l, kind, t, h)]
                        nk = len(keys_of(t)) * P
                        key = (l, *s)
                        wait_full(dve, key)
                        read(nc.vector.tensor_copy(PTB[:, u % 3, 0:nk], bank(key)[:, 0:nk]), key)
                    elif s[0] == "O" and s[3] % 4 == 3:
                        _, kind, t, h = s
                        g = groups[(l, kind, t)]
                        kv = h // 4
                        four = slice(4 * kv, 4 * kv + 4)
                        key = (l, "O", kind, t, kv)
                        wait_full(dve, key)
                        tot = AT[:, g % 2, 1, four]
                        if kind:
                            link(tt(AT[:, g % 2, 3, four], tot, AT[:, g % 2, 2, four], ALU.add))
                            tot = AT[:, g % 2, 3, four]
                        link(nc.vector.reciprocal(AT[:, g % 2, 4, four], tot))
                        if g >= 2 and kv == 0:
                            prev = [k for k, v in groups.items() if v == g - 2][0]
                            wait_full(dve, (prev[0], "YAT", *prev[1:]))
                        src = bank(key)[:, :].rearrange("p (h a d) -> p h a d", a=2, d=HD)[:, :, kv, :]
                        read(tt(YA[:, g % 2, 256 * kv:256 * kv + 256].rearrange("p (h d) -> p h d", d=HD), src,
                                AT[:, g % 2, 4, four].unsqueeze(2).to_broadcast([P, 4, HD]), ALU.mult), key)
                for s in range(T // 2):
                    for p in range(2):
                        kr, ki = (l, "DFT", s, 0, p), (l, "DFT", s, 1, p)
                        wait_full(dve, kr)
                        wait_full(dve, ki)
                        vr, vi = bank(kr)[:, :], bank(ki)[:, :]
                        Kr, Ki = KS[:, p, :], KS[:, 3 + p, :]
                        KrN = KS[:, 2, :] if p == 0 else Kr
                        link(tt(TMP[:, 0, :], vr, Kr, ALU.mult))
                        link(tt(TMP[:, 1, :], vi, Ki, ALU.mult))
                        read(tt(TMP[:, 2, :], vr, Ki, ALU.mult), kr)
                        read(tt(TMP[:, 3, :], vi, KrN, ALU.mult), ki)
                        link(tt(YS[:, s, p, :], TMP[:, 0, :], TMP[:, 1, :], ALU.subtract))
                        link(tt(YS[:, s, 2 + p, :], TMP[:, 2, :], TMP[:, 3, :], ALU.add),
                                    spec_ready, 2 * seqs[(l, s)] + p + 1)
                for s in range(T // 2):
                    for ch in range(CH):
                        key = (l, "INV", s, ch)
                        wait_full(dve, key)
                        cols = slice(SEQ * s, SEQ * s + SEQ)
                        read(stt(TMP[:, ch % 2, 0:SEQ], UC[:, 8 + ch, cols], PC[:, 112 + ch:113 + ch],
                                 bank(key)[:, 0:SEQ], ALU.mult, ALU.add), key)
                        link(tt(UC[:, ch, cols], UC[:, ch, cols], TMP[:, ch % 2, 0:SEQ], ALU.mult),
                                    yh_ready, CH * seqs[(l, s)] + ch + 1)
                for j, b in enumerate((1, 0, 2)):
                    for ch in range(KD):
                        gate, br = (l, "GATE", b, ch), (l, "BR", b, ch)
                        wait_full(dve, br)
                        wait_read(dve, gate)
                        if j == 0:
                            read(tt(MT[:, ch, 0:N], TMP[:, ch % 2, 0:N], bank(br)[:, 0:N], ALU.mult), br)
                        else:
                            read(tt(TMP[:, 2 + ch % 2, 0:N], TMP[:, ch % 2, 0:N], bank(br)[:, 0:N], ALU.mult), br)
                            ins = tt(MT[:, ch, 0:N], MT[:, ch, 0:N], TMP[:, 2 + ch % 2, 0:N], ALU.add)
                            if j == 2:
                                link(ins, merged, KD * l + ch + 1)
                            else:
                                link(ins)
                for t in range(T):
                    for half in range(2):
                        cols = slice(512 * half, 512 * half + 512)
                        key = (l, "OUT", half, t)
                        wait_full(dve, key)
                        if half == 0 and t == 0:
                            wait_read(dve, (l, "GB", 0, T // 2 - 1, 1))
                        read(tt(TMP[:, 2 + half, :], bank(key)[:, :], GB[:, t // 2, cols], ALU.mult), key)
                        link(tt(X[:, t, cols], X[:, t, cols], TMP[:, 2 + half, :], ALU.add),
                                    residual_added, residual_no(l, half, t) + 1)
                normalise_rows(l, 1)
                modulate(l, 1)
                for t in range(T):
                    key = (l, "LG", t)
                    wait_full(dve, key)
                    link(tt(RT[:, 2, t, 0:4], bank(key)[:, 0:4], RB[:, l, 0:4], ALU.add))
                    read(tt(RT[:, 3, t, :], bank(key)[:, 4:20], RB[:, l, 4:20], ALU.add), key)

                gl, le = RT[:, 2, 0:T, 0:4], RT[:, 3, 0:T, :]
                mx = RT[:, 4, 0:T, 0:1]
                fg = FIRST[:, 0:4].unsqueeze(1).to_broadcast([P, T, 4])
                fe = FIRST[:, 4:20].unsqueeze(1).to_broadcast([P, T, NEXP])

                def red(dst, src):
                    link(nc.vector.tensor_reduce(dst, src, AX_X, ALU.max))

                def op(dst, a, b, alu):
                    link(tt(dst, a, b, alu))

                def first_of_max(dst, src, best, weights, n):
                    op(dst, src, best.to_broadcast([P, T, n]), ALU.is_equal)
                    op(dst, dst, weights, ALU.mult)
                    red(RT[:, 11, 0:T, 0:1], dst)
                    op(dst, dst, RT[:, 11, 0:T, 0:1].to_broadcast([P, T, n]), ALU.is_equal)

                red(mx, gl)
                op(RT[:, 0, 0:T, 0:4], gl, mx.to_broadcast([P, T, 4]), ALU.subtract)
                og = RT[:, 5, 0:T, 0:4]
                first_of_max(og, gl, mx, fg, 4)
                for e4 in range(4):
                    link(nc.vector.tensor_copy(RT[:, 6, 0:T, e4:NEXP:4], og))
                op(le, le, RT[:, 6, 0:T, :], ALU.mult)
                link(ts(RT[:, 6, 0:T, :], RT[:, 6, 0:T, :], BIG, -BIG, ALU.mult, ALU.add))
                op(le, le, RT[:, 6, 0:T, :], ALU.add)
                m1, m2 = RT[:, 4, 0:T, 1:2], RT[:, 4, 0:T, 2:3]
                e1, e2, sel = RT[:, 7, 0:T, :], RT[:, 8, 0:T, :], RT[:, 9, 0:T, :]
                red(m1, le)
                first_of_max(e1, le, m1, fe, NEXP)
                link(ts(RT[:, 6, 0:T, :], e1, -3 * BIG, None, ALU.mult))
                op(le, le, RT[:, 6, 0:T, :], ALU.add)
                red(m2, le)
                first_of_max(e2, le, m2, fe, NEXP)
                link(tt(sel, e1, e2, ALU.add), sel_ready, l + 1)
                link(tt(RT[:, 0, 0:T, 4:5], m2, m1, ALU.subtract), logits_ready, l + 1)
                for t in range(T):
                    for half in range(2):
                        key = (l, "TK", t, half)
                        cols = slice(512 * half, 512 * half + 512)
                        dve.wait_ge(tok_high, tok_no(l, t, half) + 1)
                        read(tt(TOKR[:, t, cols], bank(key)[:, :], TOK[0][:, t, cols], ALU.subtract), key)
                dve.wait_ge(logits_exp, l + 1)
                sg_, r2, r1 = RT[:, 4, 0:T, 3:4], RT[:, 4, 0:T, 4:5], RT[:, 4, 0:T, 5:6]
                link(nc.vector.tensor_reduce(sg_, RT[:, 1, 0:T, 0:4], AX_X, ALU.add))
                link(ts(r1, RT[:, 1, 0:T, 4:5], 1.0, None, ALU.add))
                op(r1, r1, sg_, ALU.mult)
                link(nc.vector.reciprocal(r1, r1))
                op(r2, r1, RT[:, 1, 0:T, 4:5], ALU.mult)
                op(e1, e1, r1.to_broadcast([P, T, NEXP]), ALU.mult)
                op(e2, e2, r2.to_broadcast([P, T, NEXP]), ALU.mult)
                link(tt(CMB[:, 0:T, :], e1, e2, ALU.add))
                C = CAP[l]
                link(nc.vector.memset(CMBX[:, :, 0:1], 0.0))
                link(nc.vector.memset(POS[:, :, NEXP:NEXP + 1], -1.0))
                link(nc.vector.tensor_copy(CMBX[:, 0:T, 1:NEXP + 1], CMB[:, 0:T, :]))
                key = (l, "RANK")
                wait_full(dve, key)
                rank = bank(key)[:, 0:T * WIDE].rearrange("p (t n) -> p t n", t=T)[:, :, 0:NEXP]
                rk, far = RT[:, 10, 0:T, :], RT[:, 6, 0:T, :]
                link(ts(rk, rank, 1.0, None, ALU.add))
                link(nc.vector.tensor_reduce(ST[:, 40:41], bank(key)[:, T * WIDE:T * WIDE + NEXP], AX_X, ALU.max))
                read(ts(far, rank, float(C), None, ALU.is_ge), key)
                link(tt(rk, rk, sel, ALU.mult))
                link(ts(POS[:, 0:T, 0:NEXP], rk, -1.0, None, ALU.add))
                link(tt(CMB[:, 0:T, :], CMB[:, 0:T, :], far, ALU.mult))
                link(ts(FLAG[:, :], ST[:, 40:41], float(C), None, ALU.is_gt), flag_ready, l + 1)
                zeros = TMP[:, 0, :]
                link(nc.vector.memset(zeros, 0.0))
                for part in YP:
                    for half in range(2):
                        link(ts(part[:, 512 * half:512 * half + 512], zeros, 0.0, None, ALU.add))
                link(ts(STB[:, 0:N], zeros[:, 0:N], 0.0, None, ALU.add))
                places = (NEXP + 1) * l
                for t in range(T):
                    ins = ts(S[:, t, 0:C], IOTA[:, 0:C], POS[:, t, 0:1], None, ALU.is_equal)
                    if t < T - 1:
                        link(ins)
                    else:
                        link(ins, places_ready, places + 1)
                for t in range(T):
                    dve.wait_ge(tok_mid, tok_no(l, t, 1) + 1)
                    link(tt(TOK[2][:, t, 512:D], TOKR[:, t, 512:D], TOK[1][:, t, 512:D], ALU.subtract),
                         tok_low_dve, tile_no(l, t) + 1)
                dve.wait_ge(tok_low, tile_no(l, T - 1) + 1)
                link(nc.vector.memset(FACC[:, 0:T, :], 0.0))
                nx, ny = (2 * NEXP + 2) * l, (2 * NEXP + 2) * l

                def rows_low(key, n):
                    k0 = 4 * key[2]
                    dve.wait_ge(x_rounded, n)
                    return tt(XGP[1][:, k0:k0 + 4, 0:C], bank(key)[:, 0:4 * C].rearrange("p (k n) -> p k n", k=4),
                              XGP[0][:, k0:k0 + 4, 0:C].bitcast(F32), ALU.subtract)

                def low(c, e):
                    dve.wait_ge(chunk_high, e * CHUNKS + (CHUNKS * NEXP * l + c + 1))
                    split_low(nc.vector, l, c).then_inc(chunk_low, 1)

                def outputs_low(half):
                    cols = slice(512 * half, 512 * half + 512)
                    return tt(YP[1][0:C, cols], bank((l, "Y", half))[0:C, :], YP[0][0:C, cols].bitcast(F32),
                              ALU.subtract)

                for half in range(2):
                    read(rows_low((l, "GA0", half), nx + half + 1), (l, "GA0", half))
                base = steps[0]
                with dve.Fori(0, NEXP) as e:
                    for c in (0, 2, 3):
                        low(c, e)
                    for half in range(2):
                        dve.wait_ge(y_rounded, 2 * e + (ny + half + 1))
                        outputs_low(half).then_inc(bank_free[fill_at[(l, "Y", half)][0]], 1)
                    nc.vector.tensor_copy(CE[:, 0:T], CMBX[:, 0:T, bass.ds(e, 1)].rearrange("p t a -> p (t a)")) \
                        .then_inc(dve_steps, 1)
                    dve.wait_ge(dve_steps, 2 * e + (base + 1))
                    scatters = [(t, half) for t in range(T) for half in range(2)]
                    for c in range(BUFS, CHUNKS):
                        if not by_pool(c):
                            low(c, e)
                        if c - 2 in SCATTER_AFTER[0:2 * T]:
                            t, half = scatters[SCATTER_AFTER.index(c - 2)]
                            key = (l, "SC", t, half)
                            wait_full_e(dve, key, e)
                            cols = slice(512 * half, 512 * half + 512)
                            stt(FACC[:, t, cols], bank(key)[:, :], CE[:, t:t + 1], FACC[:, t, cols],
                                ALU.mult, ALU.add).then_inc(bank_free[fill_at[key][0]], 1)
                        if c == 7:
                            nc.vector.tensor_copy(PCOL[:, 0:T],
                                                  POS[:, 0:T, bass.ds(e + 1, 1)].rearrange("p t a -> p (t a)")) \
                                .then_inc(dve_steps, 1)
                            dve.wait_ge(dve_steps, 2 * e + (base + 2))
                            wait_full_e(dve, (l, "ST"), e)
                            for t in range(T):
                                ins = ts(S[:, t, 0:C], IOTA[:, 0:C], PCOL[:, t:t + 1], None, ALU.is_equal)
                            ins.then_inc(places_ready, 1)
                        if c == 16:
                            key = (l, "ST")
                            wait_full_e(dve, (l, "SC", T - 1, 1), e)
                            nc.vector.tensor_copy(STB[0:C, 0:N], bank(key)[0:C, 0:N]) \
                                .then_inc(bank_free[fill_at[key][0]], 1)
                        if c == 17:
                            key = (l, "H3")
                            wait_full_e(dve, key, e)
                            wait_read_e(dve, (l, "H1"), e)
                            tt(GM[0:C, :], TMP[0:C, 0, :], bank(key)[0:C, :], ALU.mult) \
                                .then_inc(bank_free[fill_at[key][0]], 1)
                        if c == 19:
                            key = (l, "GA", 0)
                            rows_low(key, 2 * e + (nx + 3)).then_inc(bank_free[fill_at[key][0]], 1)
                            key = (l, "GT")
                            dve.wait_ge(g_rounded, e + (NEXP * l + 1))
                            tt(GTP[1][:, :, 0:C], bank(key)[:, 0:4 * C].rearrange("p (k n) -> p k n", k=4),
                               GTP[0][:, :, 0:C].bitcast(F32), ALU.subtract).then_inc(bank_free[fill_at[key][0]], 1)
                            key = (l, "GA", 1)
                            rows_low(key, 2 * e + (nx + 4)).then_inc(bank_free[fill_at[key][0]], 1)
                steps[0] = base + 2 * NEXP
                wait_read_e(dve, (l, "GA", 1), NEXP - 1)
                dve.wait_ge(chunk_low, split_count(CHUNKS - 1)[0] * NEXP * (l + 1))
                for half in range(2):
                    key = (l, "Y", half)
                    dve.wait_ge(y_rounded, 2 * NEXP + (ny + half + 1))
                    b, n = fill_at[key]
                    link(outputs_low(half), bank_free[b], turn(key, NEXP - 1, n + 1))
                link(nc.vector.tensor_copy(CE[:, 0:T], CMBX[:, 0:T, NEXP]))
                for t in range(T):
                    for half in range(2):
                        key = (l, "SCL", t, half)
                        wait_full(dve, key)
                        cols = slice(512 * half, 512 * half + 512)
                        read(stt(FACC[:, t, cols], bank(key)[:, :], CE[:, t:t + 1], FACC[:, t, cols],
                                 ALU.mult, ALU.add), key)
                over = dve.value_load(FLAG[0:1, 0:1], min_val=0, max_val=1)
                with dve.If(over > 0):
                    for b in range(8):
                        dve.sem_inc(over_free[l][b], 1)
                    with dve.Fori(0, NEXP) as e:
                        for i in range(FE):
                            b1, n1, per = over_bank(("H1", i), T)
                            b, n, _ = over_bank(("H3", i), T)
                            dve.wait_ge(over_full[l][b], e * per + (n + 1))
                            dve.wait_ge(over_free[l][b1], e * per + (n1 + 2))
                            tt(GH[:, i, 0:N], TMP[:, i % 2, 0:N], ps[b][:, 0:N], ALU.mult) \
                                .then_inc(over_free[l][b], 1)
                        nc.vector.tensor_copy(CE[:, 0:T],
                                              CMB[:, 0:T, bass.ds(e, 1)].rearrange("p t a -> p (t a)")) \
                            .then_inc(over_steps[l], 1)
                        dve.wait_ge(over_steps[l], e + 1)
                        for t in range(T):
                            for half in range(2):
                                b, n, per = over_bank(("Y", t, half), T)
                                dve.wait_ge(over_full[l][b], e * per + (n + 1))
                                cols = slice(512 * half, 512 * half + 512)
                                stt(FACC[:, t, cols], ps[b][:, :], CE[:, t:t + 1], FACC[:, t, cols],
                                    ALU.mult, ALU.add).then_inc(over_free[l][b], 1)
                    b, n, per = over_bank(("Y", T - 1, 1), T)
                    dve.wait_ge(over_free[l][b], NEXP * per + 1)
                wait_read(dve, (l, "GB", 1, T // 2 - 1, 1))
                for t in range(T):
                    link(tt(FACC[:, t, :], FACC[:, t, :], GB[:, t // 2, :], ALU.mult))
                    link(tt(X[:, t, :], X[:, t, :], FACC[:, t, :], ALU.add),
                                experts_done, (T0 if l else 0) + t + 1)

        @block.tensor
        def _(pe):
            mm = nc.tensor.matmul

            def product(key, dst, pairs):
                for i, (a, b) in enumerate(pairs):
                    ins = mm(dst, a, b, start=(i == 0), stop=(i == len(pairs) - 1))
                return ins

            def norm_transposes(l, norm):
                T = TT if not norm else tiles_of(l)
                for k in range(KD):
                    key = (l, "N2" if norm else "N1", k)
                    wait_bank(pe, key)
                    for t in range(T):
                        if k == 0:
                            pe.wait_ge(rows_ready, row_no(l, norm, t) + 1)
                        ins = nc.tensor.transpose(bank(key)[:, t * P:(t + 1) * P], XN[:, t, k * P:(k + 1) * P],
                                                  ident[:, :])
                    full(ins, key)

            def gate_rows(l, which):
                for s in range(tiles_of(l) // 2):
                    for half in range(2):
                        key = (l, "GB", which, s, half)
                        wait_bank(pe, key)
                        for q in range(4):
                            m = (40 if which else 16) + 4 * half + q
                            ins = mm(bank(key)[:, q * P:(q + 1) * P], MOD[:, m, s:s + 1].to_broadcast([P, P]),
                                     ident[:, :], start=True, stop=True)
                        full(ins, key)

            def token_rows(key, t):
                wait_bank(pe, key)
                w = slot_kn((key[0], key[1], 0))
                full(product(key, bank(key)[:, :], [(HT[:, k, t * P:(t + 1) * P], w[:, k, :]) for k in range(KD)]), key)

            def query_transposes(l, what, src_what, t):
                key = (l, what, t)
                pe.wait_ge(qk_ready, proj[(l, src_what, t)] + 1)
                wait_bank(pe, key)
                for h in range(4):
                    ins = nc.tensor.transpose(bank(key)[:, h * P:(h + 1) * P], QN[:, t, h * P:(h + 1) * P],
                                              ident[:, :])
                full(ins, key)

            def filter_step(l, step):
                if step == 0:
                    key = (l, "F1")
                    pe.wait_ge(filter_loaded, 48 * (l + 1))
                    pe.wait_ge(network_loaded, 80)
                    wait_bank(pe, key)
                    full(mm(bank(key)[0:HID, 0:SEQ], FW[0:EMB, l, 0, :], Z, start=True, stop=True), key)
                elif step == 1:
                    key = (l, "F2")
                    pe.wait_ge(filter_sin, 2 * l + 1)
                    wait_bank(pe, key)
                    full(mm(bank(key)[0:HID, 0:SEQ], FW[:, l, 1, :], FT[:, 3, :], start=True, stop=True), key)
                elif step == 2:
                    pe.wait_ge(filter_sin, 2 * l + 2)
                    for t in range(2):
                        for half in range(2):
                            key = (l, "F3", t, half)
                            wait_bank(pe, key)
                            full(mm(bank(key)[:, :], FT[:, 4, t * P:(t + 1) * P], W3[:, 512 * half:512 * half + 512],
                                    start=True, stop=True), key)
                elif step == 3:
                    key = (l, "FN")
                    wait_bank(pe, key)
                    pe.wait_ge(filter_abs, 4 * l + 4)
                    full(product(key, bank(key)[:, :],
                                 [(ones[:, :], DEC[:, t, h, :]) for t in range(2) for h in range(2)]), key)
                else:
                    pe.wait_ge(filter_ab, 2 * l + 2)
                    pe.wait_ge(params_loaded, 16 * LATE)
                    for m in range(5):
                        key = (l, "FK", m)
                        wait_bank(pe, key)
                        full(product(key, bank(key)[:, :], [(DF[:, t, m * P:(m + 1) * P], FAB[:, t, int(m >= 3), :])
                                                            for t in range(2)]), key)

            pe.wait_ge(early_loaded, 16 * EARLY)
            pe.wait_ge(ones_ready, 2)
            for l in range(LAYERS):
                T = tiles_of(l)
                N = T * P
                key = (l, "PR")
                wait_bank(pe, key)
                full(nc.tensor.transpose(bank(key)[:, 0:116], PR[:, l, :], ident[0:116, 0:116]), key)
                if l == 0:
                    key = (l, "C")
                    pe.wait_ge(cond_ready, 1)
                    wait_bank(pe, key)
                    full(nc.tensor.transpose(bank(key)[:, 0:16], CR[:, :], ident[0:16, 0:16]), key)
                wait_read(pe, (0, "C"))
                cc = CC[:, :].rearrange("p (s k) -> p k s", s=2)
                for j in range(12):
                    if j in FILTER_SLOTS:
                        filter_step(l, FILTER_SLOTS.index(j))
                    key = (l, "MOD", j)
                    wait_slot(pe, (l, "ADA", j))
                    w = slot_kn((l, "ADA", j))
                    wait_bank(pe, key)
                    for q in range(4):
                        ins = product(key, bank(key)[:, q * WIDE:(q + 1) * WIDE],
                                      [(w[:, k, q * P:(q + 1) * P],
                                        cc[:, k, :].unsqueeze(1).to_broadcast([P, WIDE // 2, 2])) for k in range(KD)])
                    full(ins, key)
                pe.wait_ge(mod_ready, l + 1)
                norm_transposes(l, 0)
                wait_read(pe, (l, "N1", KD - 1))
                wait_slot(pe, (l, "QA", 0))
                for t in range(T):
                    token_rows((l, "QA", t), t)
                wait_slot(pe, (l, "KV", 0))
                for t in range(TT):
                    token_rows((l, "KV", t), t)
                for t in range(T):
                    query_transposes(l, "QAT", "QA", t)
                wait_slot(pe, (l, "QW", 0))
                for t in range(T):
                    token_rows((l, "QW", t), t)
                for t in range(TT):
                    key = (l, "KVT", t)
                    pe.wait_ge(qk_ready, proj[(l, "KV", t)] + 1)
                    wait_bank(pe, key)
                    for kind in range(2):
                        ins = nc.tensor.transpose(bank(key)[:, kind * P:(kind + 1) * P],
                                                  KN[:, t, kind * P:(kind + 1) * P], ident[:, :])
                    full(ins, key)
                for ch in range(12):
                    key = (l, "U", ch)
                    if ch % 4 == 0:
                        wait_slot(pe, (l, "U", ch // 4))
                    w = slot_kn((l, "U", ch // 4))
                    wait_bank(pe, key)
                    q = ch % 4
                    full(product(key, bank(key)[:, 0:N], [(w[:, k, q * P:(q + 1) * P], HT[:, k, 0:N])
                                                          for k in range(KD)]), key)
                for t in range(T):
                    query_transposes(l, "QWT", "QW", t)
                wait_read(pe, (l, "QWT", T - 1))
                for s in attention_steps(l):
                    if s[0] == "S":
                        _, kind, t, h = s
                        key = (l, *s)
                        g, r = h // 4, h % 4
                        rows = slice(HD * g, HD * g + HD)
                        k0, nk = keys_of(t)[0], len(keys_of(t))
                        wait_bank(pe, key)
                        full(mm(bank(key)[:, 0:nk * P], QT[rows, kind, r, t * P:(t + 1) * P],
                                KT[rows, kind, k0 * P:(k0 + nk) * P], start=True, stop=True), key)
                    elif s[0] == "PT":
                        _, kind, t, h = s
                        key = (l, *s)
                        u = units[(l, kind, t, h)]
                        wait_read(pe, (l, "S", kind, t, h))
                        wait_bank(pe, key)
                        for j in range(len(keys_of(t))):
                            ins = nc.tensor.transpose(bank(key)[:, j * P:(j + 1) * P],
                                                      PB[:, u % 3, j * P:(j + 1) * P], ident[:, :])
                        full(ins, key)
                    elif s[0] == "O":
                        _, kind, t, h = s
                        key = (l, "O", kind, t, h // 4)
                        u = units[(l, kind, t, h)]
                        if h % 4 == 0:
                            wait_bank(pe, key)
                        wait_read(pe, (l, "PT", kind, t, h))
                        q = h % 4
                        ins = product(key, bank(key)[:, q * P:(q + 1) * P],
                                      [(PTB[:, u % 3, j * P:(j + 1) * P], V[:, kt, kind, :])
                                       for j, kt in enumerate(keys_of(t))])
                        if q == 3:
                            full(ins, key)
                    else:
                        _, kind, t = s
                        key = (l, *s)
                        gi = groups[(l, kind, t)]
                        wait_read(pe, (l, "O", kind, t, 1))
                        wait_bank(pe, key)
                        for q in range(4):
                            ins = nc.tensor.transpose(bank(key)[:, q * P:(q + 1) * P], YA[:, gi % 2, q * P:(q + 1) * P],
                                                      ident[:, :])
                        full(ins, key)
                pe.wait_ge(gated_v, l + 1)
                for t in range(T):
                    key = (l, "VT", t)
                    wait_bank(pe, key)
                    for q in range(CH):
                        ins = nc.tensor.transpose(bank(key)[:, q * P:(q + 1) * P], UC[:, 8 + q, t * P:(t + 1) * P],
                                                  ident[:, :])
                    full(ins, key)
                for s in range(T // 2):
                    wait_read(pe, (l, "VT", 2 * s))
                    wait_read(pe, (l, "VT", 2 * s + 1))
                    for p in range(2):
                        for r in range(2):
                            key = (l, "DFT", s, r, p)
                            col = (0, 1)[p] if r == 0 else (5, 4)[p]
                            wait_bank(pe, key)
                            full(product(key, bank(key)[:, :], [(DF[:, t, col * P:(col + 1) * P], VT[:, 2 * s + t, :])
                                                                for t in range(2)]), key)
                for s in range(T // 2):
                    pe.wait_ge(spec_ready, 2 * seqs[(l, s)] + 2)
                    for ch in range(CH):
                        key = (l, "INV", s, ch)
                        wait_bank(pe, key)
                        full(product(key, bank(key)[:, 0:SEQ], [(YS[:, s, f, ch * P:(ch + 1) * P], IF[:, f, :])
                                                                for f in range(4)]), key)
                gate_rows(l, 0)
                def three(dst, a, b, first, last):
                    for i, (p, q) in enumerate(((0, 0), (1, 0), (0, 1))):
                        ins = mm(dst, a[p], b[q], start=(first and i == 0), stop=(last and i == 2))
                    return ins

                def branch(b, g):
                    wait_slot(pe, (l, "BR", b))
                    wb = slot((l, "BR", b)).rearrange("p (k n) -> p k n", k=CH)
                    for ch in range(4 * g, 4 * g + 4):
                        key = (l, "BR", b, ch)
                        wait_bank(pe, key)
                        y = [UC[:, k, 0:N] if b == 1 else YT[:, b // 2, k, 0:N] for k in range(CH)]
                        full(product(key, bank(key)[:, 0:N], [(wb[:, k, ch * P:(ch + 1) * P], y[k])
                                                              for k in range(CH)]), key)

                pe.wait_ge(yh_ready, CH * seqs[(l, T // 2 - 1)] + CH)
                branch(*GATE_GROUPS[0])
                for j, (b, g) in enumerate(GATE_GROUPS):
                    for k in range(KD):
                        n, w, _ = gate_chunk(l, j, k)
                        pe.wait_ge(ht_low, KD * l + k + 1)
                        pe.wait_ge(gate_low, n + 1)
                        for q in range(4):
                            key = (l, "GATE", b, 4 * g + q)
                            if k == 0:
                                wait_bank(pe, key)
                            ins = three(bank(key)[:, 0:N], [w[:, p, q * P:(q + 1) * P] for p in range(2)],
                                        [HTP[l][p][:, k, :] for p in range(2)], k == 0, k == KD - 1)
                            if k == KD - 1:
                                full(ins, key)
                            elif q == 3:
                                ins.then_inc(gate_used, 1)
                    if j:
                        if b != 1:
                            wait_read(pe, (l, "YAT", 1, T - 1))
                        branch(b, g)
                pe.wait_ge(merged, KD * l + KD)
                for t in range(T):
                    for half in range(2):
                        if t == 0:
                            wait_slot(pe, (l, "OUT", half))
                        w = slot_kn((l, "OUT", half))
                        key = (l, "OUT", half, t)
                        wait_bank(pe, key)
                        full(product(key, bank(key)[:, :], [(MT[:, k, t * P:(t + 1) * P], w[:, k, :])
                                                            for k in range(KD)]), key)
                norm_transposes(l, 1)
                wait_read(pe, (l, "N2", KD - 1))
                for t in range(T):
                    key = (l, "LG", t)
                    wait_bank(pe, key)
                    full(product(key, bank(key)[:, 0:100],
                                 [(HT[:, k, t * P:(t + 1) * P], RW[:, l, k, :].unsqueeze(1).to_broadcast([P, 5, 20]))
                                  for k in range(KD)]), key)
                gate_rows(l, 1)
                C = CAP[l]
                for t in range(T):
                    for half in range(2):
                        key = (l, "TK", t, half)
                        wait_bank(pe, key)
                        for q in range(4):
                            ins = nc.tensor.transpose(bank(key)[:, q * P:(q + 1) * P],
                                                      HT[:, 4 * half + q, t * P:(t + 1) * P], ident[:, :])
                        full(ins, key)
                key = (l, "RANK")
                wait_bank(pe, key)
                pe.wait_ge(sel_ready, l + 1)
                sel = RT[:, 9, :, :].unsqueeze(2).to_broadcast([P, TT, WIDE // NEXP, NEXP])
                for t in range(T):
                    product(key, bank(key)[:, t * WIDE:(t + 1) * WIDE],
                            [(TRI[:, :] if u == t else ones[:, :], sel[:, u]) for u in range(t + 1)])
                full(product(key, bank(key)[:, T * WIDE:(T + 1) * WIDE], [(ones[:, :], sel[:, u]) for u in range(T)]),
                     key)

                def gather(key):
                    for q in range(4):
                        k = 4 * key[2] + q
                        ins = product(key, bank(key)[:, q * C:(q + 1) * C],
                                      [(part[:, t, k * P:(k + 1) * P], S[:, t, 0:C]) for part in TOK
                                       for t in range(T)])
                    full(ins, key)

                def scatter(key):
                    _, _, t, half = key
                    full(product(key, bank(key)[:, :], [(STB[0:C, t * P:(t + 1) * P],
                                                         part[0:C, 512 * half:512 * half + 512]) for part in YP]), key)

                pe.wait_ge(places_ready, (NEXP + 1) * l + 1)
                pe.wait_ge(tok_low, tile_no(l, T - 1) + 1)
                pe.wait_ge(tok_low_dve, tile_no(l, T - 1) + 1)
                for half in range(2):
                    wait_bank(pe, (l, "GA0", half))
                    gather((l, "GA0", half))
                    key = (l, "Y0", half)
                    wait_bank(pe, key)
                    full(mm(bank(key)[0:C, :], STB[:, 0:C], YP[0][:, 0:512], start=True, stop=True), key)

                with pe.Fori(0, NEXP) as e:
                    key = (l, "ST")
                    wait_bank_e(pe, key, e)
                    for t in range(T):
                        ins = mm(bank(key)[0:C, t * P:(t + 1) * P], S[:, t, 0:C], ident_b[:, :], start=True, stop=True)
                    full(ins, key)
                    wait_read_e(pe, (l, "GA", 0), e, back=1)
                    for c in range(CHUNKS):
                        k = c % 8
                        if c < 16:
                            key, first, last = (l, "H1" if c < 8 else "H3"), k == 0, k == 7
                            if c == 4:
                                wait_read_e(pe, (l, "GA", 1), e, back=1)
                            a = [XGP[p][:, k, 0:C] for p in range(2)]
                        else:
                            key, k = (l, "Y", k % 2), k // 2
                            first, last = k == 0, k == FE - 1
                            if c == 16:
                                wait_read_e(pe, (l, "GT"), e)
                            a = [GTP[p][:, k, 0:C] for p in range(2)]
                        if first:
                            wait_bank_e(pe, key, e)
                        d, n = split_count(c)
                        dn, pn = split_count(CHUNKS - 1)
                        if by_pool(c):
                            pe.wait_ge(chunk_low_pool, e * pn + (pn * NEXP * l + n))
                        else:
                            pe.wait_ge(chunk_low, e * dn + (dn * NEXP * l + d))
                        ins = three(bank(key)[0:C, :], a, [WP[:, c % BUFS, p, :] for p in range(2)], first, last)
                        if last:
                            full(ins, key)
                        else:
                            ins.then_inc(chunk_used, 1)
                        if c == SCATTER_AFTER[0]:
                            wait_read_e(pe, (l, "Y", 1), e, back=1)
                            wait_read_e(pe, (l, "GT"), e, back=1)
                        if c in SCATTER_AFTER[0:2 * T]:
                            i = SCATTER_AFTER.index(c)
                            sc = (l, "SC", i // 2, i % 2)
                            wait_bank_e(pe, sc, e)
                            scatter(sc)
                        if c == 15:
                            pe.wait_ge(places_ready, e + ((NEXP + 1) * l + 2))
                            wait_bank_e(pe, (l, "GA", 0), e)
                            gather((l, "GA", 0))
                            key = (l, "GT")
                            wait_read_e(pe, (l, "H3"), e)
                            wait_bank_e(pe, key, e)
                            for i in range(FE):
                                ins = mm(bank(key)[:, i * C:(i + 1) * C], GM[0:C, i * P:(i + 1) * P],
                                         ident[0:C, 0:C], start=True, stop=True)
                            full(ins, key)
                            wait_bank_e(pe, (l, "GA", 1), e)
                            gather((l, "GA", 1))
                wait_read_e(pe, (l, "Y", 1), NEXP - 1)
                wait_read_e(pe, (l, "ST"), NEXP - 1)
                for t in range(T):
                    for half in range(2):
                        wait_bank(pe, (l, "SCL", t, half))
                        scatter((l, "SCL", t, half))
                pe.wait_ge(flag_ready, l + 1)
                over = pe.value_load(FLAG[0:1, 0:1], min_val=0, max_val=1)
                with pe.If(over > 0):
                    with pe.Fori(0, NEXP) as e:
                        for j in range(2):
                            pe.wait_ge(over_loaded[l][j], e * 16 + 16)
                        for i in range(FE):
                            for j, what in enumerate(("H1", "H3")):
                                b, n, per = over_bank((what, i), T)
                                w = ring[:, j, :].rearrange("p (k n) -> p k n", k=KD)
                                pe.wait_ge(over_free[l][b], e * per + (n + 1))
                                product(None, ps[b][:, 0:N], [(w[:, k, i * P:(i + 1) * P], HT[:, k, 0:N])
                                                              for k in range(KD)]).then_inc(over_full[l][b], 1)
                        pe.wait_ge(over_loaded[l][2], e * 16 + 16)
                        w2 = ring[:, 2, :].rearrange("p (k n) -> p k n", k=FE)
                        for i in (FE - 2, FE - 1):
                            b, n, per = over_bank(("H3", i), T)
                            pe.wait_ge(over_free[l][b], e * per + (n + 2))
                        for t in range(T):
                            for half in range(2):
                                b, n, per = over_bank(("Y", t, half), T)
                                pe.wait_ge(over_free[l][b], e * per + (n + 1))
                                product(None, ps[b][:, :],
                                        [(GH[:, k, t * P:(t + 1) * P], w2[:, k, 512 * half:512 * half + 512])
                                         for k in range(FE)]).then_inc(over_full[l][b], 1)
                    for b in range(4, 8):
                        pe.wait_ge(over_free[l][b], NEXP * (T // 2) + 1)


EARLY = 3 + 6
LATE = 6 * LAYERS + 11 * (LAYERS - 1) + 7


def constants():
    n = SEQ
    t = np.arange(n)
    f = np.arange(n)
    ang = 2 * np.pi * np.outer(t, f) / (2 * n)
    cos, sin = np.cos(ang), -np.sin(ang)
    alt = (-1.0) ** t
    cosn, sinn = cos[:, 0:P].copy(), sin[:, 0:P].copy()
    cosn[:, 0] = alt
    sinn[:, 0] = alt
    dft = np.concatenate([cos, cosn, sin, sinn], axis=1)
    icos = 2 * np.cos(ang).T / (2 * n)
    icos[0] /= 2
    isin = -2 * np.sin(ang).T / (2 * n)
    isin[0] = alt / (2 * n)
    idft = np.concatenate([icos, isin], axis=0)
    pos = (np.arange(n) / (n - 1)).astype(np.float32)
    deltas = np.abs(np.linspace(np.log(1e-2) / 1.5, np.log(1e-2) / 0.3, HW)).astype(np.float32)
    dec = np.exp(-pos[:, None] * deltas[None]).astype(np.float32)
    dec2 = np.stack([dec, dec], axis=1)
    dec2[0, 1] = 0.0
    bands = np.linspace(1e-4, 15, 16).astype(np.float32)
    za = (2 * np.pi * bands.astype(np.float64)[None] * np.arange(n)[:, None] / n)
    z = np.concatenate([pos[:, None], np.cos(za), -np.sin(za)], axis=1).T
    inv = 10000.0 ** (-np.arange(16) / 16.0)
    row, col = np.arange(n) // 64, np.arange(n) % 64
    a = np.stack([row[:, None] * inv, col[:, None] * inv], axis=1)
    c = np.stack([np.cos(a), np.cos(a)], axis=2).reshape(n, HD)
    s = np.stack([-np.sin(a), np.sin(a)], axis=2).reshape(n, HD)
    rope = np.stack([c, s], axis=1)
    mask = np.where(np.abs(np.arange(n)[None] - np.arange(n)[:, None]) <= 128, 0.0, -BIG)
    first = np.concatenate([np.arange(4, 0, -1), np.arange(16, 0, -1)])
    out = {"k_ident": np.eye(P), "k_dft": dft, "k_idft": idft, "k_decay": dec2, "k_z": z, "k_rope": rope,
           "k_mask": mask, "k_first": first, "k_tri": np.triu(np.ones((P, P)), 1), "k_iota": np.arange(P)}
    return {k: np.ascontiguousarray(v, dtype=np.float32) for k, v in out.items()}


_INS = ["x", "c", "ctx", "c_ctx", "ada_w", "ada_b", "norm1_g", "norm2_g", "w_in", "qk_g", "hy_short_w", "hy_short_b",
        "hy_f_w1", "hy_f_b1", "hy_f_freq", "hy_f_w2", "hy_f_b2", "hy_f_w3", "hy_bias", "sinks", "w_branch", "w_out",
        "router_g_w", "router_g_b", "router_e_w", "router_e_b", "exp_w1", "exp_w3", "exp_w2"]


def kernel(**inputs):
    import concourse.bacc as _bacc
    from concourse.bass_utils import run_bass_kernel_spmd as _run

    nc = _bacc.Bacc("TRN2", target_bir_lowering=False, num_devices=1)
    arrays, args = {}, []
    data = {k: np.ascontiguousarray(inputs[k]) for k in _INS}
    data.update(constants())
    for name, a in data.items():
        arrays[f"in_{name}"] = a
        args.append(nc.dram_tensor(f"in_{name}", a.shape, mybir.dt.from_np(a.dtype), kind="ExternalInput").ap())
    args.append(nc.dram_tensor("out_0", (1, SEQ, D), F32, kind="ExternalOutput").ap())
    build(nc, *args)
    r = _run(nc, [arrays], core_ids=[0])
    return r.results[0]["out_0"]
```
